# Optimizing a Trainium2 kernel written in Bass

```python
import math
import jax, jax.numpy as jnp
from jax import lax
import numpy as np

D_MODEL = 1024
BATCH = 1
SEQ = 256
DEPTH = 2
DEC_BATCH = 8
DEC_SEQ = 8
PAST_LEN = 1024
PAGE_SIZE = 128

N_EVEN = (DEPTH + 1) // 2
N_ODD = DEPTH // 2
H_A = 8
DK_A = 32
DV_A = 64
QK_A = H_A * 2 * DK_A
W_A = H_A * DV_A
A_COLS = 2 * QK_A + W_A
H_B = 8
N_B = 64
W_B = H_B * N_B
LORA_W = 64
LORA_A = 64
LORA_G = 128
B_COLS = 3 * W_B + LORA_W + LORA_A + LORA_G
IN_COLS_EVEN = A_COLS + B_COLS
MIX_EVEN = W_A + W_B
CHUNK = 128
G_C = 8
E_C = 2 * D_MODEL
CG = E_C // G_C
D_FF = 2816
N_EXPERTS = 8
TOP_K = 2
D_FF_E = 1408
Q_BLOCK = 128
RMS_EPS = 1e-6
LN_EPS = 1e-5
LNX_EPS = 64e-5
NEG_INF = -1e30

kernel_name = 'hybrid_diffattn_rwkv7_gmlp_moe_step'

def _rmsnorm(x, g):
    xf = x.astype(jnp.float32)
    y = xf * lax.rsqrt(jnp.mean(xf * xf, axis=-1, keepdims=True) + RMS_EPS)
    return (y * g.astype(jnp.float32)).astype(x.dtype)

def _layernorm(x, g, b, eps):
    xf = x.astype(jnp.float32)
    xc = xf - jnp.mean(xf, axis=-1, keepdims=True)
    y = xc * lax.rsqrt(jnp.mean(xc * xc, axis=-1, keepdims=True) + eps)
    return (y * g.astype(jnp.float32) + b.astype(jnp.float32)).astype(x.dtype)

def _swiglu(h, w_gate, w_up, w_down):
    return (jax.nn.silu(h @ w_gate) * (h @ w_up)) @ w_down

def _moe_swiglu(h, w_r, b_r, e_gate, e_up, e_down):
    logits = (h @ w_r).astype(jnp.float32) + b_r.astype(jnp.float32)
    top_v, top_i = lax.top_k(logits, TOP_K)
    wts = jax.nn.softmax(top_v, axis=-1)
    gate = jnp.sum(jax.nn.one_hot(top_i, N_EXPERTS, dtype=jnp.float32) * wts[..., None], axis=-2)
    gate = gate.astype(h.dtype)
    out = jnp.zeros_like(h)
    for e in range(N_EXPERTS):
        out = out + gate[..., e:e + 1] * _swiglu(h, e_gate[e], e_up[e], e_down[e])
    return out

def _diff_attention(q, k, v, q_pos, k_pos, lam):
    n, t = q.shape[:2]
    slopes = jnp.exp2(-8.0 * jnp.arange(1, H_A + 1, dtype=jnp.float32) / H_A)
    kf = k.astype(jnp.float32)
    vf = v.astype(jnp.float32)
    scale = DK_A ** -0.5

    def block(args):
        qb, qp = args
        s = jnp.einsum('nthmd,nshmd->nmhts', qb.astype(jnp.float32), kf) * scale
        dist = jnp.abs(qp[:, None] - k_pos[None, :]).astype(jnp.float32)
        s = s - slopes[:, None, None] * dist
        s = jnp.where(k_pos[None, :] <= qp[:, None], s, NEG_INF)
        pr = jax.nn.softmax(s, axis=-1)
        pr = pr[:, 0] - lam * pr[:, 1]
        return jnp.einsum('nhts,nshd->nthd', pr, vf)

    if t <= Q_BLOCK:
        return block((q, q_pos))
    nb = -(-t // Q_BLOCK)
    pad = nb * Q_BLOCK - t
    qpad = jnp.pad(q, ((0, 0), (0, pad), (0, 0), (0, 0), (0, 0)))
    ppad = jnp.pad(q_pos, (0, pad), mode='edge')
    qb = jnp.swapaxes(qpad.reshape(n, nb, Q_BLOCK, H_A, 2, DK_A), 0, 1)
    pb = ppad.reshape(nb, Q_BLOCK)
    out = lax.map(block, (qb, pb))
    return jnp.swapaxes(out, 0, 1).reshape(n, nb * Q_BLOCK, H_A, DV_A)[:, :t]

def _rwkv7_scan(r, w, k, v, kk, a, s0):
    def step(s, inp):
        r_t, w_t, k_t, v_t, kk_t, a_t = inp
        sa = jnp.einsum('nhvk,nhk->nhv', s, kk_t)
        s = (s * w_t[:, :, None, :] - sa[..., None] * (kk_t * a_t)[:, :, None, :]
             + v_t[..., None] * k_t[:, :, None, :])
        return s, jnp.einsum('nhvk,nhk->nhv', s, r_t)
    xs = tuple(jnp.moveaxis(z, 1, 0) for z in (r, w, k, v, kk, a))
    s_fin, ys = lax.scan(step, s0, xs)
    return jnp.moveaxis(ys, 0, 1), s_fin

def _even_mixer(h, p, j, layer_idx, past_k, past_v, wkv0, shift0):
    n, t, _ = h.shape
    f32 = jnp.float32
    proj = h @ p['w_in_e'][j]
    pa, pb = proj[..., :A_COLS], proj[..., A_COLS:]
    q = pa[..., :QK_A].reshape(n, t, H_A, 2, DK_A)
    k = pa[..., QK_A:2 * QK_A].reshape(n, t, H_A, 2, DK_A)
    v = pa[..., 2 * QK_A:].reshape(n, t, H_A, DV_A)
    if past_k is None:
        start = 0
        k_all, v_all = k, v
    else:
        start = past_k.shape[1]
        k_all = jnp.concatenate([past_k.reshape(n, start, H_A, 2, DK_A).astype(k.dtype), k], axis=1)
        v_all = jnp.concatenate([past_v.astype(v.dtype), v], axis=1)
    q_pos = start + jnp.arange(t, dtype=jnp.int32)
    k_pos = jnp.arange(start + t, dtype=jnp.int32)
    lam_init = 0.8 - 0.6 * math.exp(-0.3 * layer_idx)
    lam = (jnp.exp(jnp.sum(p['lam_q1'][j].astype(f32) * p['lam_k1'][j].astype(f32)))
           - jnp.exp(jnp.sum(p['lam_q2'][j].astype(f32) * p['lam_k2'][j].astype(f32))) + lam_init)
    oa = _diff_attention(q, k_all, v_all, q_pos, k_pos, lam)
    oa = _rmsnorm(oa, p['subln_g'][j]) * (1.0 - lam_init)
    oa = oa.reshape(n, t, W_A).astype(h.dtype)
    prev = jnp.concatenate([shift0[:, None, :].astype(pb.dtype), pb[:, :-1]], axis=1)
    xb = pb + (prev - pb) * p['mu_b'][j]
    o1, o2, o3 = W_B, 2 * W_B, 3 * W_B
    o4 = o3 + LORA_W
    o5 = o4 + LORA_A
    r = xb[..., :o1].astype(f32)
    kb = xb[..., o1:o2].astype(f32)
    vb = xb[..., o2:o3].astype(f32)
    w_log = (p['w0'][j] + jnp.tanh(xb[..., o3:o4]) @ p['w_up'][j]).astype(f32)
    decay = jnp.exp(-jnp.exp(-jax.nn.softplus(-w_log) - 0.5))
    a = jax.nn.sigmoid((p['a0'][j] + xb[..., o4:o5] @ p['a_up'][j]).astype(f32))
    g = (jax.nn.sigmoid(xb[..., o5:]) @ p['g_up'][j]).astype(f32)

    def heads(z):
        return z.reshape(n, t, H_B, N_B)

    kk = heads(kb * p['k_k'][j].astype(f32))
    kk = kk / jnp.maximum(jnp.linalg.norm(kk, axis=-1, keepdims=True), 1e-12)
    kb = kb * (1.0 + (a - 1.0) * p['k_a'][j].astype(f32))
    rh, kh, vh, ah, dh = heads(r), heads(kb), heads(vb), heads(a), heads(decay)
    yb, s_fin = _rwkv7_scan(rh, dh, kh, vh, kk, ah, wkv0.astype(f32))
    yb = _layernorm(yb, p['lnx_g'][j].reshape(H_B, N_B), p['lnx_b'][j].reshape(H_B, N_B), LNX_EPS)
    yb = yb + jnp.sum(rh * kh * p['r_k'][j].astype(f32), axis=-1, keepdims=True) * vh
    ob = (yb.reshape(n, t, W_B) * g).astype(h.dtype)
    out = jnp.concatenate([oa, ob], axis=-1) @ p['w_out_e'][j]
    return out, k.reshape(n, t, H_A, 2 * DK_A), v, s_fin.astype(h.dtype), pb[:, -1]

def _odd_mixer(h, p, j):
    n, t, _ = h.shape
    uv = jax.nn.gelu(h @ p['w_in_o'][j], approximate=False)
    u, v = uv[..., :E_C], uv[..., E_C:]
    v = _layernorm(v, p['lnv_g'][j], p['lnv_b'][j], LN_EPS)
    length = min(t, CHUNK)
    nc = -(-t // length)
    pad = nc * length - t
    vp = jnp.pad(v, ((0, 0), (0, pad), (0, 0))).reshape(n, nc, length, G_C, CG)
    ws = jnp.tril(p['w_s'][j][:, :length, :length])
    bs = p['b_s'][j][:, :length]
    mixed = jnp.einsum('gts,ncsgd->nctgd', ws, vp) + bs.T[:, :, None]
    mixed = mixed.reshape(n, nc * length, E_C)[:, :t]
    return (u * mixed) @ p['w_out_o'][j], v

def _forward(x, c, p, cache_k, cache_v, page_table, state_wkv, state_shift):
    n = x.shape[0]
    new_k, new_v, new_wkv, new_shift, new_cv = [], [], [], [], []
    for i in range(DEPTH):
        j = i // 2
        mod = jax.nn.silu(c) @ p['w_mod'][i] + p['b_mod'][i]
        sh1, sc1, g1, sh2, sc2, g2 = jnp.split(mod[:, None, :], 6, axis=-1)
        hn = _rmsnorm(x, p['norm1_g'][i]) * (1.0 + sc1) + sh1
        if i % 2 == 0:
            if cache_k is None:
                pk = None
                pv = None
                wkv0 = jnp.zeros((n, H_B, N_B, N_B), x.dtype)
                sh0 = jnp.zeros((n, B_COLS), x.dtype)
            else:
                pk = cache_k[j][page_table].reshape(n, -1, H_A, 2 * DK_A)
                pv = cache_v[j][page_table].reshape(n, -1, H_A, DV_A)
                wkv0 = state_wkv[j]
                sh0 = state_shift[j]
            mix, kn, vn, s_fin, sh_last = _even_mixer(hn, p, j, i, pk, pv, wkv0, sh0)
            new_k.append(kn)
            new_v.append(vn)
            new_wkv.append(s_fin)
            new_shift.append(sh_last)
            x = x + g1 * mix
            hn = _rmsnorm(x, p['norm2_g'][i]) * (1.0 + sc2) + sh2
            ffn = _swiglu(hn, p['ffn_gate'][j], p['ffn_up'][j], p['ffn_down'][j])
        else:
            mix, v_rows = _odd_mixer(hn, p, j)
            new_cv.append(v_rows)
            x = x + g1 * mix
            hn = _rmsnorm(x, p['norm2_g'][i]) * (1.0 + sc2) + sh2
            ffn = _moe_swiglu(hn, p['router_w'][j], p['router_b'][j],
                              p['exp_gate'][j], p['exp_up'][j], p['exp_down'][j])
        x = x + g2 * ffn
    y = _rmsnorm(x, p['final_g'])
    return (y, jnp.stack(new_k), jnp.stack(new_v), jnp.stack(new_wkv),
            jnp.stack(new_shift), jnp.stack(new_cv))

def setup_inputs(seed: int = 0) -> dict:
    key = jax.random.key(seed)
    keys = list(jax.random.split(key, 64))
    f32 = jnp.float32

    def nrm(shape, scale):
        return jax.random.normal(keys.pop(), shape, f32) * scale

    d = D_MODEL
    n_pages = PAST_LEN // PAGE_SIZE
    used = DEC_BATCH * n_pages
    n_pool = used + max(1, used // 4)
    page_table = jax.random.permutation(keys.pop(), n_pool)[:used].reshape(DEC_BATCH, n_pages).astype(jnp.int32)
    inp = {}
    inp['x_prompt'] = nrm((BATCH, SEQ, d), 1.0)
    inp['x_sample'] = nrm((DEC_BATCH, DEC_SEQ, d), 1.0)
    inp['cache_k'] = nrm((N_EVEN, n_pool, PAGE_SIZE, H_A, 2 * DK_A), 1.0)
    inp['cache_v'] = nrm((N_EVEN, n_pool, PAGE_SIZE, H_A, DV_A), 1.0)
    inp['state_wkv'] = nrm((N_EVEN, DEC_BATCH, H_B, N_B, N_B), 0.5)
    inp['state_shift'] = nrm((N_EVEN, DEC_BATCH, B_COLS), 1.0)
    inp['page_table'] = page_table
    inp['c_prompt'] = nrm((BATCH, d), 1.0)
    inp['c_sample'] = nrm((DEC_BATCH, d), 1.0)
    inp['w_mod'] = nrm((DEPTH, d, 6 * d), 0.5 * d ** -0.5)
    inp['b_mod'] = nrm((DEPTH, 6 * d), 0.02)
    inp['norm1_g'] = 1.0 + nrm((DEPTH, d), 0.02)
    inp['norm2_g'] = 1.0 + nrm((DEPTH, d), 0.02)
    inp['final_g'] = 1.0 + nrm((d,), 0.02)
    inp['w_in_e'] = nrm((N_EVEN, d, IN_COLS_EVEN), d ** -0.5)
    inp['w_out_e'] = nrm((N_EVEN, MIX_EVEN, d), MIX_EVEN ** -0.5)
    inp['lam_q1'] = nrm((N_EVEN, DK_A), 0.1)
    inp['lam_k1'] = nrm((N_EVEN, DK_A), 0.1)
    inp['lam_q2'] = nrm((N_EVEN, DK_A), 0.1)
    inp['lam_k2'] = nrm((N_EVEN, DK_A), 0.1)
    inp['subln_g'] = 1.0 + nrm((N_EVEN, DV_A), 0.02)
    inp['mu_b'] = jax.random.uniform(keys.pop(), (N_EVEN, B_COLS), f32)
    inp['w0'] = nrm((N_EVEN, W_B), 1.0) - 1.0
    inp['w_up'] = nrm((N_EVEN, LORA_W, W_B), LORA_W ** -0.5)
    inp['a0'] = nrm((N_EVEN, W_B), 0.5)
    inp['a_up'] = nrm((N_EVEN, LORA_A, W_B), LORA_A ** -0.5)
    inp['g_up'] = nrm((N_EVEN, LORA_G, W_B), LORA_G ** -0.5)
    inp['k_k'] = 0.85 + nrm((N_EVEN, W_B), 0.02)
    inp['k_a'] = 1.0 + nrm((N_EVEN, W_B), 0.02)
    inp['r_k'] = nrm((N_EVEN, H_B, N_B), 0.1)
    inp['lnx_g'] = 1.0 + nrm((N_EVEN, W_B), 0.02)
    inp['lnx_b'] = nrm((N_EVEN, W_B), 0.02)
    inp['w_in_o'] = nrm((N_ODD, d, 2 * E_C), d ** -0.5)
    inp['lnv_g'] = 1.0 + nrm((N_ODD, E_C), 0.02)
    inp['lnv_b'] = nrm((N_ODD, E_C), 0.02)
    inp['w_s'] = nrm((N_ODD, G_C, CHUNK, CHUNK), CHUNK ** -0.5)
    inp['b_s'] = 1.0 + nrm((N_ODD, G_C, CHUNK), 0.02)
    inp['w_out_o'] = nrm((N_ODD, E_C, d), E_C ** -0.5)
    inp['ffn_gate'] = nrm((N_EVEN, d, D_FF), d ** -0.5)
    inp['ffn_up'] = nrm((N_EVEN, d, D_FF), d ** -0.5)
    inp['ffn_down'] = nrm((N_EVEN, D_FF, d), D_FF ** -0.5)
    inp['router_w'] = nrm((N_ODD, d, N_EXPERTS), d ** -0.5)
    inp['router_b'] = nrm((N_ODD, N_EXPERTS), 0.01)
    inp['exp_gate'] = nrm((N_ODD, N_EXPERTS, d, D_FF_E), d ** -0.5)
    inp['exp_up'] = nrm((N_ODD, N_EXPERTS, d, D_FF_E), d ** -0.5)
    inp['exp_down'] = nrm((N_ODD, N_EXPERTS, D_FF_E, d), D_FF_E ** -0.5)
    return inp

def reference(x_prompt, x_sample, cache_k, cache_v, state_wkv, state_shift, page_table,
              c_prompt, c_sample, w_mod, b_mod, norm1_g, norm2_g, final_g, w_in_e, w_out_e,
              lam_q1, lam_k1, lam_q2, lam_k2, subln_g, mu_b, w0, w_up, a0, a_up, g_up,
              k_k, k_a, r_k, lnx_g, lnx_b, w_in_o, lnv_g, lnv_b, w_s, b_s, w_out_o,
              ffn_gate, ffn_up, ffn_down, router_w, router_b, exp_gate, exp_up, exp_down):
    p = dict(w_mod=w_mod, b_mod=b_mod, norm1_g=norm1_g, norm2_g=norm2_g, final_g=final_g,
             w_in_e=w_in_e, w_out_e=w_out_e, lam_q1=lam_q1, lam_k1=lam_k1, lam_q2=lam_q2,
             lam_k2=lam_k2, subln_g=subln_g, mu_b=mu_b, w0=w0, w_up=w_up, a0=a0, a_up=a_up,
             g_up=g_up, k_k=k_k, k_a=k_a, r_k=r_k, lnx_g=lnx_g, lnx_b=lnx_b, w_in_o=w_in_o,
             lnv_g=lnv_g, lnv_b=lnv_b, w_s=w_s, b_s=b_s, w_out_o=w_out_o, ffn_gate=ffn_gate,
             ffn_up=ffn_up, ffn_down=ffn_down, router_w=router_w, router_b=router_b,
             exp_gate=exp_gate, exp_up=exp_up, exp_down=exp_down)
    y_prompt, k_p, v_p, wkv_p, sh_p, _ = _forward(x_prompt, c_prompt, p, None, None, None, None, None)
    y_sample, k_s, v_s, wkv_s, sh_s, cv_s = _forward(x_sample, c_sample, p, cache_k, cache_v,
                                                     page_table, state_wkv, state_shift)
    return (y_prompt, y_sample, k_p, v_p, wkv_p, sh_p, k_s, v_s, wkv_s, sh_s, cv_s)


_drawn_inputs = setup_inputs


def setup_inputs(seed=0):
    import zlib

    import numpy as np

    out = dict(_drawn_inputs(seed))
    spreads = {}
    factors = {'norm2_g': 3.098,
     'final_g': 2.865,
     'lam_q1': 2.889,
     'lam_k1': 8.0,
     'lam_k2': 2.9,
     'subln_g': 3.677,
     'k_k': 5.546,
     'lnx_g': 3.262,
     'lnx_b': 3.568,
     'lnv_g': 2.779,
     'lnv_b': 2.853,
     'b_s': 5.323,
     'router_b': 4.023}
    for name, (base, spread) in spreads.items():
        noise = np.random.default_rng([zlib.crc32(name.encode()), seed]).standard_normal(out[name].shape)
        drawn = base * np.exp(spread * noise) if base else spread * noise
        out[name] = __import__('jax').numpy.asarray(drawn.astype(out[name].dtype))
    for name, factor in factors.items():
        out[name] = (out[name] * factor).astype(out[name].dtype)
    return out
```

```python
import math
from contextlib import ExitStack

import concourse.bass as bass
import numpy as np
from concourse import mybir

F32 = mybir.dt.float32
I32 = mybir.dt.int32
ALU = mybir.AluOpType
ACT = mybir.ActivationFunctionType
AX = mybir.AxisListType
ds = bass.ds

P = 128
D = 1024
KT = D // P
TP, NB, DS = 256, 8, 8
TS = NB * DS
T = TP + TS
NC_ = 1 + NB
PAST, PAGE = 1024, 128
NPG = PAST // PAGE
N_POOL = 80
H = 8
DK, DV = 32, 64
EC, GC, CHUNK = 2048, 8, 128
DFF, DFE, NE = 2816, 1408, 8
FT, FE = DFF // P, DFE // P
RING = 4
SLOT = 22 * P
CAP = 128
LAM_INIT = 0.8 - 0.6 * math.exp(0.0)
KAPPA = math.exp(-0.5)
SCALE = DK ** -0.5
RMS_EPS, LN_EPS, LNX_EPS = 1e-6, 1e-5, 64e-5
RC = 32
SH1, SC1, G1, SH2, SC2, G2 = (KT * i for i in range(6))

N_MOD, N_IN_E, N_OUT_E, N_GU, N_DN = 24, 13, 4, FT, 8
N_IN_O, N_OUT_O, N_EXP = 16, 8, FE + 4
G_MOD0 = 0
G_IN_E = G_MOD0 + N_MOD
G_MOD1 = G_IN_E + N_IN_E
G_OUT_E = G_MOD1 + N_MOD
G_GU = G_OUT_E + N_OUT_E
G_DN = G_GU + N_GU
G_IN_O = G_DN + N_DN
G_OUT_O = G_IN_O + N_IN_O
G_EXP = G_OUT_O + N_OUT_O
DONE0 = RING
READ0 = 2


class Steps:

    def __init__(self, sem, names, base=0):
        self.sem, self.names, self.base = sem, names, base

    def at(self, name, turn=0):
        return turn * len(self.names) + (self.base + self.names.index(name) + 1)


def by_four(eng, n, body):
    full = n // RING
    if full > 1:
        with eng.Fori(0, full) as i:
            for k in range(RING):
                body(i * RING + k, k, i)
    elif full:
        for k in range(RING):
            body(k, k, 0)
    for k in range(n % RING):
        body(full * RING + k, k, full)


def const_columns():
    p = np.arange(P)[:, None]
    f = np.arange(P)[None, :]
    c = {}
    c["ident"] = (p == f)
    c["block64"] = (p // 64 == f // 64)
    c["low16"] = (f < p) & (f // 16 == p // 16)
    c["up16"] = (p < f) & (f // 16 == p // 16)
    c["up32off"] = (p < f) & (f // 32 == p // 32) & (f // 16 != p // 16)
    c["up32"] = (p < f) & (f // 32 == p // 32)
    c["up32incl"] = (p <= f) & (f // 32 == p // 32)
    c["up"] = (p < f)
    c["upincl"] = (p <= f)
    c["upincl8"] = (p <= f) & (p // DS == f // DS)
    c["iota"] = f + 0 * p
    e = np.arange(64)[None, :]
    c["lower_e"] = (e % 8 < e // 8) & (p >= 0)
    c["slope"] = np.exp2(-8.0 * np.arange(1, H + 1) / H)[None, :] + 0 * p
    c["rowmask"] = (p // 32 == np.arange(4)[None, :])
    c["map0"] = ((p // DS) % 2 == 0)
    c["map1"] = ((p // DS) % 2 == 1)
    c["valid"] = np.stack([np.ones(P), np.ones(P), np.arange(P) < TS], 1)
    hq = (p // 16) * DS + p % DS
    c["pairsum"] = (hq == np.arange(64)[None, :])
    c["sumheads"] = (p % DS == np.arange(DS)[None, :])
    return {k: np.ascontiguousarray(v.astype(np.float32)) for k, v in c.items()}


def attention_constants():
    q = np.arange(P)[:, None]
    k = np.arange(TP)[None, :]
    dist = np.stack([np.where(k <= q + P * b, k - (q + P * b), -1e30) for b in range(2)], 1)
    r = np.arange(P)
    head, qs = r // 16, r % DS
    slope = np.exp2(-8.0 * (head + 1) / H)[:, None]
    pos = np.arange(PAST + DS)[None, :]
    qp = (PAST + qs)[:, None]
    bias = np.where(pos <= qp, -slope * np.abs(qp - pos), -1e30)
    rows = np.arange(P) % 64
    own = (rows[:, None] // DS == np.arange(512)[None, :] // DV)
    return np.concatenate([dist.reshape(P, -1), bias, own], 1).astype(np.float32)


def scan_mask():
    t = np.arange(T)
    keep = np.where(t < TP, t % RC != 0, (t - TP) % DS != 0)
    return np.ascontiguousarray(np.broadcast_to(np.tile(keep, 4), (P, 4 * T)).astype(np.float32))


def build(nc, a, o):
    ctx = ExitStack()
    with ctx:
        program(nc, ctx, a, o)


def program(nc, ctx, a, o):
    def sb(name, shape, dt=F32):
        return ctx.enter_context(nc.sbuf_tensor(name, shape, dt))

    def sem(name):
        return ctx.enter_context(nc.semaphore(name))

    ring = sb("ring", [P, RING, SLOT])
    xT = sb("xT", [P, KT, T])
    hT = sb("hT", [P, KT, T])
    modT = sb("modT", [P, 2, 48, NC_])
    bmod = sb("bmod", [P, 2, 48])
    gains = sb("gains", [P, 5, KT])
    sqbuf_cols = const_columns()
    n_const = sum(v.shape[1] for v in sqbuf_cols.values())
    consts = sb("consts", [P, n_const])
    cst, at = {}, 0
    for name, v in sqbuf_cols.items():
        cst[name] = consts[:, at:at + v.shape[1]]
        at += v.shape[1]
    ones = sb("ones", [P, P])
    cT = sb("cT", [P, KT, 32])
    gsc = sb("gsc", [P, KT, NC_])
    rstd = sb("rstd", [P, T])
    ptab = sb("ptab", [1, NB * NPG], I32)
    small = sb("small", [P, 64])
    colsE = sb("colsE", [P, 74])
    modrow = sb("modrow", [P, 2 * P])
    gtmp = sb("gtmp", [P, TS])
    lamw = sb("lamw", [P, 4, DK])
    shift_in = sb("shift_in", [P, 14, NB])
    shift_out = sb("shift_out", [P, 14, NC_])
    rounds_i = sb("rounds_i", [P, 2], I32)
    n_arena = nc.sbuf_bytes_remaining // 4 - 8
    arena = sb("arena", [P, n_arena])
    ps = ctx.enter_context(nc.psum_tensor("ps", [P, 8, 512], F32))

    class Area:

        def __init__(self, at=0):
            self.at = at

        def take(self, *shape):
            n = int(np.prod(shape))
            v = arena[:, self.at:self.at + n]
            self.at += n
            assert self.at <= n_arena, (self.at, n_arena)
            if len(shape) == 2:
                v = v.rearrange("p (a b) -> p a b", b=shape[1])
            elif len(shape) == 3:
                v = v.rearrange("p (a b c) -> p a b c", b=shape[1], c=shape[2])
            return v

    ident, block64 = cst["ident"], cst["block64"]
    mu, w0c, a0c, kkc, kac, rkc, lgc, lbc, sgc, lamv = (
        colsE[:, 0:14], colsE[:, 14:18], colsE[:, 18:22], colsE[:, 22:26], colsE[:, 26:30],
        colsE[:, 30:34], colsE[:, 34:38], colsE[:, 38:42], colsE[:, 42:43], colsE[:, 43:44])

    landed = [sem(f"weights_landed{s}") for s in range(RING)]
    chunk_done, chunk_read = sem("chunk_done"), sem("chunk_read")
    inputs_in, consts_in = sem("inputs_in"), sem("consts_in")
    stores = sem("stores")

    def slot(g0, k):
        return (g0 + k) % RING

    def use(g0, k, i):
        return i + (g0 + k) // RING

    def wait_weights(eng, g0, k, i):
        eng.wait_ge(landed[slot(g0, k)], 16 * (use(g0, k, i) + 1))

    def wait_psum(eng, g0, c):
        eng.wait_ge(chunk_read, c + (g0 + 1))

    def wait_done(eng, g0, c):
        eng.wait_ge(chunk_done, c + (g0 + 1 + DONE0))

    def pbank(g0, k):
        return 2 * ((g0 + k) % 2)

    def slot_view(g0, k, kt, n):
        return ring[:, slot(g0, k), 0:kt * n].rearrange("p (k n) -> p k n", n=n)

    silu_ready, modrow_ready, mod_turned, mod_ready = (
        sem("silu_ready"), sem("modrow_ready"), sem("mod_turned"), sem("mod_ready"))
    mod_evac_bank = 6

    def mod_tensor(pe, layer, u, g0):
        pe.wait_ge(silu_ready, 1)
        for k in range(4):
            wait_weights(pe, g0, k, u)
        pe.wait_ge(chunk_read, RING * u + (g0 + 1))
        for kt in range(KT):
            for k in range(4):
                mm = nc.tensor.matmul(ps[32 * k:32 * k + 32, 5, 0:2 * P], cT[:, kt, :],
                                      slot_view(g0, k, KT, 2 * P)[:, kt, :],
                                      start=kt == 0, stop=kt == KT - 1)
                if kt == KT - 1:
                    mm.then_inc(chunk_done, 1)
        pe.wait_ge(modrow_ready, u + (6 * layer + 1))
        for hh in range(2):
            mm = nc.tensor.transpose(ps[:, 6, hh * P:hh * P + P], modrow[:, hh * P:hh * P + P], ident)
        mm.then_inc(mod_turned, 1)

    def mod_scalar(act, layer, u, g0):
        act.wait_ge(chunk_done, RING * u + (g0 + RING + DONE0))
        if True:
            act.wait_ge(mod_ready, u + (6 * layer + 1))
        nc.scalar.activation(modrow[:, :], ps[:, 5, 0:2 * P], ACT.Copy).then_inc(chunk_read, 4)
        act.drain().then_inc(modrow_ready, 1)

    def mod_vector(dve, layer, u):
        dve.wait_ge(mod_turned, u + (6 * layer + 1))
        for hh in range(2):
            first = 8 * u + hh
            for k in range(4):
                at_ = layer * 48 + first + 2 * k
                flat = modT[:, :, :, :].rearrange("p l m c -> p (l m) c")
                fb = bmod[:, :, :].rearrange("p l m -> p (l m)")
                out = flat[:, ds(at_, 1), :]
                mm = nc.vector.tensor_scalar(
                    out, ps[:, 6:7, hh * P + 32 * k:hh * P + 32 * k + NC_],
                    fb[:, ds(at_, 1)], None, ALU.add)
        mm.then_inc(mod_ready, 1)

    area0 = Area(n_arena - KT * T)
    sq = area0.take(KT, T)
    sq_ready, ssum_ready, var_ready, root_ready, h_ready, x_ready = (
        sem("sq_ready"), sem("ssum_ready"), sem("var_ready"), sem("root_ready"), sem("h_ready"),
        sem("x_ready"))

    def norm_scalar(act, n):
        act.wait_ge(x_ready, n + 1)
        if n:
            act.wait_ge(ssum_ready, n)
        nc.scalar.activation(sq[:, :, :], xT[:, :, :], ACT.Square).then_inc(sq_ready, 1)
        act.wait_ge(var_ready, n + 1)
        nc.scalar.activation(rstd[:, :], rstd[:, :], ACT.Sqrt).then_inc(root_ready, 1)

    def norm_tensor(pe, n):
        pe.wait_ge(sq_ready, n + 1)
        for kt in range(KT):
            mm = nc.tensor.matmul(ps[:, 7, 0:T], ones[:, :], sq[:, kt, :], start=kt == 0,
                                  stop=kt == KT - 1)
        mm.then_inc(ssum_ready, 1)

    def norm_vector(dve, n, layer, sc, sh, mod_count):
        dve.wait_ge(ssum_ready, n + 1)
        nc.vector.tensor_scalar(rstd[:, :], ps[:, 7, 0:T], 1.0 / D, RMS_EPS, ALU.mult,
                                ALU.add).then_inc(var_ready, 1)
        if layer is not None:
            dve.wait_ge(mod_ready, mod_count + 1)
            dve.drain()
            nc.vector.scalar_tensor_tensor(
                gsc[:, :, :], modT[:, layer, sc:sc + KT, :], 1.0,
                gains[:, n, :].unsqueeze(2).to_broadcast([P, KT, NC_]), ALU.add, ALU.mult)
        dve.wait_ge(root_ready, n + 1)
        nc.vector.reciprocal(rstd[:, :], rstd[:, :])
        dve.drain()
        nc.vector.tensor_tensor(hT[:, :, :], xT[:, :, :],
                                rstd[:, :].unsqueeze(1).to_broadcast([P, KT, T]), ALU.mult)
        dve.drain()
        if layer is None:
            for kt in range(KT):
                last = nc.vector.tensor_scalar(hT[:, kt, :], hT[:, kt, :], gains[:, n, kt:kt + 1],
                                               None, ALU.mult)
        else:
            for kt in range(KT):
                nc.vector.tensor_scalar(hT[:, kt, 0:TP], hT[:, kt, 0:TP], gsc[:, kt, 0:1],
                                        modT[:, layer, sh + kt, 0:1], ALU.mult, ALU.add)
            hs = hT[:, :, TP:T].rearrange("p k (b s) -> p k b s", s=DS)
            full = [P, KT, NB, DS]
            nc.vector.tensor_tensor(hs, hs, gsc[:, :, 1:NC_].unsqueeze(3).to_broadcast(full),
                                    ALU.mult)
            dve.drain()
            last = nc.vector.tensor_tensor(
                hs, hs, modT[:, layer, sh:sh + KT, 1:NC_].unsqueeze(3).to_broadcast(full), ALU.add)
        last.then_inc(h_ready, 1)


    def residual_tile(dve, src, layer, gate, m, inc):
        flat = modT[:, :, :, :].rearrange("p l m c -> p (l m) c")
        row = flat[:, ds(m + (layer * 48 + gate), 1), :]
        x = xT[:, ds(m, 1), :]
        nc.vector.scalar_tensor_tensor(x[:, :, 0:TP], src[:, :, 0:TP], row[:, 0, 0:1],
                                       x[:, :, 0:TP], ALU.mult, ALU.add)
        g = row[:, 0, 1:NC_].unsqueeze(2).to_broadcast([P, NB, DS])
        t3 = gtmp[:, :].rearrange("p (b s) -> p b s", s=DS)
        dve.drain()
        nc.vector.tensor_tensor(t3, src[:, 0, TP:T].rearrange("p (b s) -> p b s", s=DS), g,
                                ALU.mult)
        dve.drain()
        ins = nc.vector.tensor_tensor(x[:, 0, TP:T], x[:, 0, TP:T], gtmp[:, :], ALU.add)
        if inc is not None:
            ins.then_inc(inc, 1)

    def columns_tensor(pe, g0, n, kt, tiles, rhs, first_wait):
        first_wait(pe)

        def body(c, k, i):
            wait_weights(pe, g0, k, i)
            wait_psum(pe, g0, c)
            w = slot_view(g0, k, kt, tiles * P)
            for t in range(tiles):
                for q in range(kt):
                    mm = nc.tensor.matmul(ps[:, pbank(g0, k) + t, 0:T], w[:, q, t * P:t * P + P],
                                          rhs[:, q, :], start=q == 0, stop=q == kt - 1)
            mm.then_inc(chunk_done, 1)
        by_four(pe, n, body)

    def residual_vector(dve, g0, n, tiles, layer, gate):
        def body(c, k, i):
            dve.drain()
            wait_done(dve, g0, c)
            for t in range(tiles):
                if t:
                    dve.drain()
                residual_tile(dve, ps[:, pbank(g0, k) + t:pbank(g0, k) + t + 1, :], layer, gate,
                              c * tiles + t, chunk_read if t == tiles - 1 else None)
        by_four(dve, n, body)
        dve.drain().then_inc(x_ready, 1)

    aA = Area(0)
    projT = aA.take(26, T)
    xb = projT[:, 12:26, :]
    base_b = aA.at
    proj_ready = sem("proj_ready")
    mixT = hT

    def in_e_scalar(act):
        def body(c, k, i):
            wait_done(act, G_IN_E, c)
            nc.scalar.activation(projT[:, ds(2 * c, 2), :],
                                 ps[:, pbank(G_IN_E, k):pbank(G_IN_E, k) + 2, 0:T],
                                 ACT.Copy).then_inc(chunk_read, 1)
        by_four(act, N_IN_E, body)
        act.drain().then_inc(proj_ready, 1)

    aB = Area(base_b)
    attc = aB.take(2 * TP + PAST + DS + 512)
    dist = attc[:, 0:2 * TP].rearrange("p (b k) -> p b k", b=2)
    biasS = attc[:, 2 * TP:2 * TP + PAST + DS]
    ownhead = attc[:, 2 * TP + PAST + DS:]
    Kp, Vp = [], []
    for _ in range(2):
        kv_at = aB.at
        Kp.append(aB.take(NPG, 4, P))
        Vp.append(aB.take(NPG, 512))
    sS = [aB.take(PAST + DS) for _ in range(2)]
    Qs = [aB.take(4, 32) for _ in range(2)]
    kvn = [aB.take(8, DS) for _ in range(2)]
    vn = [aB.take(512) for _ in range(2)]
    Cm = [aB.take(64) for _ in range(2)]
    prTs = [aB.take(NPG, 64) for _ in range(2)]
    prn = [aB.take(64) for _ in range(2)]
    om = [sS[par][:, 0:512] for par in range(2)]
    aP = Area(kv_at)
    Vtok = aP.take(2, 512)
    Qm = aP.take(4, TP)
    Vst = aP.take(2, P)
    sP = [aP.take(4, TP) for _ in range(2)]
    prP = [aP.take(2, TP) for _ in range(2)]
    prPT = [aP.take(4, P) for _ in range(2)]
    lam = small[:, 0:1]
    nmaxP, lP = small[:, 2:10], small[:, 10:18]
    nmaxS, lS = small[:, 18:20], small[:, 20:22]
    coef = small[:, 22:23]
    lamt = small[:, 24:28]

    vtok_pe, vtok_act = sem("vtok_turned"), sem("vtok_ready")
    lam_d, lam_a, lam_ready = sem("lam_dots"), sem("lam_exps"), sem("lam_ready")
    pa_pe = Steps(sem("pattn_pe"), ["S0", "S1", "prT0", "prT1", "o0", "o1"])
    pa_dve = Steps(sem("pattn_dve"), ["stage", "smax0", "smax1", "pr0", "pr1"])
    pa_act = Steps(sem("pattn_act"), ["exp0", "exp1", "prTs0", "prTs1", "os0", "os1"])

    def lambda_vector(dve):
        dve.wait_ge(consts_in, 16 * N_CONST_LOADS)
        nc.vector.tensor_tensor(lamw[:, 0:4:2, :], lamw[:, 0:4:2, :], lamw[:, 1:4:2, :], ALU.mult)
        dve.drain()
        nc.vector.tensor_reduce(lamt[:, 0:2], lamw[:, 0:4:2, :], AX.X, ALU.add).then_inc(lam_d, 1)
        dve.wait_ge(lam_a, 1)
        nc.vector.tensor_tensor(lam, lamt[:, 2:3], lamt[:, 3:4], ALU.subtract)
        dve.drain()
        nc.vector.tensor_scalar(lam, lam, LAM_INIT, None, ALU.add)
        dve.drain()
        nc.vector.tensor_scalar(coef, cst["map1"], lam, -1.0, ALU.mult, ALU.mult)
        dve.drain()
        nc.vector.tensor_tensor(coef, coef, cst["map0"], ALU.add).then_inc(lam_ready, 1)

    def lambda_scalar(act):
        act.wait_ge(lam_d, 1)
        nc.scalar.activation(lamt[:, 2:4], lamt[:, 0:2], ACT.Exp).then_inc(lam_a, 1)

    def vtok_tensor(pe):
        pe.wait_ge(proj_ready, 1)
        for n in range(2):
            for j in range(4):
                mm = nc.tensor.transpose(ps[:, n, j * P:j * P + P], projT[:, 8 + j, n * P:n * P + P],
                                         ident)
        mm.then_inc(vtok_pe, 1)

    def vtok_scalar(act):
        act.wait_ge(vtok_pe, 1)
        nc.scalar.activation(Vtok[:, :, :], ps[:, 0:2, :], ACT.Copy).then_inc(vtok_act, 1)

    def pattn_tensor(pe, j):
        for b in range(2):
            if b == 0:
                pe.wait_ge(pa_dve.sem, pa_dve.at("stage", j))
            for i in range(4):
                mm = nc.tensor.matmul(ps[:, 2 * b + i // 2, (i % 2) * TP:(i % 2) * TP + TP],
                                      Qm[:, i, b * P:b * P + P], projT[:, ds(j + 4, 1), 0:TP],
                                      start=True, stop=True)
            mm.then_inc(pa_pe.sem, 1)
        for b in range(2):
            pe.wait_ge(pa_dve.sem, pa_dve.at(f"pr{b}", j))
            for h2 in range(2):
                for kt in range(2):
                    mm = nc.tensor.transpose(ps[:, 4 + 3 * b, (2 * h2 + kt) * P:(2 * h2 + kt + 1) * P],
                                             prP[b][:, h2, kt * P:kt * P + P], ident)
            mm.then_inc(pa_pe.sem, 1)
        for b in range(2):
            pe.wait_ge(pa_act.sem, pa_act.at(f"prTs{b}", j))
            for h2 in range(2):
                for kt in range(b + 1):
                    mm = nc.tensor.matmul(ps[64 * h2:64 * h2 + 64, b, 0:P],
                                          Vst[:, kt, 64 * h2:64 * h2 + 64],
                                          prPT[b][:, 2 * h2 + kt, :], start=kt == 0, stop=kt == b)
            mm.then_inc(pa_pe.sem, 1)

    def pattn_vector(dve, j):
        dve.wait_ge(pa_pe.sem, 6 * j + PA0)
        for i in range(4):
            nc.vector.tensor_scalar(Qm[:, i:i + 1, :], projT[:, ds(j, 1), 0:TP],
                                    cst["rowmask"][:, i:i + 1], SCALE, ALU.mult, ALU.mult)
        nc.vector.tensor_copy(Vst[:, :, :], Vtok[:, :, ds(j * P, P)]).then_inc(pa_dve.sem, 1)
        for b in range(2):
            dve.wait_ge(pa_pe.sem, pa_pe.at(f"S{b}", j) + PA0)
            for h2 in range(2):
                nc.vector.scalar_tensor_tensor(
                    sP[b][:, 2 * h2:2 * h2 + 2, :], dist[:, b, :].unsqueeze(1).to_broadcast([P, 2, TP]),
                    cst["slope"][:, ds(2 * j + h2, 1)],
                    ps[:, 2 * b + h2, :].rearrange("p (m k) -> p m k", m=2), ALU.mult, ALU.add)
            dve.drain()
            nc.vector.tensor_reduce(nmaxP[:, 4 * b:4 * b + 4], sP[b][:, :, :], AX.X, ALU.max)
            dve.drain()
            nc.vector.tensor_scalar(nmaxP[:, 4 * b:4 * b + 4], nmaxP[:, 4 * b:4 * b + 4], -1.0,
                                    None, ALU.mult).then_inc(pa_dve.sem, 1)
        for b in range(2):
            dve.wait_ge(pa_act.sem, pa_act.at(f"exp{b}", j))
            l = lP[:, 4 * b:4 * b + 4]
            nc.vector.reciprocal(l, l)
            dve.drain()
            nc.vector.tensor_scalar(l[:, 1:4:2], l[:, 1:4:2], lam, None, ALU.mult)
            dve.drain()
            for h2 in range(2):
                nc.vector.tensor_scalar(sP[b][:, 2 * h2 + 1, :], sP[b][:, 2 * h2 + 1, :],
                                        l[:, 2 * h2 + 1:2 * h2 + 2], None, ALU.mult)
            dve.drain()
            for h2 in range(2):
                last = nc.vector.scalar_tensor_tensor(
                    prP[b][:, h2, :], sP[b][:, 2 * h2, :], l[:, 2 * h2:2 * h2 + 1],
                    sP[b][:, 2 * h2 + 1, :], ALU.mult, ALU.subtract)
            last.then_inc(pa_dve.sem, 1)

    def pattn_scalar(act, j):
        for b in range(2):
            act.wait_ge(pa_dve.sem, pa_dve.at(f"smax{b}", j))
            for i in range(4):
                last = nc.scalar.activation(sP[b][:, i, :], sP[b][:, i, :], ACT.Exp,
                                            bias=nmaxP[:, 4 * b + i:4 * b + i + 1],
                                            accum_out=lP[:, 4 * b + i:4 * b + i + 1])
            last.then_inc(pa_act.sem, 1)
        for b in range(2):
            act.wait_ge(pa_pe.sem, pa_pe.at(f"prT{b}", j) + PA0)
            nc.scalar.activation(prPT[b][:, :, :].rearrange("p a k -> p (a k)"),
                                 ps[:, 4 + 3 * b, :], ACT.Copy).then_inc(pa_act.sem, 1)
        for b in range(2):
            act.wait_ge(pa_pe.sem, pa_pe.at(f"o{b}", j) + PA0)
            nc.scalar.activation(mixT[:, ds(j, 1), b * P:b * P + P], ps[:, b:b + 1, 0:P],
                                 ACT.Copy).then_inc(pa_act.sem, 1)

    PA0 = 1

    k_landed = [sem(f"k_pages{i}") for i in range(2)]
    v_landed = [sem(f"v_pages{i}") for i in range(2)]
    SA = ["q0", "q1", "smax0", "smax1", "cm0", "om0", "cm1", "om1"]
    sa_dve = Steps(sem("sattn_dve"), SA)
    sa_pe = Steps(sem("sattn_pe"), ["S0", "S1", "PT0", "O0", "F0", "PT1", "O1", "F1"], 1)
    sa_act = Steps(sem("sattn_act"), ["vn0", "exp0", "vn1", "exp1", "pT0", "ms0", "pT1", "ms1"], 1)
    pattn_over = sem("prompt_attention_over")

    def sattn_load(pool):
        pool.wait_ge(consts_in, 16 * N_CONST_LOADS)
        k_h, v_h = a["cache_k"], a["cache_v"]
        pool.wait_ge(shift_done, 1)
        with pool.Fori(0, NB // 2) as i:
            for par in range(2):
                pool.wait_ge(sa_pe.sem, 8 * i + 1)
                if par == 1:
                    pool.wait_ge(pa_pe.sem, 4 * 6 + PA0)
                for g in range(NPG):
                    page = pool.value_load(ptab[0:1, ds(i * (2 * NPG) + (par * NPG + g), 1)],
                                           min_val=0, max_val=N_POOL - 1)
                    pool.dma_start(Kp[par][:, g, :, :].rearrange("p j n -> p (j n)"),
                                   k_h[ds(page, 1)].rearrange("o p n -> p (o n)")
                                   ).then_inc(k_landed[par], 16)
                    pool.dma_start(Vp[par][:, g, :],
                                   v_h[ds(page, 1)].rearrange("o p n -> p (o n)")
                                   ).then_inc(v_landed[par], 16)

    def sattn_vector(dve, i):
        for par in range(2):
            dve.wait_ge(sa_pe.sem, sa_pe.at("F1", i) - 8)
            tok = i * (2 * DS) + (TP + par * DS)
            for r in range(4):
                nc.vector.tensor_scalar(Qs[par][:, :, 8 * r:8 * r + 8], projT[:, 0:4, ds(tok, DS)],
                                        cst["rowmask"][:, r:r + 1], SCALE, ALU.mult, ALU.mult)
            nc.vector.tensor_copy(kvn[par][:, :, :], projT[:, 4:12, ds(tok, DS)]
                                  ).then_inc(sa_dve.sem, 1)
        for par in range(2):
            dve.wait_ge(sa_pe.sem, sa_pe.at(f"S{par}", i))
            s = sS[par]
            nc.vector.tensor_tensor(s[:, 0:PAST].rearrange("p (h k) -> p h k", h=2),
                                    ps[:, 2 * par:2 * par + 2, :],
                                    biasS[:, 0:PAST].rearrange("p (h k) -> p h k", h=2), ALU.add)
            nc.vector.tensor_tensor(s[:, PAST:PAST + DS], ps[:, 4 + par, 0:DS],
                                    biasS[:, PAST:PAST + DS], ALU.add)
            dve.drain()
            nm = nmaxS[:, par:par + 1]
            nc.vector.tensor_reduce(nm, s, AX.X, ALU.max)
            dve.drain()
            nc.vector.tensor_scalar(nm, nm, -1.0, None, ALU.mult).then_inc(sa_dve.sem, 1)
        for par in range(2):
            dve.wait_ge(sa_act.sem, sa_act.at(f"exp{par}", i))
            l = lS[:, par:par + 1]
            nc.vector.reciprocal(l, l)
            dve.drain()
            nc.vector.tensor_scalar(Cm[par], cst["pairsum"], l, coef, ALU.mult,
                                    ALU.mult).then_inc(sa_dve.sem, 1)
            dve.wait_ge(sa_pe.sem, sa_pe.at(f"O{par}", i))
            nc.vector.tensor_tensor(om[par], ps[:, 6 + par, :], ownhead, ALU.mult
                                    ).then_inc(sa_dve.sem, 1)

    def sattn_tensor(pe, i):
        pe.wait_ge(sa_act.sem, 8 * i + 1)
        for par in range(2):
            pe.wait_ge(sa_dve.sem, sa_dve.at(f"q{par}", i))
            pe.wait_ge(k_landed[par], 16 * NPG * (i + 1))
            for hf in range(2):
                for j in range(4):
                    nc.tensor.matmul(ps[32 * j:32 * j + 32, 2 * par + hf, :], Qs[par][:, j, :],
                                     Kp[par][:, 4 * hf:4 * hf + 4, j, :], start=True, stop=True)
            for j in range(4):
                nc.tensor.matmul(ps[32 * j:32 * j + 32, 4 + par, 0:DS], Qs[par][:, j, :],
                                 kvn[par][:, j, :], start=True, stop=True)
            for j in range(4):
                mm = nc.tensor.transpose(ps[0:DS, 6 + par, j * P:j * P + P], kvn[par][:, 4 + j, :],
                                         ident)
            mm.then_inc(sa_pe.sem, 1)
        for par in range(2):
            pe.wait_ge(sa_dve.sem, sa_dve.at(f"cm{par}", i))
            for g in range(NPG):
                nc.tensor.matmul(ps[:, 2 * par, 64 * g:64 * g + 64], sS[par][:, g * P:g * P + P],
                                 Cm[par], start=True, stop=True)
            mm = nc.tensor.matmul(ps[0:DS, 2 * par + 1, 0:64], sS[par][:, PAST:PAST + DS], Cm[par],
                                  start=True, stop=True)
            mm.then_inc(sa_pe.sem, 1)
            pe.wait_ge(sa_act.sem, sa_act.at(f"pT{par}", i))
            pe.wait_ge(v_landed[par], 16 * NPG * (i + 1))
            nc.tensor.matmul(ps[0:64, 6 + par, :], prn[par][0:DS, :], vn[par][0:DS, :],
                             start=True, stop=False)
            for g in range(NPG):
                half = 64 * (g % 2)
                mm = nc.tensor.matmul(ps[half:half + 64, 6 + par, :], prTs[par][:, g, :],
                                      Vp[par][:, g, :], start=g == 1, stop=g >= NPG - 2)
            mm.then_inc(sa_pe.sem, 1)
            pe.wait_ge(sa_dve.sem, sa_dve.at(f"om{par}", i))
            for j in range(4):
                mm = nc.tensor.matmul(ps[:, 2 * par + 1, 64 + DS * j:64 + DS * j + DS],
                                      om[par][:, j * P:j * P + P], cst["sumheads"],
                                      start=True, stop=True)
            mm.then_inc(sa_pe.sem, 1)

    def sattn_scalar(act, i):
        for par in range(2):
            act.wait_ge(sa_pe.sem, sa_pe.at(f"S{par}", i))
            nc.scalar.activation(vn[par][0:DS, :], ps[0:DS, 6 + par, :], ACT.Copy
                                 ).then_inc(sa_act.sem, 1)
            act.wait_ge(sa_dve.sem, sa_dve.at(f"smax{par}", i))
            nc.scalar.activation(sS[par], sS[par], ACT.Exp, bias=nmaxS[:, par:par + 1],
                                 accum_out=lS[:, par:par + 1]).then_inc(sa_act.sem, 1)
        for par in range(2):
            act.wait_ge(sa_pe.sem, sa_pe.at(f"PT{par}", i))
            nc.scalar.activation(prn[par][0:DS, :], ps[0:DS, 2 * par + 1, 0:64], ACT.Copy)
            nc.scalar.activation(prTs[par][:, :, :].rearrange("p g n -> p (g n)"),
                                 ps[:, 2 * par, :], ACT.Copy).then_inc(sa_act.sem, 1)
            act.wait_ge(sa_pe.sem, sa_pe.at(f"F{par}", i))
            nc.scalar.activation(
                mixT[:, 0:4, ds(i * (2 * DS) + (TP + par * DS), DS)],
                ps[:, 2 * par + 1, 64:64 + 4 * DS].rearrange("p (j s) -> p j s", s=DS),
                ACT.Copy).then_inc(sa_act.sem, 1)

    sub_sq = arena[:, 26 * T:30 * T].rearrange("p (j t) -> p j t", t=T)
    sub = {n: sem(f"subnorm_{n}") for n in ("sq", "sum", "var", "root", "done")}

    def subnorm_scalar(act):
        act.drain()
        nc.scalar.activation(sub_sq[:, :, :], mixT[:, 0:4, :], ACT.Square).then_inc(sub["sq"], 1)
        act.wait_ge(sub["var"], 1)
        nc.scalar.activation(sub_sq[:, :, :], sub_sq[:, :, :], ACT.Sqrt).then_inc(sub["root"], 1)

    def subnorm_tensor(pe):
        pe.wait_ge(sub["sq"], 1)
        for j in range(4):
            mm = nc.tensor.matmul(ps[:, j, 0:T], block64, sub_sq[:, j, :], start=True, stop=True)
        mm.then_inc(sub["sum"], 1)

    def subnorm_vector(dve):
        dve.wait_ge(sub["sum"], 1)
        nc.vector.tensor_scalar(sub_sq[:, :, :], ps[:, 0:4, 0:T], 1.0 / DV, RMS_EPS, ALU.mult,
                                ALU.add).then_inc(sub["var"], 1)
        dve.wait_ge(sub["root"], 1)
        nc.vector.reciprocal(sub_sq[:, :, :], sub_sq[:, :, :])
        dve.drain()
        nc.vector.tensor_tensor(mixT[:, 0:4, :], mixT[:, 0:4, :], sub_sq[:, :, :], ALU.mult)
        dve.drain()
        nc.vector.tensor_scalar(mixT[:, 0:4, :], mixT[:, 0:4, :], sgc, 1.0 - LAM_INIT, ALU.mult,
                                ALU.mult).then_inc(sub["done"], 1)

    xr, xk, xv = xb[:, 0:4, :], xb[:, 4:8, :], xb[:, 8:12, :]
    aR1 = Area(0)
    cumprev = aR1.take(4, T)
    cum = aR1.take(4, T)
    kk = aR1.take(4, T)
    aR = Area(base_b)
    kmod = aR.take(4, T)
    nb = aR.take(4, T)
    gup = aR.take(512)
    st = aR.take(5, 4 * P)
    stR, stQ, stK, stB, stV = (st[:, n, :].rearrange("p (j t) -> p j t", t=P) for n in range(5))
    ATm = aR.take(2, 512)
    S9 = aR.take(9, 256)
    Cst = aR.take(2, 256)
    Sbd = aR.take(2, 512)
    T1 = aR.take(256)
    T2 = aR.take(256)
    RW = aR.take(4, P)
    Y0 = aR.take(4, P)
    tokK, tokB, tokV = (aR.take(512) for _ in range(3))
    mats_at = aR.at
    mats = [{n: aR.take(512) for n in ("A0", "A1", "A2", "G", "ET", "MT", "NT", "QT", "X")}
            for _ in range(2)]
    ZF = aR.take(1024)
    for x in range(2):
        mats[x]["A3"] = ZF[:, 512 * x:512 * x + 512]
    pend = aR.take(4, 4)
    ex1, ex2, ex3 = (mats[0][n].rearrange("p (j t) -> p j t", t=P) for n in ("A0", "A1", "A2"))
    aM = Area(mats_at)
    scan_keep = aM.take(4 * T)
    waup = aM.take(512)
    aval = aM.take(4, T)
    tmpR = aM.take(4, T)
    yT = mixT[:, 4:8, :]
    post_sq = tmpR
    gg, bonus = cumprev, kk
    aD = Area(base_b + 2 * TP + PAST + DS + 512)
    diff = aD.take(14, T)

    shift_done, shift_saved = sem("token_shift_done"), sem("shift_saved")
    kv_stored, ones_ready = sem("outputs_stored"), sem("ones_ready")
    rwkv_in, attn_over = sem("rwkv_loads"), sem("attention_over")
    mix_ready = sem("mix_ready")
    rw_over = sem("rwkv_over")

    def shift_vector(dve):
        pb = projT[:, 12:26, :]
        dve.wait_ge(proj_ready, 1)
        nc.vector.tensor_copy(shift_out[:, :, :], pb[:, :, TP - 1:T:DS]).then_inc(shift_saved, 1)
        nc.vector.tensor_tensor(diff[:, :, 1:T], pb[:, :, 0:T - 1], pb[:, :, 1:T], ALU.subtract)
        dve.drain()
        nc.vector.tensor_scalar(diff[:, :, 0:1], pb[:, :, 0:1], -1.0, None, ALU.mult)
        nc.vector.tensor_tensor(diff[:, :, TP:T:DS], shift_in[:, :, :], pb[:, :, TP:T:DS],
                                ALU.subtract)
        dve.drain()
        for m in range(14):
            last = nc.vector.scalar_tensor_tensor(pb[:, m, :], diff[:, m, :], mu[:, m:m + 1],
                                                  pb[:, m, :], ALU.mult, ALU.add)
        last.then_inc(shift_done, 1)

    rp = {n: sem("rwkv_" + n) for n in ("gates", "lora", "sig", "kk_sq", "kk_sum", "kk_root",
                                        "kk_read", "prep")}

    def rwkv_loads(pool):
        pool.wait_ge(sub["done"], 1)
        pool.wait_ge(attn_over, 1)
        pool.wait_ge(kv_stored, 32)
        for dst, src in ((waup, a["wa_up"]), (gup, a["g_up"]), (scan_keep, a["scan_keep"]),
                         (S9[:, 1:9, :], a["s_init"])):
            pool.dma_start(dst, src).then_inc(rwkv_in, 16)

    def rwkv_prep_scalar(act):
        act.drain().then_inc(attn_over, 1)
        act.wait_ge(shift_done, 1)
        nc.scalar.activation(xb[0:64, 12, :], xb[0:64, 12, :], ACT.Tanh)
        nc.scalar.activation(xb[:, 13, :], xb[:, 13, :], ACT.Sigmoid).then_inc(rp["gates"], 1)
        act.wait_ge(rp["lora"], 1)
        act.wait_ge(kv_stored, 32)
        for j in range(4):
            nc.scalar.activation(cumprev[:, j, :], ps[:, j, 0:T], ACT.Sigmoid, bias=w0c[:, j:j + 1])
        for j in range(4):
            last = nc.scalar.activation(aval[:, j, :], ps[:, 4 + j, 0:T], ACT.Sigmoid,
                                        bias=a0c[:, j:j + 1])
        last.then_inc(rp["sig"], 1)
        act.wait_ge(rp["kk_sum"], 1)
        nc.scalar.activation(tmpR[:, :, :], ps[:, 0:4, 0:T], ACT.Sqrt).then_inc(rp["kk_root"], 1)

    def rwkv_prep_tensor(pe):
        pe.wait_ge(rp["gates"], 1)
        pe.wait_ge(rwkv_in, 64)
        pe.wait_ge(sub["var"], 1)
        for j in range(4):
            nc.tensor.matmul(ps[:, j, 0:T], waup[0:64, j * P:j * P + P], xb[0:64, 12, :],
                             start=True, stop=True)
        for j in range(4):
            mm = nc.tensor.matmul(ps[:, 4 + j, 0:T], waup[64:P, j * P:j * P + P], xb[64:P, 12, :],
                                  start=True, stop=True)
        mm.then_inc(rp["lora"], 1)
        pe.wait_ge(rp["kk_sq"], 1)
        pe.wait_ge(rp["sig"], 1)
        for j in range(4):
            mm = nc.tensor.matmul(ps[:, j, 0:T], block64, tmpR[:, j, :], start=True, stop=True)
        mm.then_inc(rp["kk_sum"], 1)

    def rwkv_prep_vector(dve):
        dve.wait_ge(rwkv_in, 64)
        for j in range(4):
            nc.vector.tensor_scalar(kk[:, j, :], xk[:, j, :], kkc[:, j:j + 1], None, ALU.mult)
        nc.vector.memset(S9[:, 0, :], 0.0)
        nc.vector.memset(Sbd[:, :, :], 0.0)
        dve.drain()
        nc.vector.tensor_tensor(tmpR[:, :, :], kk[:, :, :], kk[:, :, :], ALU.mult
                                ).then_inc(rp["kk_sq"], 1)
        dve.wait_ge(rp["sig"], 1)
        flat = "p j t -> p (j t)"
        nc.vector.tensor_tensor_scan(cum[:, :, :].rearrange(flat), scan_keep,
                                     cumprev[:, :, :].rearrange(flat), 0.0, ALU.mult, ALU.add)
        dve.drain()
        nc.vector.tensor_tensor(cumprev[:, :, :], cum[:, :, :], cumprev[:, :, :], ALU.subtract)
        for j in range(4):
            nc.vector.tensor_scalar(kmod[:, j, :], aval[:, j, :], 1.0, kac[:, j:j + 1],
                                    ALU.subtract, ALU.mult)
        dve.drain()
        nc.vector.scalar_tensor_tensor(kmod[:, :, :].rearrange(flat), kmod[:, :, :].rearrange(flat),
                                       1.0, xk[:, :, :].rearrange(flat), ALU.add, ALU.mult)
        dve.wait_ge(rp["kk_root"], 1)
        nc.vector.tensor_scalar(tmpR[:, :, :], tmpR[:, :, :], 1e-12, None, ALU.max)
        dve.drain()
        nc.vector.reciprocal(tmpR[:, :, :], tmpR[:, :, :])
        dve.drain()
        nc.vector.tensor_tensor(kk[:, :, :], kk[:, :, :], tmpR[:, :, :], ALU.mult)
        dve.drain()
        nc.vector.scalar_tensor_tensor(nb[:, :, :].rearrange(flat), kk[:, :, :].rearrange(flat),
                                       -1.0, aval[:, :, :].rearrange(flat), ALU.mult, ALU.mult)
        dve.drain().then_inc(rp["prep"], 1)

    PER = ["turn"] + [f"{x}{h}" for x in ("s1", "s2", "s3", "s4", "s5", "s6", "s7", "s8")
                      for h in range(2)]
    PER += ["yr", "wc0", "wc1", "y0", "wc2", "y1", "wc3", "y2", "y3"]
    DVR = ["prod"] + [f"m1{h}" for h in range(2)] + [f"qx{h}" for h in range(2)]
    DVR += [f"g{n}{h}" for n in (1, 2, 3) for h in range(2)] + [f"zf{h}" for h in range(2)]
    DVR += ["rw", "ac0", "ac1", "s0", "ac2", "s1", "ac3", "s2", "s3", "yt"]
    ACR = ["exps", "tok"] + [f"{x}{h}" for x in ("sq2", "sq4", "sq8", "z", "ez") for h in range(2)]
    ACR += ["y0"] + [f"bd{c}" for c in range(4)]
    r_pe, r_dve, r_act = sem("rtile_pe"), sem("rtile_dve"), sem("rtile_act")
    rpe = [Steps(r_pe, PER, x * 2 * len(PER)) for x in range(2)]
    RD0 = 1
    rdve = [Steps(r_dve, DVR, x * 2 * len(DVR) + RD0) for x in range(2)]
    ract = [Steps(r_act, ACR, x * 2 * len(ACR)) for x in range(2)]

    UW = ZF.rearrange("p (j u h v) -> p j u h v", j=4, u=2, h=2)

    def heads4(m):
        return m.rearrange("p (h t) -> p h t", t=P)

    def tile_views(part, i):
        if part == 0:
            return (lambda x: x[:, :, ds(i * P, P)], lambda x: x, lambda x: x, P)
        four = "p j (b s) -> p j b s"
        return (lambda x: x[:, :, ds(i * 4 * DS + TP, 4 * DS)].rearrange(four, s=DS),
                lambda x: x.rearrange("p j (b s) -> p j b s", s=RC)[:, :, :, 0:DS],
                lambda x: x[:, :, 0:4 * DS].rearrange(four, s=DS), 4 * DS)

    def state(part, i, cc):
        return S9[:, 0:1, :] if part == 0 else S9[:, ds(i * 4 + (cc + 1), 1), :]

    def rtile_vector(dve, part, i):
        col, stg, comp, n = tile_views(part, i)
        D_, A_, P_ = rdve[part], ract[part], rpe[part]
        dve.wait_ge(r_act, A_.at("exps", i))
        for dst, x, e in ((stR, xr, ex1), (stQ, kk, ex3), (stK, kmod, ex2), (stB, nb, ex2)):
            nc.vector.tensor_tensor(stg(dst), col(x), comp(e), ALU.mult)
        nc.vector.tensor_copy(stg(stV), col(xv))
        step = n // 4
        nc.vector.tensor_copy(pend[:, :, :], ex1[:, :, step - 1:n:step]).then_inc(r_dve, 1)

        def masked(dst, b, mask):
            nc.vector.tensor_tensor(heads4(dst), heads4(ps[:, b, :]),
                                    cst[mask].unsqueeze(1).to_broadcast([P, 4, P]), ALU.mult)
        for h in range(2):
            m, b = mats[h], 4 * h
            dve.wait_ge(r_pe, P_.at(f"s1{h}", i))
            masked(m["A0"], b, "low16")
            masked(m["A1"], b + 1, "up16")
            masked(m["ET"], b + 1, "up32off")
            masked(m["MT"], b + 2, "up32")
            masked(m["NT"], b + 3, "up32incl")
            dve.drain()
            nc.vector.tensor_tensor(heads4(m["G"]), heads4(m["A1"]),
                                    ident.unsqueeze(1).to_broadcast([P, 4, P]), ALU.add
                                    ).then_inc(r_dve, 1)
        for h in range(2):
            m, b = mats[h], 4 * h
            dve.wait_ge(r_pe, P_.at(f"s2{h}", i))
            masked(m["QT"], b + 2, "up32incl")
            nc.vector.tensor_copy(heads4(m["X"])[:, :, 0:64],
                                  ps[:, b + 3, 0:256].rearrange("p (k v) -> p k v", v=64)
                                  ).then_inc(r_dve, 1)
        for s, src in (("s3", 2), ("s4", 3), ("s5", 1)):
            for h in range(2):
                m, b = mats[h], 4 * h
                dve.wait_ge(r_pe, P_.at(f"{s}{h}", i))
                nc.vector.tensor_tensor(m["G"], m["G"], ps[:, b + src, :], ALU.add
                                        ).then_inc(r_dve, 1)
        for h in range(2):
            m, b = mats[h], 4 * h
            dve.wait_ge(r_pe, P_.at(f"s8{h}", i))
            v = "p (k u v) -> p k u v"
            nc.vector.tensor_tensor(UW[:, :, :, h, :], m["A0"].rearrange(v, u=2, v=64),
                                    ps[:, b, :].rearrange(v, u=2, v=64), ALU.add
                                    ).then_inc(r_dve, 1)
        dve.wait_ge(r_pe, P_.at("yr", i))
        nc.vector.tensor_tensor(RW[:, :, :].rearrange("p j t -> p (j t)"), st[:, 0, :],
                                ps[:, 1, :], ALU.add).then_inc(r_dve, 1)

        def chunk_matrices(cc):
            dve.wait_ge(r_pe, P_.at(f"wc{cc}", i))
            t = cc % 2
            nc.vector.tensor_tensor(heads4(ATm[:, t, :]), heads4(ps[:, 2 + 2 * t, :]),
                                    block64.unsqueeze(1).to_broadcast([P, 4, P]), ALU.mult)
            for q in (0, 64):
                last = nc.vector.tensor_tensor(
                    Cst[q:q + 64, t, :].rearrange("p (j v) -> p j v", v=64),
                    heads4(ps[q:q + 64, 3 + 2 * t, :])[:, :, q:q + 64],
                    pend[q:q + 64, :, cc:cc + 1].to_broadcast([64, 4, 64]), ALU.mult)
            last.then_inc(r_dve, 1)

        def chunk_state(cc):
            s = state(part, i, cc)
            pe4 = pend[:, :, cc:cc + 1].to_broadcast([P, 4, 64])
            v4 = "p o (j v) -> p (o j) v"
            nc.vector.tensor_tensor(T1.rearrange("p (j v) -> p j v", v=64), s.rearrange(v4, v=64),
                                    pe4, ALU.mult)
            dve.drain()
            nc.vector.tensor_tensor(T1, T1, Cst[:, cc % 2, :], ALU.add)
            dve.wait_ge(r_pe, P_.at(f"y{cc}", i))
            nc.vector.tensor_tensor(T2.rearrange("p (j v) -> p j v", v=64),
                                    ps[:, 6, 0:256].rearrange("p (j v) -> p j v", v=64), pe4,
                                    ALU.mult)
            dve.drain()
            nc.vector.tensor_tensor(s, T1.unsqueeze(1), T2.unsqueeze(1), ALU.add
                                    ).then_inc(r_dve, 1)
            dve.drain()
        chunk_matrices(0)
        chunk_matrices(1)
        chunk_state(0)
        chunk_matrices(2)
        chunk_state(1)
        chunk_matrices(3)
        chunk_state(2)
        chunk_state(3)
        dve.wait_ge(r_act, A_.at("y0", i))
        nc.vector.tensor_tensor(col(yT), stg(ps[:, 7, :].rearrange("p (j t) -> p j t", t=P)),
                                stg(Y0), ALU.add).then_inc(r_dve, 1)

    def rtile_scalar(act, part, i):
        col, stg, comp, n = tile_views(part, i)
        D_, A_, P_ = rdve[part], ract[part], rpe[part]
        if part == 0:
            act.wait_ge(rp["prep"], 1)
        act.wait_ge(r_dve, D_.base + i * len(DVR))
        for dst, src, s in ((ex1, cum, -KAPPA), (ex2, cum, KAPPA), (ex3, cumprev, -KAPPA)):
            last = nc.scalar.activation(comp(dst), col(src), ACT.Exp, scale=s)
        last.then_inc(r_act, 1)
        act.wait_ge(r_pe, P_.at("turn", i))
        for dst, b in ((tokK, 1), (tokB, 2), (tokV, 3)):
            nc.scalar.activation(dst, ps[:, b, :], ACT.Copy)
        for h in range(2):
            last = nc.scalar.activation(
                heads4(mats[h]["X"])[:, :, 64:P],
                ps[:, 0, :].rearrange("p (k h v) -> p k h v", h=2, v=64)[:, :, h, :], ACT.Copy)
        last.then_inc(r_act, 1)
        for s, pairs in (("s2", (("A2", 0), ("A3", 1))), ("s3", (("A0", 0), ("A1", 1))),
                         ("s4", (("A2", 0),)), ("s6", (("A0", 2),)), ("s7", (("A1", 3),))):
            for h in range(2):
                act.wait_ge(r_pe, P_.at(f"{s}{h}", i))
                for dst, b in pairs:
                    last = nc.scalar.activation(mats[h][dst], ps[:, 4 * h + b, :], ACT.Copy)
                last.then_inc(r_act, 1)
        act.wait_ge(r_pe, P_.at("yr", i))
        nc.scalar.activation(Y0[:, :, :].rearrange("p j t -> p (j t)"), ps[:, 0, :], ACT.Copy
                             ).then_inc(r_act, 1)
        for cc in range(4):
            if cc:
                act.wait_ge(r_dve, D_.at(f"s{cc - 1}", i))
            if cc > 1:
                act.wait_ge(r_pe, P_.at(f"y{cc - 2}", i))
            s = state(part, i, cc)
            for q in (0, 64):
                last = nc.scalar.activation(
                    Sbd[q:q + 64, cc % 2, :].rearrange("p (o j v) -> p o j v", o=1, v=P)[:, :, :, q:q + 64],
                    s[q:q + 64, :, :].rearrange("p o (j v) -> p o j v", v=64), ACT.Copy)
            last.then_inc(r_act, 1)

    def rtile_tensor(pe, part, i):
        D_, A_, P_ = rdve[part], ract[part], rpe[part]
        mm_ = nc.tensor.matmul
        pe.wait_ge(r_dve, D_.at("prod", i))
        for b, src in ((0, stQ), (1, stK), (2, stB), (3, stV)):
            for j in range(4):
                last = nc.tensor.transpose(ps[:, b, j * P:j * P + P], src[:, j, :], ident)
        last.then_inc(r_pe, 1)

        def head(x, h, k):
            return x[64 * h:64 * h + 64, k, :]

        def four(b, f):
            for k in range(4):
                lhsT, rhs = f(k)
                n = rhs.free_size()
                last = mm_(ps[:, b, k * n:k * n + n], lhsT, rhs, start=True, stop=True)
            return last

        def mat(h, name):
            m = mats[h][name]
            return lambda k: m[:, k * P:k * P + P]
        for h in range(2):
            b = 4 * h
            if h == 0:
                pe.wait_ge(r_act, A_.at("tok", i))
            four(b, lambda k: (head(stQ, h, k), head(stB, h, k)))
            four(b + 1, lambda k: (head(stB, h, k), head(stQ, h, k)))
            four(b + 2, lambda k: (head(stK, h, k), head(stQ, h, k)))
            four(b + 3, lambda k: (head(stK, h, k), head(stR, h, k))).then_inc(r_pe, 1)
        for h in range(2):
            b = 4 * h
            pe.wait_ge(r_dve, D_.at(f"m1{h}", i))
            A0, A1, MT = mat(h, "A0"), mat(h, "A1"), mat(h, "MT")
            four(b, lambda k: (A1(k), A0(k)))
            four(b + 1, lambda k: (A0(k), A1(k)))
            four(b + 2, lambda k: (head(stB, h, k), head(stR, h, k)))
            four(b + 3, lambda k: (MT(k), tokV[:, (2 * k + h) * 64:(2 * k + h) * 64 + 64])
                 ).then_inc(r_pe, 1)
        for h in range(2):
            b = 4 * h
            A2, A3, G = mat(h, "A2"), mat(h, "A3"), mat(h, "G")
            pe.wait_ge(r_act, A_.at(f"sq2{h}", i))
            four(b, lambda k: (A3(k), A2(k)))
            four(b + 1, lambda k: (A2(k), A3(k)))
            pe.wait_ge(r_dve, D_.at(f"qx{h}", i))
            four(b + 2, lambda k: (A2(k), G(k))).then_inc(r_pe, 1)
        for h in range(2):
            b = 4 * h
            A0, A1, G = mat(h, "A0"), mat(h, "A1"), mat(h, "G")
            pe.wait_ge(r_act, A_.at(f"sq4{h}", i))
            four(b, lambda k: (A1(k), A0(k)))
            pe.wait_ge(r_dve, D_.at(f"g1{h}", i))
            four(b + 3, lambda k: (A0(k), G(k))).then_inc(r_pe, 1)
        for h in range(2):
            b = 4 * h
            A2, G = mat(h, "A2"), mat(h, "G")
            pe.wait_ge(r_act, A_.at(f"sq8{h}", i))
            pe.wait_ge(r_dve, D_.at(f"g2{h}", i))
            four(b + 1, lambda k: (A2(k), G(k))).then_inc(r_pe, 1)
        for h in range(2):
            b = 4 * h
            G = mat(h, "G")
            pe.wait_ge(r_dve, D_.at(f"g3{h}", i))
            X = mat(h, "X")
            four(b + 2, lambda k: (G(k), X(k))).then_inc(r_pe, 1)
        for h in range(2):
            b = 4 * h
            ET = mat(h, "ET")
            pe.wait_ge(r_act, A_.at(f"z{h}", i))
            A0 = mat(h, "A0")
            four(b + 3, lambda k: (ET(k), A0(k))).then_inc(r_pe, 1)
        for h in range(2):
            b = 4 * h
            G = mat(h, "G")
            pe.wait_ge(r_act, A_.at(f"ez{h}", i))
            A1 = mat(h, "A1")
            four(b, lambda k: (G(k), A1(k))).then_inc(r_pe, 1)
        pe.wait_ge(r_dve, D_.at("zf1", i))
        for q in range(8):
            h, k = q % 2, q // 2
            half, j = 64 * (q % 2), q // 2
            U0, W = UW[:, k, 0, h, :], UW[:, k, 1, h, :]
            QT, NT = mat(h, "QT")(k), mat(h, "NT")(k)
            y = ps[half:half + 64, 0, j * P:j * P + P]
            mm_(y, tokV[:, q * 64:q * 64 + 64], NT, start=True, stop=False)
            mm_(y, U0, QT, start=False, stop=True)
            last = mm_(ps[half:half + 64, 1, j * P:j * P + P], W, QT, start=True, stop=True)
        last.then_inc(r_pe, 1)

        def chunk_products(cc):
            t, r = cc % 2, slice(RC * cc, RC * cc + RC)
            for j in range(4):
                m = ZF[r, 2 * P * j:2 * P * j + 2 * P]
                B, K, V = (x[r, j * P:j * P + P] for x in (tokB, tokK, tokV))
                mm_(ps[:, 2 + 2 * t, j * P:j * P + P], m[:, P:2 * P], B, start=True, stop=True)
                c = ps[:, 3 + 2 * t, j * P:j * P + P]
                mm_(c, K, V, start=True, stop=False)
                last = mm_(c, B, m[:, 0:P], start=False, stop=True)
            last.then_inc(r_pe, 1)

        def chunk_step(cc):
            s = state(part, i, cc)
            pe.wait_ge(r_dve, D_.at(f"ac{cc}", i))
            if cc:
                pe.wait_ge(r_dve, D_.at(f"s{cc - 1}", i))
            for j in range(4):
                mm_(ps[:, 6, j * 64:j * 64 + 64], ATm[:, cc % 2, j * P:j * P + P],
                    s[:, :, j * 64:j * 64 + 64], start=True, stop=True)
            pe.wait_ge(r_act, A_.at(f"bd{cc}", i))
            for j in range(4):
                last = mm_(ps[:, 7, j * P + RC * cc:j * P + RC * cc + RC],
                           Sbd[:, cc % 2, j * P:j * P + P], RW[:, j, RC * cc:RC * cc + RC],
                           start=True, stop=True)
            last.then_inc(r_pe, 1)
        chunk_products(0)
        chunk_products(1)
        pe.wait_ge(r_dve, D_.at("rw", i))
        chunk_step(0)
        chunk_products(2)
        chunk_step(1)
        chunk_products(3)
        chunk_step(2)
        chunk_step(3)


    po = {n: sem("rwkv_post_" + n) for n in ("rk", "sums", "g", "mean", "cent", "sq", "var",
                                             "varr", "root", "over")}

    def rwkv_post_scalar(act):
        act.wait_ge(po["sums"], 1)
        nc.scalar.activation(gg[:, :, :], ps[:, 0:4, 0:T], ACT.Copy).then_inc(po["g"], 1)
        act.wait_ge(po["cent"], 1)
        nc.scalar.activation(post_sq[:, :, :], yT, ACT.Square).then_inc(po["sq"], 1)
        act.wait_ge(po["varr"], 1)
        nc.scalar.activation(post_sq[:, :, :], post_sq[:, :, :], ACT.Sqrt).then_inc(po["root"], 1)

    def rwkv_post_tensor(pe):
        pe.wait_ge(po["rk"], 1)
        for j in range(4):
            nc.tensor.matmul(ps[:, j, 0:T], gup[:, j * P:j * P + P], xb[:, 13, :], start=True,
                             stop=True)
        for j in range(4):
            mm = nc.tensor.matmul(ps[:, 4 + j, 0:T], block64, post_sq[:, j, :], start=True,
                                  stop=True)
        mm.then_inc(po["sums"], 1)
        pe.wait_ge(po["g"], 1)
        for j in range(4):
            mm = nc.tensor.matmul(ps[:, j, 0:T], block64, yT[:, j, :], start=True, stop=True)
        mm.then_inc(po["mean"], 1)
        pe.wait_ge(po["sq"], 1)
        for j in range(4):
            mm = nc.tensor.matmul(ps[:, 4 + j, 0:T], block64, post_sq[:, j, :], start=True,
                                  stop=True)
        mm.then_inc(po["var"], 1)

    def rwkv_post_vector(dve):
        dve.drain().then_inc(rw_over, 1)
        nc.vector.tensor_tensor(post_sq[:, :, :], xr, kmod[:, :, :], ALU.mult)
        dve.drain()
        for j in range(4):
            last = nc.vector.tensor_scalar(post_sq[:, j, :], post_sq[:, j, :], rkc[:, j:j + 1],
                                           None, ALU.mult)
        last.then_inc(po["rk"], 1)
        dve.wait_ge(po["sums"], 1)
        nc.vector.tensor_tensor(bonus[:, :, :], ps[:, 4:8, 0:T], xv, ALU.mult)
        dve.wait_ge(po["mean"], 1)
        nc.vector.scalar_tensor_tensor(yT, ps[:, 0:4, 0:T], -1.0 / 64, yT, ALU.mult, ALU.add
                                       ).then_inc(po["cent"], 1)
        dve.wait_ge(po["var"], 1)
        nc.vector.tensor_scalar(post_sq[:, :, :], ps[:, 4:8, 0:T], 1.0 / 64, LNX_EPS, ALU.mult,
                                ALU.add).then_inc(po["varr"], 1)
        dve.wait_ge(po["root"], 1)
        nc.vector.reciprocal(post_sq[:, :, :], post_sq[:, :, :])
        dve.drain()
        nc.vector.tensor_tensor(yT, yT, post_sq[:, :, :], ALU.mult)
        dve.drain()
        for j in range(4):
            nc.vector.tensor_scalar(yT[:, j, :], yT[:, j, :], lgc[:, j:j + 1], lbc[:, j:j + 1],
                                    ALU.mult, ALU.add)
        dve.drain()
        nc.vector.tensor_tensor(yT, yT, bonus[:, :, :], ALU.add)
        dve.drain()
        nc.vector.tensor_tensor(yT, yT, gg[:, :, :], ALU.mult).then_inc(mix_ready, 1)

    def rwkv_scalar(act):
        rwkv_prep_scalar(act)
        with act.Fori(0, 2) as i:
            rtile_scalar(act, 0, i)
            mod_scalar(act, 1, i + 4, G_MOD1)
        with act.Fori(0, 2) as i:
            rtile_scalar(act, 1, i)
        rwkv_post_scalar(act)

    def rwkv_vector(dve):
        rwkv_prep_vector(dve)
        dve.drain().then_inc(r_dve, RD0)
        with dve.Fori(0, 2) as i:
            rtile_vector(dve, 0, i)
            mod_vector(dve, 1, i + 4)
        nc.vector.memset(st[:, :, :], 0.0)
        dve.drain()
        with dve.Fori(0, 2) as i:
            rtile_vector(dve, 1, i)
        rwkv_post_vector(dve)

    def rwkv_tensor(pe):
        rwkv_prep_tensor(pe)
        with pe.Fori(0, 2) as i:
            rtile_tensor(pe, 0, i)
            pe.wait_ge(r_dve, rdve[0].at("yt", i))
            mod_tensor(pe, 1, i + 4, G_MOD1)
        with pe.Fori(0, 2) as i:
            rtile_tensor(pe, 1, i)
        rwkv_post_tensor(pe)

    aF = Area(0)
    hid = aF.take(FT, T)
    sgate = [aF.take(T) for _ in range(2)]
    hid_act, hid_ready = sem("gate_silu"), sem("hidden_ready")

    def gu_tensor(pe):
        pe.wait_ge(h_ready, 2)

        def body(c, k, i):
            wait_weights(pe, G_GU, k, i)
            wait_psum(pe, G_GU, c)
            w = slot_view(G_GU, k, 2 * KT, P)
            for t in range(2):
                for q in range(KT):
                    mm = nc.tensor.matmul(ps[:, pbank(G_GU, k) + t, 0:T], w[:, t * KT + q, :],
                                          hT[:, q, :], start=q == 0, stop=q == KT - 1)
            mm.then_inc(chunk_done, 1)
        by_four(pe, N_GU, body)

    def gu_scalar(act):
        def body(c, k, i):
            wait_done(act, G_GU, c)
            act.wait_ge(hid_ready, c + 1)
            nc.scalar.activation(sgate[k % 2], ps[:, pbank(G_GU, k), 0:T], ACT.Silu
                                 ).then_inc(hid_act, 1)
        by_four(act, N_GU, body)

    def gu_vector(dve):
        dve.drain().then_inc(hid_ready, 2)

        def body(c, k, i):
            dve.wait_ge(hid_act, c + 1)
            nc.vector.tensor_tensor(hid[:, ds(c, 1), :], sgate[k % 2].unsqueeze(1),
                                    ps[:, pbank(G_GU, k) + 1:pbank(G_GU, k) + 2, 0:T], ALU.mult
                                    ).then_inc(chunk_read, 1)
            dve.drain().then_inc(hid_ready, 1)
        by_four(dve, N_GU, body)

    aO = Area(0)
    uT = aO.take(EC // P, T)
    vtk = aO.take(3, EC)
    lnvg = aO.take(EC)
    lnvb = aO.take(EC)
    bsB = aO.take(GC, T)
    wsT = aO.take(GC, CHUNK)
    wsS = aO.take(GC, TS)
    stats = aO.take(3, 4, 6)
    aggr = aO.take(3, 2)
    odd_in, odd_masked = sem("gmlp_loads"), sem("spatial_masked")
    u_ready, v_part = sem("u_ready"), sem("v_part")
    lnv_var, lnv_root, v_ready = sem("lnv_var"), sem("lnv_root"), sem("v_ready")
    mixed_mm, mixed_rd = sem("mixed_product"), sem("mixed_read")

    def odd_loads(pool):
        pool.wait_ge(x_ready, 3)
        for dst, src in ((lnvg, a["lnv_g"].partition_broadcast(P)),
                         (lnvb, a["lnv_b"].partition_broadcast(P)),
                         (bsB[:, :, :].rearrange("p g t -> p (g t)"), a["b_s"].partition_broadcast(P)),
                         (wsT[:, :, :], a["w_s"]), (wsS[0:TS, :, :], a["w_s8"])):
            pool.dma_start(dst, src).then_inc(odd_in, 16)

    def in_o_tensor(pe):
        columns_tensor(pe, G_IN_O, 8, KT, 2, hT, lambda e: e.wait_ge(h_ready, 3))

        def body(c, k, i):
            g0 = G_IN_O + 8
            wait_weights(pe, g0, k, i)
            wait_psum(pe, g0, c)
            w = slot_view(g0, k, KT, 2 * P)
            for n in range(3):
                rows = P if n < 2 else TS
                for q in range(KT):
                    mm = nc.tensor.matmul(
                        ps[0:rows, pbank(g0, k) + n // 2, (n % 2) * 256:(n % 2) * 256 + 256],
                        hT[:, q, n * P:n * P + rows], w[:, q, :], start=q == 0, stop=q == KT - 1)
            mm.then_inc(chunk_done, 1)
        by_four(pe, 8, body)

    def in_o_scalar(act):
        def body_u(c, k, i):
            wait_done(act, G_IN_O, c)
            b = pbank(G_IN_O, k)
            nc.scalar.activation(uT[:, ds(2 * c, 2), :], ps[:, b:b + 2, 0:T], ACT.Gelu
                                 ).then_inc(chunk_read, 1)
        by_four(act, 8, body_u)
        act.drain().then_inc(u_ready, 1)

        def body_v(c, k, i):
            g0 = G_IN_O + 8
            wait_done(act, g0, c)
            b = pbank(g0, k)
            nc.scalar.activation(vtk[:, 0:2, ds(c * 256, 256)],
                                 ps[:, b, :].rearrange("p (n f) -> p n f", n=2), ACT.Gelu)
            nc.scalar.activation(vtk[0:TS, 2, ds(c * 256, 256)], ps[0:TS, b + 1, 0:256], ACT.Gelu
                                 ).then_inc(chunk_read, 1)
        by_four(act, 8, body_v)
        act.drain().then_inc(v_part, 1)
        act.wait_ge(lnv_var, 1)
        nc.scalar.activation(aggr[:, 0:2, 1:2], aggr[:, 0:2, 1:2], ACT.Sqrt)
        nc.scalar.activation(aggr[0:TS, 2, 1:2], aggr[0:TS, 2, 1:2], ACT.Sqrt
                             ).then_inc(lnv_root, 1)

    def v_norm_vector(dve):
        dve.wait_ge(odd_in, 16 * 5)
        nc.vector.tensor_tensor(wsT[:, :, :], wsT[:, :, :],
                                cst["upincl"].unsqueeze(1).to_broadcast([P, GC, CHUNK]), ALU.mult)
        nc.vector.tensor_tensor(wsS[0:TS, :, :], wsS[0:TS, :, :],
                                cst["upincl8"][0:TS, 0:TS].unsqueeze(1).to_broadcast([TS, GC, TS]),
                                ALU.mult).then_inc(odd_masked, 1)
        dve.wait_ge(v_part, 1)
        for n in range(3):
            rows = P if n < 2 else TS
            for q in range(4):
                nc.vector.bn_stats(stats[0:rows, n, q, :], vtk[0:rows, n, q * 512:q * 512 + 512])
        dve.drain()
        for n in range(3):
            rows = P if n < 2 else TS
            nc.vector.bn_aggr(aggr[0:rows, n, :], stats[0:rows, n, :, :])
        dve.drain()
        nc.vector.tensor_scalar(aggr[:, 0:2, 1:2], aggr[:, 0:2, 1:2], LN_EPS, None, ALU.add)
        nc.vector.tensor_scalar(aggr[0:TS, 2, 1:2], aggr[0:TS, 2, 1:2], LN_EPS, None, ALU.add
                                ).then_inc(lnv_var, 1)
        dve.wait_ge(lnv_root, 1)
        nc.vector.reciprocal(aggr[:, 0:2, 1:2], aggr[:, 0:2, 1:2])
        nc.vector.reciprocal(aggr[0:TS, 2, 1:2], aggr[0:TS, 2, 1:2])
        dve.drain()
        for n in range(3):
            rows = P if n < 2 else TS
            v = vtk[0:rows, n, :]
            nc.vector.tensor_scalar(v, v, aggr[0:rows, n, 0:1], aggr[0:rows, n, 1:2], ALU.subtract,
                                    ALU.mult)
            dve.drain()
            nc.vector.tensor_tensor(v, v, lnvg[0:rows, :], ALU.mult)
            dve.drain()
            last = nc.vector.tensor_tensor(v, v, lnvb[0:rows, :], ALU.add)
            last.then_inc(v_ready, 1)

    def mixed_tensor(pe):
        pe.wait_ge(odd_masked, 1)
        pe.wait_ge(v_ready, 3)
        for m in range(EC // P):
            g = m // 2
            if m >= 4:
                pe.wait_ge(mixed_rd, m - 3)
            for n in range(2):
                nc.tensor.matmul(ps[:, 4 + m % 4, n * P:n * P + P], vtk[:, n, m * P:m * P + P],
                                 wsT[:, g, :], start=True, stop=True)
            nc.tensor.matmul(ps[:, 4 + m % 4, TP:T], vtk[0:TS, 2, m * P:m * P + P],
                             wsS[0:TS, g, :], start=True, stop=True).then_inc(mixed_mm, 1)

    def mixed_vector(dve):
        dve.wait_ge(u_ready, 1)
        mtmp = lnvg[:, 0:2 * T].rearrange("p (a t) -> p a t", a=2)
        for m in range(EC // P):
            dve.wait_ge(mixed_mm, m + 1)
            nc.vector.tensor_tensor(mtmp[:, m % 2, :], ps[:, 4 + m % 4, 0:T], bsB[:, m // 2, :],
                                    ALU.add).then_inc(mixed_rd, 1)
            dve.drain()
            nc.vector.tensor_tensor(uT[:, m, :], uT[:, m, :], mtmp[:, m % 2, :], ALU.mult)
        dve.drain().then_inc(um_ready, 1)

    um_ready = sem("gated_ready")

    aE = Area(0)
    h2tok = aE.take(3, D)
    acc = aE.take(KT, T)
    xg = [aE.take(KT, CAP) for _ in range(2)]
    hidE = [aE.take(FE, CAP) for _ in range(2)]
    sgE = [aE.take(CAP) for _ in range(2)]
    ye = aE.take(D)
    PgT = aE.take(T)
    Psel = [aE.take(3, CAP) for _ in range(2)]
    Pgat = [aE.take(3, CAP) for _ in range(2)]
    rw = aE.take(KT, NE)
    rbB = aE.take(NE)
    lgT = aE.take(T)
    lg = aE.take(3, NE)
    ex = aE.take(3, NE)
    cmpA = aE.take(3, 64)
    cmpB = aE.take(3, 64)
    beaten = aE.take(3, NE)
    sel = aE.take(3, NE)
    gate = aE.take(3, NE)
    rank = aE.take(3, NE)
    tot = aE.take(NE)
    r1 = aE.take(3)
    r2 = aE.take(3)
    rounds_f = aE.take(2)
    router_in = sem("router_loads")
    rt_pe = Steps(sem("router_pe"), ["logits", "lgtok", "h2a", "h2b", "h2c", "rank"])
    rt_act = Steps(sem("router_act"), ["lgT", "h2a", "h2b", "h2c", "exp"])
    rt_dve = Steps(sem("router_dve"), ["max", "gate", "rounds"])
    EX0 = 1
    ex_pe = Steps(sem("expert_pe"), ["gather", "turned", "scatterA", "scatterB"], EX0)
    ex_dve = Steps(sem("expert_dve"), ["select", "accA", "accB"], EX0)
    ex_act = Steps(sem("expert_act"), ["xg", "PgT", "ye"], EX0)
    silu_e, hid_e = sem("expert_silu"), sem("expert_hidden")
    moe_over = sem("experts_over")

    def router_loads(pool):
        pool.wait_ge(x_ready, 4)
        pool.dma_start(rw[:, :, :], a["router_w"]).then_inc(router_in, 16)
        pool.dma_start(rbB, a["router_b"].partition_broadcast(P)).then_inc(router_in, 16)

    def router_tensor(pe):
        pe.wait_ge(router_in, 32)
        pe.wait_ge(h_ready, 4)
        for q in range(KT):
            mm = nc.tensor.matmul(ps[0:NE, 0, 0:T], rw[:, q, :], hT[:, q, :], start=q == 0,
                                  stop=q == KT - 1)
        mm.then_inc(rt_pe.sem, 1)
        pe.wait_ge(rt_act.sem, rt_act.at("lgT"))
        for n in range(3):
            rows = P if n < 2 else TS
            mm = nc.tensor.transpose(ps[0:rows, 1, n * NE:n * NE + NE], lgT[0:NE, n * P:n * P + rows],
                                     ident[0:NE, 0:NE])
        mm.then_inc(rt_pe.sem, 1)
        for n, name in enumerate("abc"):
            rows = P if n < 2 else TS
            for q in range(KT):
                mm = nc.tensor.transpose(ps[0:rows, 2 + 2 * n + q // 4, (q % 4) * P:(q % 4) * P + P],
                                         hT[:, q, n * P:n * P + rows], ident)
            mm.then_inc(rt_pe.sem, 1)
        pe.wait_ge(rt_dve.sem, rt_dve.at("gate"))
        up = cst["up"]
        for n in range(3):
            for m in range(n + 1):
                nc.tensor.matmul(ps[:, 0, n * NE:n * NE + NE], up if m == n else ones[:, :],
                                 sel[:, m, :], start=m == 0, stop=m == n)
        for m in range(3):
            mm = nc.tensor.matmul(ps[:, 0, 32:32 + NE], ones[:, :], sel[:, m, :], start=m == 0,
                                  stop=m == 2)
        mm.then_inc(rt_pe.sem, 1)

    def router_scalar(act):
        act.wait_ge(rt_pe.sem, rt_pe.at("logits"))
        nc.scalar.activation(lgT[0:NE, :], ps[0:NE, 0, 0:T], ACT.Copy).then_inc(rt_act.sem, 1)
        for n, name in enumerate("abc"):
            rows = P if n < 2 else TS
            act.wait_ge(rt_pe.sem, rt_pe.at("h2" + name))
            nc.scalar.activation(h2tok[0:rows, n, :].rearrange("p (a b) -> p a b", a=2),
                                 ps[0:rows, 2 + 2 * n:4 + 2 * n, :], ACT.Copy
                                 ).then_inc(rt_act.sem, 1)
        act.wait_ge(rt_dve.sem, rt_dve.at("max"))
        nc.scalar.activation(ex[:, :, :], ex[:, :, :], ACT.Exp).then_inc(rt_act.sem, 1)

    def router_vector(dve):
        dve.wait_ge(router_in, 32)
        nc.vector.memset(lg[:, :, :], 0.0)
        nc.vector.memset(acc[:, :, :], 0.0)
        dve.drain()
        dve.wait_ge(rt_pe.sem, rt_pe.at("lgtok"))
        b3 = rbB.unsqueeze(1)
        nc.vector.tensor_tensor(lg[:, 0:2, :], ps[:, 1, 0:2 * NE].rearrange("p (n e) -> p n e", e=NE),
                                b3.to_broadcast([P, 2, NE]), ALU.add)
        nc.vector.tensor_tensor(lg[0:TS, 2, :], ps[0:TS, 1, 2 * NE:3 * NE], rbB[0:TS, :], ALU.add)
        dve.drain()
        nc.vector.tensor_reduce(r1, lg[:, :, :], AX.X, ALU.max)
        dve.drain()
        nc.vector.tensor_tensor(ex[:, :, :], lg[:, :, :], r1.unsqueeze(2).to_broadcast([P, 3, NE]),
                                ALU.subtract).then_inc(rt_dve.sem, 1)
        full = [P, 3, NE, NE]
        mine = lg[:, :, :].unsqueeze(3).to_broadcast(full)
        other = lg[:, :, :].unsqueeze(2).to_broadcast(full)
        c4 = cmpA[:, :, :].rearrange("p n (e f) -> p n e f", f=NE)
        d4 = cmpB[:, :, :].rearrange("p n (e f) -> p n e f", f=NE)
        nc.vector.tensor_tensor(c4, other, mine, ALU.is_gt)
        nc.vector.tensor_tensor(d4, other, mine, ALU.is_equal)
        dve.drain()
        nc.vector.tensor_tensor(cmpB[:, :, :], cmpB[:, :, :],
                                cst["lower_e"].unsqueeze(1).to_broadcast([P, 3, 64]), ALU.mult)
        dve.drain()
        nc.vector.tensor_tensor(cmpA[:, :, :], cmpA[:, :, :], cmpB[:, :, :], ALU.add)
        dve.drain()
        nc.vector.tensor_reduce(beaten[:, :, :], c4, AX.X, ALU.add)
        dve.drain()
        nc.vector.tensor_scalar(sel[:, :, :], beaten[:, :, :], 1.5, None, ALU.is_lt)
        dve.drain()
        nc.vector.tensor_tensor(sel[:, :, :], sel[:, :, :],
                                cst["valid"].unsqueeze(2).to_broadcast([P, 3, NE]), ALU.mult)
        dve.wait_ge(rt_act.sem, rt_act.at("exp"))
        dve.drain()
        nc.vector.tensor_scalar(beaten[:, :, :], beaten[:, :, :], 1.5, None, ALU.is_lt)
        dve.drain()
        nc.vector.tensor_tensor(ex[:, :, :], ex[:, :, :], beaten[:, :, :], ALU.mult)
        dve.drain()
        nc.vector.tensor_reduce(r2, ex[:, :, :], AX.X, ALU.add)
        dve.drain()
        nc.vector.reciprocal(r2, r2)
        dve.drain()
        nc.vector.tensor_tensor(gate[:, :, :], ex[:, :, :], r2.unsqueeze(2).to_broadcast([P, 3, NE]),
                                ALU.mult).then_inc(rt_dve.sem, 1)
        dve.wait_ge(rt_pe.sem, rt_pe.at("rank"))
        nc.vector.tensor_copy(rank[:, :, :], ps[:, 0, 0:3 * NE].rearrange("p (n e) -> p n e", e=NE))
        nc.vector.tensor_reduce(tot[:, 0:1], ps[:, 0, 32:32 + NE], AX.X, ALU.max)
        dve.drain()
        nc.vector.tensor_scalar(rounds_f[:, 0:1], tot[:, 0:1], CAP + 0.5, 1.0, ALU.is_gt, ALU.add)
        nc.vector.tensor_scalar(rounds_f[:, 1:2], tot[:, 0:1], 2 * CAP + 0.5, None, ALU.is_gt)
        dve.drain()
        nc.vector.tensor_tensor(rounds_i[:, 0:1], rounds_f[:, 0:1], rounds_f[:, 1:2], ALU.add
                                ).then_inc(rt_dve.sem, 1)

    def rounds(eng):
        eng.wait_ge(rt_dve.sem, rt_dve.at("rounds"))
        return eng.value_load(rounds_i[0:1, 0:1], min_val=1, max_val=3)

    def each_expert(eng, body, after_round=None):
        n = rounds(eng)
        with eng.Fori(0, n) as r:
            with eng.Fori(0, NE) as e:
                body(e, r * NE + e)
            if after_round is not None:
                after_round()

    S_BASE = [len([g for g in range(G_EXP) if g % RING == s]) for s in range(RING)]

    def expert_slot(j):
        return (G_EXP + j) % RING

    def expert_use(j, turn):
        s = expert_slot(j)
        per = len([q for q in range(N_EXP) if expert_slot(q) == s])
        before = len([q for q in range(j) if expert_slot(q) == s])
        return turn * per + (S_BASE[s] + before + 1)

    def expert_tensor(pe):
        def body(e, t):
            pe.wait_ge(ex_dve.sem, ex_dve.at("select", t))
            pe.wait_ge(ex_act.sem, ex_act.at("ye", t) - 3)
            for q in range(KT):
                for n in range(3):
                    rows = P if n < 2 else TS
                    mm = nc.tensor.matmul(ps[:, 4 + q // 4, (q % 4) * CAP:(q % 4) * CAP + CAP],
                                          h2tok[0:rows, n, q * P:q * P + P], Psel[0][0:rows, n, :],
                                          start=n == 0, stop=n == 2)
            mm.then_inc(ex_pe.sem, 1)
            for n in range(3):
                rows = P if n < 2 else TS
                mm = nc.tensor.transpose(ps[:, 6, n * P:n * P + rows], Pgat[0][0:rows, n, :],
                                         ident[0:rows, 0:rows])
            mm.then_inc(ex_pe.sem, 1)
            pe.wait_ge(ex_act.sem, ex_act.at("xg", t))
            for j in range(FE):
                g = G_EXP + j
                pe.wait_ge(landed[expert_slot(j)], 16 * expert_use(j, t))
                pe.wait_ge(chunk_read, N_EXP * t + (g + 1))
                w = ring[:, expert_slot(j), 0:2 * KT * P].rearrange("p (k n) -> p k n", n=P)
                for gu in range(2):
                    for q in range(KT):
                        mm = nc.tensor.matmul(ps[:, j % 2, gu * CAP:gu * CAP + CAP],
                                              w[:, gu * KT + q, :], xg[0][:, q, :], start=q == 0,
                                              stop=q == KT - 1)
                mm.then_inc(chunk_done, 1)
            pe.wait_ge(hid_e, FE * t + (FE + 2))
            for j in range(4):
                g = G_EXP + FE + j
                pe.wait_ge(landed[expert_slot(FE + j)], 16 * expert_use(FE + j, t))
                pe.wait_ge(chunk_read, N_EXP * t + (g + 1))
                w = ring[:, expert_slot(FE + j), 0:FE * 256].rearrange("p (k n) -> p k n", n=256)
                for q in range(FE):
                    mm = nc.tensor.matmul(ps[:, 2 + j % 2, 0:256], hidE[0][:, q, :], w[:, q, :],
                                          start=q == 0, stop=q == FE - 1)
                mm.then_inc(chunk_done, 1)
            pe.wait_ge(ex_act.sem, ex_act.at("ye", t))
            for hf in range(2):
                if hf == 1:
                    pe.wait_ge(ex_dve.sem, ex_dve.at("accA", t))
                for q in range(4):
                    m = 4 * hf + q
                    mm = nc.tensor.matmul(ps[:, 4 + q, 0:T], ye[:, m * P:m * P + P], PgT,
                                          start=True, stop=True)
                mm.then_inc(ex_pe.sem, 1)
        each_expert(pe, body)

    def expert_scalar(act):
        act.drain().then_inc(ex_act.sem, EX0)

        def body(e, t):
            act.wait_ge(ex_pe.sem, ex_pe.at("gather", t))
            nc.scalar.activation(xg[0][:, :, :].rearrange("p (a k) c -> p a (k c)", a=2),
                                 ps[:, 4:6, :], ACT.Copy).then_inc(ex_act.sem, 1)
            act.wait_ge(ex_pe.sem, ex_pe.at("turned", t))
            nc.scalar.activation(PgT, ps[:, 6, 0:T], ACT.Copy).then_inc(ex_act.sem, 1)
            for j in range(FE):
                act.wait_ge(chunk_done, N_EXP * t + (G_EXP + j + 1 + DONE0))
                act.wait_ge(hid_e, FE * t + (j + 1))
                nc.scalar.activation(sgE[j % 2], ps[:, j % 2, 0:CAP], ACT.Silu
                                     ).then_inc(silu_e, 1)
            for j in range(4):
                act.wait_ge(chunk_done, N_EXP * t + (G_EXP + FE + j + 1 + DONE0))
                nc.scalar.activation(ye[:, j * 256:j * 256 + 256], ps[:, 2 + j % 2, 0:256],
                                     ACT.Copy).then_inc(chunk_read, 1)
            act.drain().then_inc(ex_act.sem, 1)
        each_expert(act, body)

    def expert_vector(dve):
        dve.drain().then_inc(ex_dve.sem, EX0)
        dve.drain().then_inc(hid_e, 2)

        def body(e, t):
            dve.wait_ge(ex_pe.sem, ex_pe.at("scatterB", t) - 4)
            for n in range(3):
                nc.vector.tensor_scalar(Psel[0][:, n, :], cst["iota"], rank[:, n, ds(e, 1)],
                                        sel[:, n, ds(e, 1)], ALU.is_equal, ALU.mult)
            dve.drain()
            for n in range(3):
                last = nc.vector.tensor_scalar(Pgat[0][:, n, :], Psel[0][:, n, :],
                                               gate[:, n, ds(e, 1)], None, ALU.mult)
            last.then_inc(ex_dve.sem, 1)
            for j in range(FE):
                dve.wait_ge(silu_e, FE * t + (j + 1))
                nc.vector.tensor_tensor(hidE[0][:, j, :], sgE[j % 2], ps[:, j % 2, CAP:2 * CAP],
                                        ALU.mult).then_inc(chunk_read, 1)
                dve.drain().then_inc(hid_e, 1)
            for hf, name in enumerate("AB"):
                dve.wait_ge(ex_pe.sem, ex_pe.at("scatter" + name, t))
                nc.vector.tensor_tensor(acc[:, 4 * hf:4 * hf + 4, :], acc[:, 4 * hf:4 * hf + 4, :],
                                        ps[:, 4:8, 0:T], ALU.add).then_inc(ex_dve.sem, 1)
            dve.drain()

        def after_round():
            dve.drain()
            nc.vector.tensor_scalar(rank[:, :, :], rank[:, :, :], -float(CAP), None, ALU.add)
            dve.drain()
        each_expert(dve, body, after_round)
        for m in range(KT):
            residual_tile(dve, acc[:, m:m + 1, :], 1, G2, m, None)
            dve.drain()
        dve.drain().then_inc(x_ready, 1)

    def load_weights(sp):
        def phase(g0, n, w, c0=0):
            size = w.shape[2]

            def body(c, k, i):
                sp.wait_ge(chunk_done, c + (g0 + 1))
                sp.dma_start(ring[:, slot(g0, k), 0:size],
                             w[ds(c + c0, 1)].rearrange("o p n -> p (o n)")
                             ).then_inc(landed[slot(g0, k)], 16)
            by_four(sp, n, body)
        phase(G_MOD0, N_MOD, a["w_mod"])
        phase(G_IN_E, N_IN_E, a["w_in_e"])
        phase(G_MOD1, N_MOD, a["w_mod"], N_MOD)
        phase(G_OUT_E, N_OUT_E, a["w_out_e"])
        phase(G_GU, N_GU, a["ffn_gu"])
        phase(G_DN, N_DN, a["ffn_down"])
        phase(G_IN_O, N_IN_O, a["w_in_o"])
        phase(G_OUT_O, N_OUT_O, a["w_out_o"])

        def body(e, t):
            for j in range(N_EXP):
                s = expert_slot(j)
                back = [q for q in range(j) if expert_slot(q) == s]
                if back:
                    need = back[-1] + 1
                else:
                    need = max([q for q in range(N_EXP) if expert_slot(q) == s][-1] + 1 - N_EXP,
                               j - RING + 1)
                sp.wait_ge(chunk_done, N_EXP * t + (G_EXP + DONE0 + need))
                if j < FE:
                    src, size = a["exp_gu"][ds(e * FE + j, 1)], 2 * KT * P
                else:
                    src, size = a["exp_down"][ds(e * 4 + (j - FE), 1)], FE * 256
                sp.dma_start(ring[:, s, 0:size], src.rearrange("o p n -> p (o n)")
                             ).then_inc(landed[s], 16)
        each_expert(sp, body)

    CONST_LOADS = [
        (gains[:, :, :], a["gains"]), (bmod[:, :, :], a["b_mod"]), (colsE[:, :], a["colsE"]),
        (attc, a["attc"]), (lamw[:, :, :].rearrange("p a k -> p (a k)"), a["lamv"].partition_broadcast(P)),
        (ptab[:, :], a["page_table"])]
    N_CONST_LOADS = len(CONST_LOADS) + 1

    block = ctx.enter_context(nc.Block())

    @block.sync
    def _(sp):
        sp.dma_start(cT[:, :, :], a["c_t"]).then_inc(inputs_in, 16)
        sp.dma_start(consts[:, :], a["consts"]).then_inc(inputs_in, 16)
        sp.dma_start(xT[:, :, :], a["x_t"]).then_inc(inputs_in, 16)
        load_weights(sp)
        sp.wait_ge(h_ready, 5)
        sp.dma_start(o["y"], hT[:, :, :]).then_inc(stores, 16)
        sp.wait_ge(stores, 16)

    @block.gpsimd
    def _(pool):
        for dst, src in CONST_LOADS:
            pool.dma_start(dst, src).then_inc(consts_in, 16)
        pool.dma_start(shift_in[:, :, :], a["shift"]).then_inc(consts_in, 16)
        pool.wait_ge(proj_ready, 1)
        pool.dma_start(o["k"], projT[:, 4:8, :]).then_inc(kv_stored, 16)
        pool.dma_start(o["v"], projT[:, 8:12, :]).then_inc(kv_stored, 16)
        pool.wait_ge(shift_saved, 1)
        sattn_load(pool)
        pool.dma_start(o["shift"], shift_out[:, :, :]).then_inc(kv_stored, 16)
        rwkv_loads(pool)
        pool.wait_ge(rw_over, 1)
        pool.dma_start(o["wkv"], S9[:, :, :]).then_inc(kv_stored, 16)
        odd_loads(pool)
        pool.wait_ge(v_ready, 3)
        pool.dma_start(o["cv"], vtk[0:TS, 2, :]).then_inc(kv_stored, 16)
        pool.wait_ge(kv_stored, 16 * 5)
        router_loads(pool)

    @block.scalar
    def _(act):
        act.wait_ge(inputs_in, 48)
        nc.scalar.activation(cT[:, :, :], cT[:, :, :], ACT.Silu).then_inc(silu_ready, 1)
        norm0 = norm_scalar
        with act.Fori(0, 6) as u:
            mod_scalar(act, 0, u, G_MOD0)
        norm0(act, 0)
        in_e_scalar(act)
        lambda_scalar(act)
        vtok_scalar(act)
        with act.Fori(0, 4) as j:
            pattn_scalar(act, j)
            mod_scalar(act, 1, j, G_MOD1)
        act.drain().then_inc(sa_act.sem, 1)
        with act.Fori(0, NB // 2) as i:
            sattn_scalar(act, i)
        subnorm_scalar(act)
        rwkv_scalar(act)
        norm_scalar(act, 1)
        gu_scalar(act)
        norm_scalar(act, 2)
        in_o_scalar(act)
        norm_scalar(act, 3)
        router_scalar(act)
        expert_scalar(act)
        norm_scalar(act, 4)

    @block.vector
    def _(dve):
        nc.vector.memset(ones[:, :], 1.0).then_inc(ones_ready, 1)
        dve.drain().then_inc(mod_ready, 1)
        dve.drain().then_inc(chunk_read, READ0)
        dve.wait_ge(inputs_in, 48)
        dve.drain().then_inc(x_ready, 1)
        dve.wait_ge(consts_in, 16 * N_CONST_LOADS)
        with dve.Fori(0, 6) as u:
            mod_vector(dve, 0, u)
        norm_vector(dve, 0, 0, SC1, SH1, 6)
        lambda_vector(dve)
        shift_vector(dve)
        dve.wait_ge(vtok_act, 1)
        with dve.Fori(0, 4) as j:
            pattn_vector(dve, j)
            mod_vector(dve, 1, j)
        with dve.Fori(0, NB // 2) as i:
            sattn_vector(dve, i)
        subnorm_vector(dve)
        rwkv_vector(dve)
        residual_vector(dve, G_OUT_E, N_OUT_E, 2, 0, G1)
        norm_vector(dve, 1, 0, SC2, SH2, 12)
        gu_vector(dve)
        residual_vector(dve, G_DN, N_DN, 1, 0, G2)
        norm_vector(dve, 2, 1, SC1, SH1, 12)
        v_norm_vector(dve)
        mixed_vector(dve)
        residual_vector(dve, G_OUT_O, N_OUT_O, 1, 1, G1)
        norm_vector(dve, 3, 1, SC2, SH2, 12)
        router_vector(dve)
        expert_vector(dve)
        norm_vector(dve, 4, None, 0, 0, 12)

    @block.tensor
    def _(pe):
        pe.drain().then_inc(chunk_done, DONE0)
        pe.drain().then_inc(pa_pe.sem, PA0)
        pe.drain().then_inc(sa_pe.sem, 1)
        pe.drain().then_inc(ex_pe.sem, EX0)
        pe.wait_ge(ones_ready, 1)
        pe.wait_ge(inputs_in, 48)
        with pe.Fori(0, 6) as u:
            mod_tensor(pe, 0, u, G_MOD0)
        norm_tensor(pe, 0)
        columns_tensor(pe, G_IN_E, N_IN_E, KT, 2, hT, lambda e: e.wait_ge(h_ready, 1))
        vtok_tensor(pe)
        with pe.Fori(0, 4) as j:
            pattn_tensor(pe, j)
            mod_tensor(pe, 1, j, G_MOD1)
        with pe.Fori(0, NB // 2) as i:
            sattn_tensor(pe, i)
        subnorm_tensor(pe)
        rwkv_tensor(pe)
        columns_tensor(pe, G_OUT_E, N_OUT_E, KT, 2, mixT, lambda e: (e.wait_ge(mix_ready, 1)))
        norm_tensor(pe, 1)
        gu_tensor(pe)
        columns_tensor(pe, G_DN, N_DN, FT, 1, hid, lambda e: e.wait_ge(hid_ready, N_GU + 2))
        norm_tensor(pe, 2)
        in_o_tensor(pe)
        mixed_tensor(pe)
        columns_tensor(pe, G_OUT_O, N_OUT_O, EC // P, 1, uT, lambda e: e.wait_ge(um_ready, 1))
        norm_tensor(pe, 3)
        router_tensor(pe)
        expert_tensor(pe)
        norm_tensor(pe, 4)


def kernel(**inputs):
    import concourse.bacc as _bacc
    from concourse.bass_utils import run_bass_kernel_spmd as _run

    n = {k: np.asarray(v) for k, v in inputs.items()}

    def tiles(w, cols):
        k, m = w.shape
        return w.reshape(k // P, P, m // cols, cols).transpose(2, 1, 0, 3).reshape(m // cols, P, -1)

    def columns(v):
        return v.reshape(-1, P).T

    x = np.concatenate([n["x_prompt"].reshape(TP, D), n["x_sample"].reshape(TS, D)])
    c = np.concatenate([n["c_prompt"], n["c_sample"], np.zeros((32 - NC_, D), np.float32)])
    k, v = n["cache_k"][0], n["cache_v"][0]
    wo = n["w_in_o"][0]
    ws = n["w_s"][0].transpose(2, 0, 1)
    gu = np.stack([tiles(n["ffn_gate"][0], P), tiles(n["ffn_up"][0], P)], 2)
    eg = np.stack([np.stack([tiles(n[w][0][e], P) for e in range(NE)]) for w in ("exp_gate", "exp_up")], 3)
    given = {
        "x_t": x.reshape(T, KT, P).transpose(2, 1, 0),
        "c_t": c.reshape(32, KT, P).transpose(2, 1, 0),
        "consts": np.concatenate(list(const_columns().values()), 1),
        "attc": attention_constants(),
        "scan_keep": scan_mask(),
        "gains": np.stack([columns(g) for g in (n["norm1_g"][0], n["norm2_g"][0], n["norm1_g"][1],
                                                n["norm2_g"][1], n["final_g"])], 1),
        "b_mod": n["b_mod"].reshape(2, 48, P).transpose(2, 0, 1),
        "colsE": np.concatenate(
            [columns(n["mu_b"][0])] + [columns(n[q].reshape(-1)) for q in
             ("w0", "a0", "k_k", "k_a", "r_k", "lnx_g", "lnx_b")]
            + [np.tile(n["subln_g"][0], 2)[:, None]] + [np.zeros((P, 31), np.float32)], 1),
        "lamv": np.stack([n[q][0] for q in ("lam_q1", "lam_k1", "lam_q2", "lam_k2")]).reshape(-1),
        "page_table": n["page_table"].reshape(1, -1),
        "shift": n["state_shift"][0].reshape(NB, 14, P).transpose(2, 1, 0),
        "s_init": n["state_wkv"][0].reshape(NB, 4, 2, 64, 64).transpose(2, 4, 0, 1, 3).reshape(P, NB, 256),
        "cache_k": k.reshape(N_POOL, PAGE, 4, P).transpose(0, 3, 2, 1).reshape(N_POOL, P, -1),
        "cache_v": v.reshape(N_POOL, PAGE, 512),
        "wa_up": np.concatenate([n["w_up"][0], n["a_up"][0]]),
        "g_up": n["g_up"][0],
        "w_mod": np.concatenate([tiles(n["w_mod"][q], 256) for q in range(2)]),
        "w_in_e": tiles(n["w_in_e"][0], 256),
        "w_out_e": tiles(n["w_out_e"][0], 256),
        "ffn_gu": gu.reshape(FT, P, -1),
        "ffn_down": tiles(n["ffn_down"][0], P),
        "w_in_o": tiles(wo, 256),
        "lnv_g": n["lnv_g"][0], "lnv_b": n["lnv_b"][0],
        "b_s": np.concatenate([n["b_s"][0], n["b_s"][0], np.tile(n["b_s"][0][:, :DS], (1, NB))], 1).reshape(-1),
        "w_s": ws,
        "w_s8": np.tile(ws[:DS, :, :DS], (NB, 1, NB)),
        "w_out_o": tiles(n["w_out_o"][0], P),
        "router_w": n["router_w"][0].reshape(KT, P, NE).transpose(1, 0, 2),
        "router_b": n["router_b"][0],
        "exp_gu": eg.reshape(NE * FE, P, -1),
        "exp_down": np.concatenate([tiles(n["exp_down"][0][e], 256) for e in range(NE)]),
    }
    returned = {"y": [P, KT, T], "k": [P, 4, T], "v": [P, 4, T], "shift": [P, 14, NC_],
                "wkv": [P, NC_, 256], "cv": [TS, EC]}
    nc = _bacc.Bacc("TRN2", target_bir_lowering=False, num_devices=1)
    arrays, a, o = {}, {}, {}
    for name, array in given.items():
        array = np.ascontiguousarray(array)
        arrays["in_" + name] = array
        a[name] = nc.dram_tensor("in_" + name, array.shape, mybir.dt.from_np(array.dtype),
                                 kind="ExternalInput").ap()
    for name, shape in returned.items():
        o[name] = nc.dram_tensor("out_" + name, shape, F32, kind="ExternalOutput").ap()
    build(nc, a, o)
    r = _run(nc, [arrays], core_ids=[0]).results[0]
    r = {name: np.asarray(r["out_" + name]) for name in returned}

    def rows(v):
        return v.transpose(2, 1, 0).reshape(v.shape[2], -1)
    y, kn, vn, sh = rows(r["y"]), rows(r["k"]), rows(r["v"]), rows(r["shift"])
    s = r["wkv"].reshape(2, 64, NC_, 4, 64).transpose(2, 3, 0, 4, 1).reshape(NC_, H, 64, 64)
    return (y[:TP].reshape(1, TP, D), y[TP:].reshape(NB, DS, D),
            kn[:TP].reshape(1, 1, TP, H, 2 * DK), vn[:TP].reshape(1, 1, TP, H, DV),
            s[:1][None], sh[:1][None],
            kn[TP:].reshape(1, NB, DS, H, 2 * DK), vn[TP:].reshape(1, NB, DS, H, DV),
            s[1:][None], sh[1:][None], r["cv"].reshape(1, NB, DS, EC))
```

```python
import math
from contextlib import ExitStack

import concourse.bass as bass
import numpy as np
from concourse import mybir

F32 = mybir.dt.float32
F32R = mybir.dt.float32r
I32 = mybir.dt.int32
ALU = mybir.AluOpType
ACT = mybir.ActivationFunctionType
AX = mybir.AxisListType
ds = bass.ds

P = 128
D = 1024
KT = D // P
TP, NB, DS = 256, 8, 8
TS = NB * DS
T = TP + TS
NC_ = 1 + NB
PAST, PAGE = 1024, 128
NPG = PAST // PAGE
N_POOL = 80
H = 8
DK, DV = 32, 64
EC, GC, CHUNK = 2048, 8, 128
DFF, DFE, NE = 2816, 1408, 8
FT, FE = DFF // P, DFE // P
RING = 4
SLOT = 22 * P
CAP = 128
LAM_INIT = 0.8 - 0.6 * math.exp(0.0)
KAPPA = math.exp(-0.5)
SCALE = DK ** -0.5
RMS_EPS, LN_EPS, LNX_EPS = 1e-6, 1e-5, 64e-5
RC = 32
SH1, SC1, G1, SH2, SC2, G2 = (KT * i for i in range(6))

N_MOD_A, N_MOD_B = 2 * 4, 10 * 4
N_IN_E, N_OUT_E, N_GU, N_DN = 13, 4, FT, 8
N_IN_O, N_OUT_O, N_EXP = 16, 8, FE + 4
G_MOD0 = 0
G_IN_E = G_MOD0 + N_MOD_A
G_MOD1 = G_IN_E + N_IN_E
G_OUT_E = G_MOD1 + N_MOD_B
G_GU = G_OUT_E + N_OUT_E
G_DN = G_GU + N_GU
G_IN_O = G_DN + N_DN
G_OUT_O = G_IN_O + N_IN_O
G_EXP = G_OUT_O + N_OUT_O
DONE0 = RING
READ0 = 2
S_IN_E = 0
S_GU = S_IN_E + N_IN_E
S_DN = S_GU + N_GU
S_IN_O = S_DN + N_DN
S_OUT_O = S_IN_O + N_IN_O


class Steps:

    def __init__(self, sem, names, base=0):
        self.sem, self.names, self.base = sem, names, base

    def at(self, name, turn=0):
        return turn * len(self.names) + (self.base + self.names.index(name) + 1)


def by_four(eng, n, body):
    full = n // RING
    if full > 1:
        with eng.Fori(0, full) as i:
            for k in range(RING):
                body(i * RING + k, k, i)
    elif full:
        for k in range(RING):
            body(k, k, 0)
    for k in range(n % RING):
        body(full * RING + k, k, full)


def const_columns():
    p = np.arange(P)[:, None]
    f = np.arange(P)[None, :]
    c = {}
    c["ident"] = (p == f)
    c["block64"] = (p // 64 == f // 64)
    c["low16"] = (f < p) & (f // 16 == p // 16)
    c["up16"] = (p < f) & (f // 16 == p // 16)
    c["up32off"] = (p < f) & (f // 32 == p // 32) & (f // 16 != p // 16)
    c["up32"] = (p < f) & (f // 32 == p // 32)
    c["up32incl"] = (p <= f) & (f // 32 == p // 32)
    c["up"] = (p < f)
    c["upincl"] = (p <= f)
    c["upincl8"] = (p <= f) & (p // DS == f // DS)
    c["iota"] = f + 0 * p
    e = np.arange(64)[None, :]
    c["lower_e"] = (e % 8 < e // 8) & (p >= 0)
    c["slope"] = np.exp2(-8.0 * np.arange(1, H + 1) / H)[None, :] + 0 * p
    c["rowmask"] = (p // 32 == np.arange(4)[None, :])
    c["map0"] = ((p // DS) % 2 == 0)
    c["map1"] = ((p // DS) % 2 == 1)
    c["valid"] = np.stack([np.ones(P), np.ones(P), np.arange(P) < TS], 1)
    hq = (p // 16) * DS + p % DS
    c["pairsum"] = (hq == np.arange(64)[None, :])
    c["sumheads"] = (p % DS == np.arange(DS)[None, :])
    return {k: np.ascontiguousarray(v.astype(np.float32)) for k, v in c.items()}


def attention_constants():
    q = np.arange(P)[:, None]
    k = np.arange(TP)[None, :]
    dist = np.stack([np.where(k <= q + P * b, k - (q + P * b), -1e30) for b in range(2)], 1)
    r = np.arange(P)
    head, qs = r // 16, r % DS
    slope = np.exp2(-8.0 * (head + 1) / H)[:, None]
    pos = np.arange(PAST + DS)[None, :]
    qp = (PAST + qs)[:, None]
    bias = np.where(pos <= qp, -slope * np.abs(qp - pos), -1e30)
    rows = np.arange(P) % 64
    own = (rows[:, None] // DS == np.arange(512)[None, :] // DV)
    return np.concatenate([dist.reshape(P, -1), bias, own], 1).astype(np.float32)


def scan_mask():
    t = np.arange(T)
    keep = np.where(t < TP, t % RC != 0, (t - TP) % DS != 0)
    return np.ascontiguousarray(np.broadcast_to(np.tile(keep, 4), (P, 4 * T)).astype(np.float32))


def build(nc, a, o):
    ctx = ExitStack()
    with ctx:
        program(nc, ctx, a, o)


def program(nc, ctx, a, o):
    def sb(name, shape, dt=F32):
        return ctx.enter_context(nc.sbuf_tensor(name, shape, dt))

    def sem(name):
        return ctx.enter_context(nc.semaphore(name))

    ring = sb("ring", [P, RING, SLOT])
    xT = sb("xT", [P, KT, T])
    hT = sb("hT", [P, KT, T])
    modT = sb("modT", [P, 2, 48, NC_])
    bmod = sb("bmod", [P, 2, 48])
    gains = sb("gains", [P, 5, KT])
    sqbuf_cols = const_columns()
    n_const = sum(v.shape[1] for v in sqbuf_cols.values())
    consts = sb("consts", [P, n_const])
    cst, at = {}, 0
    for name, v in sqbuf_cols.items():
        cst[name] = consts[:, at:at + v.shape[1]]
        at += v.shape[1]
    ones = sb("ones", [P, P])
    cT = sb("cT", [P, KT, 32])
    gsc = sb("gsc", [P, KT, NC_])
    rstd = sb("rstd", [P, T])
    ptab = sb("ptab", [1, NB * NPG], I32)
    small = sb("small", [P, 64])
    colsE = sb("colsE", [P, 74])
    modrow = sb("modrow", [P, 2 * P])
    gtmp = sb("gtmp", [P, TS])
    lamw = sb("lamw", [P, 4, DK])
    shift_in = sb("shift_in", [P, 14, NB])
    shift_out = sb("shift_out", [P, 14, NC_])
    rounds_i = sb("rounds_i", [P, 2], I32)
    n_arena = nc.sbuf_bytes_remaining // 4 - 8
    with nc.sbuf_tensor("arena", [P, n_arena], F32) as arena:
        pass

    def split_tensor(name, at, *shape):
        assert at + int(np.prod(shape)) <= n_arena
        with ExitStack() as place:
            if at:
                place.enter_context(nc.sbuf_tensor(f"below_{name}", [P, at], F32))
            return place.enter_context(nc.sbuf_tensor(name, [P, *shape], F32R))

    hid_hi, hid_lo = (split_tensor(n, x * FT * T, FT, T) for x, n in enumerate(("hid_hi", "hid_lo")))
    at_split = 2 * FT * T
    wsplit = split_tensor("wsplit", at_split, 4 * SLOT)
    at_um = at_split + 4 * KT * 256
    at_sgate = at_split + 4 * SLOT
    at_hx = at_um + 2 * EC
    assert at_hx >= at_sgate + 2 * T
    hx_hi, hx_lo = (split_tensor(n, at_hx + x * KT * T, KT, T) for x, n in enumerate(("hx_hi", "hx_lo")))
    at_htmp = at_hx + 2 * KT * T
    um_hi, um_lo = (split_tensor(n, at_um + x * (EC // P) * T, EC // P, T)
                    for x, n in enumerate(("um_hi", "um_lo")))
    ps = ctx.enter_context(nc.psum_tensor("ps", [P, 8, 512], F32))

    class Area:

        def __init__(self, at=0):
            self.at = at

        def take(self, *shape):
            n = int(np.prod(shape))
            v = arena[:, self.at:self.at + n]
            self.at += n
            assert self.at <= n_arena, (self.at, n_arena)
            if len(shape) == 2:
                v = v.rearrange("p (a b) -> p a b", b=shape[1])
            elif len(shape) == 3:
                v = v.rearrange("p (a b c) -> p a b c", b=shape[1], c=shape[2])
            return v

    ident, block64 = cst["ident"], cst["block64"]
    mu, w0c, a0c, kkc, kac, rkc, lgc, lbc, sgc, lamv = (
        colsE[:, 0:14], colsE[:, 14:18], colsE[:, 18:22], colsE[:, 22:26], colsE[:, 26:30],
        colsE[:, 30:34], colsE[:, 34:38], colsE[:, 38:42], colsE[:, 42:43], colsE[:, 43:44])

    landed = [sem(f"weights_landed{s}") for s in range(RING)]
    chunk_done, chunk_read = sem("chunk_done"), sem("chunk_read")
    inputs_in, consts_in = sem("inputs_in"), sem("consts_in")
    stores = sem("stores")

    def slot(g0, k):
        return (g0 + k) % RING

    def use(g0, k, i):
        return i + (g0 + k) // RING

    def wait_weights(eng, g0, k, i):
        eng.wait_ge(landed[slot(g0, k)], 16 * (use(g0, k, i) + 1))

    def wait_psum(eng, g0, c):
        eng.wait_ge(chunk_read, c + (g0 + 1))

    def wait_done(eng, g0, c):
        eng.wait_ge(chunk_done, c + (g0 + 1 + DONE0))

    def pbank(g0, k):
        return 2 * ((g0 + k) % 2)

    def slot_view(g0, k, kt, n):
        return ring[:, slot(g0, k), 0:kt * n].rearrange("p (k n) -> p k n", n=n)

    hi_ready, lo_ready = sem("weights_hi"), sem("weights_lo")

    def parts(s0, k, kt, n, stride=SLOT):
        at = ((s0 + k) % 2) * stride
        return [wsplit[:, x + at:x + at + kt * n].rearrange("p (k n) -> p k n", n=n)
                for x in (0, 2 * stride)]

    def split_hi(eng, copy, g0, s0, c, k, i, kt, n, stride=SLOT):
        wait_weights(eng, g0, k, i)
        eng.wait_ge(chunk_done, c + (g0 - 1 + DONE0))
        copy(parts(s0, k, kt, n, stride)[0], slot_view(g0, k, kt, n)).then_inc(hi_ready, 1)

    def split_lo(eng, g0, s0, c, k, i, kt, n, stride=SLOT):
        eng.wait_ge(hi_ready, c + (s0 + 1))
        hi, lo = parts(s0, k, kt, n, stride)
        eng.tensor_tensor(lo, slot_view(g0, k, kt, n), hi.bitcast(F32), ALU.subtract
                          ).then_inc(lo_ready, 1)

    def split_both(dve, g0, s0, n_chunks, kt, n, stride=SLOT):
        def body(c, k, i):
            split_hi(dve, nc.vector.tensor_copy, g0, s0, c, k, i, kt, n, stride)
            split_lo(dve, g0, s0, c, k, i, kt, n, stride)
        by_four(dve, n_chunks, body)

    def act_copy(out, in_):
        return nc.scalar.activation(out, in_, ACT.Copy)

    def split_hi_all(act, g0, s0, n_chunks, kt, n, stride=SLOT):
        by_four(act, n_chunks, lambda c, k, i: split_hi(act, act_copy, g0, s0, c, k, i, kt, n, stride))

    def split_lo_all(pool, g0, s0, n_chunks, kt, n, stride=SLOT):
        by_four(pool, n_chunks, lambda c, k, i: split_lo(pool, g0, s0, c, k, i, kt, n, stride))

    def three_passes(out, w, x, first, last):
        for p, (u, v) in enumerate(((w[0], x[0]), (w[0], x[1]), (w[1], x[0]))):
            mm = nc.tensor.matmul(out, u, v, start=first and p == 0, stop=last and p == 2)
        return mm

    silu_ready, modrow_ready, mod_turned, mod_ready = (
        sem("silu_ready"), sem("modrow_ready"), sem("mod_turned"), sem("mod_ready"))

    def mod_tensor(pe, g0, u, unit):
        pe.wait_ge(silu_ready, 1)
        pe.wait_ge(mod_ready, unit + 1)
        for k in range(4):
            wait_weights(pe, g0, k, u)
            if k == 0:
                pe.wait_ge(chunk_read, RING * u + (g0 + READ0))
            w = slot_view(g0, k, 2, D)
            for q in range(2):
                for c in range(4):
                    mm = nc.tensor.matmul(ps[32 * c:32 * c + 32, 5, 0:2 * P], cT[:, 2 * k + q, :],
                                          w[:, q, 256 * c:256 * c + 256],
                                          start=k + q == 0, stop=k + q == 4)
            mm.then_inc(chunk_done, 1)
        pe.wait_ge(modrow_ready, unit + 1)
        for hh in range(2):
            mm = nc.tensor.transpose(ps[:, 5, (2 + hh) * P:(3 + hh) * P], modrow[:, hh * P:hh * P + P], ident)
        mm.then_inc(mod_turned, 1)

    def mod_scalar(act, g0, u, unit):
        act.wait_ge(chunk_done, RING * u + (g0 + RING + DONE0))
        act.wait_ge(mod_ready, unit + 1)
        nc.scalar.activation(modrow[:, :], ps[:, 5, 0:2 * P], ACT.Copy).then_inc(chunk_read, 4)
        act.drain().then_inc(modrow_ready, 1)

    def mod_vector(dve, unit):
        dve.wait_ge(mod_turned, unit + 1)
        flat = modT[:, :, :, :].rearrange("p l m c -> p (l m) c")
        fb = bmod[:, :, :].rearrange("p l m -> p (l m)")
        for hh in range(2):
            for c in range(4):
                m = 8 * unit + (hh + 2 * c)
                last = nc.vector.tensor_scalar(
                    flat[:, ds(m, 1), :], ps[:, 5:6, (2 + hh) * P + 32 * c:(2 + hh) * P + 32 * c + NC_],
                    fb[:, ds(m, 1)], None, ALU.add)
        last.then_inc(mod_ready, 1)

    area0 = Area(n_arena - KT * T)
    sq = area0.take(KT, T)
    sq_ready, ssum_ready, var_ready, root_ready, h_ready, x_ready = (
        sem("sq_ready"), sem("ssum_ready"), sem("var_ready"), sem("root_ready"), sem("h_ready"),
        sem("x_ready"))

    def norm_scalar(act, n):
        act.wait_ge(x_ready, n + 1)
        if n:
            act.wait_ge(ssum_ready, n)
        nc.scalar.activation(sq[:, :, :], xT[:, :, :], ACT.Square).then_inc(sq_ready, 1)
        act.wait_ge(var_ready, n + 1)
        nc.scalar.activation(rstd[:, :], rstd[:, :], ACT.Sqrt).then_inc(root_ready, 1)

    def norm_tensor(pe, n):
        pe.wait_ge(sq_ready, n + 1)
        for kt in range(KT):
            mm = nc.tensor.matmul(ps[:, 7, 0:T], ones[:, :], sq[:, kt, :], start=kt == 0,
                                  stop=kt == KT - 1)
        mm.then_inc(ssum_ready, 1)

    def norm_vector(dve, n, layer, sc, sh, mod_count):
        dve.wait_ge(ssum_ready, n + 1)
        nc.vector.tensor_scalar(rstd[:, :], ps[:, 7, 0:T], 1.0 / D, RMS_EPS, ALU.mult,
                                ALU.add).then_inc(var_ready, 1)
        if layer is not None:
            dve.wait_ge(mod_ready, mod_count + 1)
            dve.drain()
            nc.vector.scalar_tensor_tensor(
                gsc[:, :, :], modT[:, layer, sc:sc + KT, :], 1.0,
                gains[:, n, :].unsqueeze(2).to_broadcast([P, KT, NC_]), ALU.add, ALU.mult)
        dve.wait_ge(root_ready, n + 1)
        nc.vector.reciprocal(rstd[:, :], rstd[:, :])
        dve.drain()
        nc.vector.tensor_tensor(hT[:, :, :], xT[:, :, :],
                                rstd[:, :].unsqueeze(1).to_broadcast([P, KT, T]), ALU.mult)
        dve.drain()
        if layer is None:
            for kt in range(KT):
                last = nc.vector.tensor_scalar(hT[:, kt, :], hT[:, kt, :], gains[:, n, kt:kt + 1],
                                               None, ALU.mult)
        else:
            for kt in range(KT):
                nc.vector.tensor_scalar(hT[:, kt, 0:TP], hT[:, kt, 0:TP], gsc[:, kt, 0:1],
                                        modT[:, layer, sh + kt, 0:1], ALU.mult, ALU.add)
            hs = hT[:, :, TP:T].rearrange("p k (b s) -> p k b s", s=DS)
            full = [P, KT, NB, DS]
            nc.vector.tensor_tensor(hs, hs, gsc[:, :, 1:NC_].unsqueeze(3).to_broadcast(full),
                                    ALU.mult)
            dve.drain()
            last = nc.vector.tensor_tensor(
                hs, hs, modT[:, layer, sh:sh + KT, 1:NC_].unsqueeze(3).to_broadcast(full), ALU.add)
        if n < 3:
            dve.drain()
            nc.vector.tensor_copy(hx_hi[:, :, :], hT[:, :, :])
            dve.drain()
            last = nc.vector.tensor_tensor(hx_lo[:, :, :], hT[:, :, :], hx_hi[:, :, :].bitcast(F32),
                                           ALU.subtract)
        last.then_inc(h_ready, 1)


    def residual_tile(dve, src, layer, gate, m, inc):
        flat = modT[:, :, :, :].rearrange("p l m c -> p (l m) c")
        row = flat[:, ds(m + (layer * 48 + gate), 1), :]
        x = xT[:, ds(m, 1), :]
        nc.vector.scalar_tensor_tensor(x[:, :, 0:TP], src[:, :, 0:TP], row[:, 0, 0:1],
                                       x[:, :, 0:TP], ALU.mult, ALU.add)
        g = row[:, 0, 1:NC_].unsqueeze(2).to_broadcast([P, NB, DS])
        t3 = gtmp[:, :].rearrange("p (b s) -> p b s", s=DS)
        dve.drain()
        nc.vector.tensor_tensor(t3, src[:, 0, TP:T].rearrange("p (b s) -> p b s", s=DS), g,
                                ALU.mult)
        dve.drain()
        ins = nc.vector.tensor_tensor(x[:, 0, TP:T], x[:, 0, TP:T], gtmp[:, :], ALU.add)
        if inc is not None:
            ins.then_inc(inc, 1)

    def columns_tensor(pe, g0, n, kt, tiles, rhs, first_wait):
        first_wait(pe)

        def body(c, k, i):
            wait_weights(pe, g0, k, i)
            wait_psum(pe, g0, c)
            w = slot_view(g0, k, kt, tiles * P)
            for t in range(tiles):
                for q in range(kt):
                    mm = nc.tensor.matmul(ps[:, pbank(g0, k) + t, 0:T], w[:, q, t * P:t * P + P],
                                          rhs[:, q, :], start=q == 0, stop=q == kt - 1)
            mm.then_inc(chunk_done, 1)
        by_four(pe, n, body)

    def columns_split(pe, g0, s0, n, kt, tiles, x, first_wait, stride=SLOT):
        first_wait(pe)

        def body(c, k, i):
            pe.wait_ge(lo_ready, c + (s0 + 1))
            wait_psum(pe, g0, c)
            w = parts(s0, k, kt, tiles * P, stride)
            for t in range(tiles):
                for q in range(kt):
                    mm = three_passes(ps[:, pbank(g0, k) + t, 0:T],
                                      [v[:, q, t * P:t * P + P] for v in w],
                                      [v[:, q, :] for v in x], q == 0, q == kt - 1)
            mm.then_inc(chunk_done, 1)
        by_four(pe, n, body)

    def residual_vector(dve, g0, n, tiles, layer, gate):
        def body(c, k, i):
            dve.drain()
            wait_done(dve, g0, c)
            for t in range(tiles):
                if t:
                    dve.drain()
                residual_tile(dve, ps[:, pbank(g0, k) + t:pbank(g0, k) + t + 1, :], layer, gate,
                              c * tiles + t, chunk_read if t == tiles - 1 else None)
        by_four(dve, n, body)
        dve.drain().then_inc(x_ready, 1)

    aA = Area(0)
    projT = aA.take(26, T)
    xb = projT[:, 12:26, :]
    base_b = aA.at
    proj_ready = sem("proj_ready")
    mixT = hT

    def in_e_scalar(act):
        def body(c, k, i):
            wait_done(act, G_IN_E, c)
            nc.scalar.activation(projT[:, ds(2 * c, 2), :],
                                 ps[:, pbank(G_IN_E, k):pbank(G_IN_E, k) + 2, 0:T],
                                 ACT.Copy).then_inc(chunk_read, 1)
        by_four(act, N_IN_E, body)
        act.drain().then_inc(proj_ready, 1)

    aB = Area(base_b)
    attc = aB.take(2 * TP + PAST + DS + 512)
    dist = attc[:, 0:2 * TP].rearrange("p (b k) -> p b k", b=2)
    biasS = attc[:, 2 * TP:2 * TP + PAST + DS]
    ownhead = attc[:, 2 * TP + PAST + DS:]
    Kp, Vp = [], []
    for _ in range(2):
        kv_at = aB.at
        Kp.append(aB.take(NPG, 4, P))
        Vp.append(aB.take(NPG, 512))
    sS = [aB.take(PAST + DS) for _ in range(2)]
    Qs = [aB.take(4, 32) for _ in range(2)]
    kvn = [aB.take(8, DS) for _ in range(2)]
    vn = [aB.take(512) for _ in range(2)]
    Cm = [aB.take(64) for _ in range(2)]
    prTs = [aB.take(NPG, 64) for _ in range(2)]
    prn = [aB.take(64) for _ in range(2)]
    om = [sS[par][:, 0:512] for par in range(2)]
    aP = Area(kv_at)
    Vtok = aP.take(2, 512)
    Qm = aP.take(4, TP)
    Vst = aP.take(2, P)
    sP = [aP.take(4, TP) for _ in range(2)]
    prP = [aP.take(2, TP) for _ in range(2)]
    prPT = [aP.take(4, P) for _ in range(2)]
    lam = small[:, 0:1]
    nmaxP, lP = small[:, 2:10], small[:, 10:18]
    nmaxS, lS = small[:, 18:20], small[:, 20:22]
    coef = small[:, 22:23]
    lamt = small[:, 24:28]

    vtok_pe, vtok_act = sem("vtok_turned"), sem("vtok_ready")
    lam_d, lam_a, lam_ready = sem("lam_dots"), sem("lam_exps"), sem("lam_ready")
    pa_scored = sem("pattn_scored")
    pa_queries = sem("pattn_queries")
    pa_pe = Steps(sem("pattn_pe"), ["prT0", "prT1", "o0", "o1"], 4)
    pa_dve = Steps(sem("pattn_dve"), ["pr0", "pr1", "values"])
    pa_max, pa_exp = sem("pattn_max"), sem("pattn_exp")
    pa_act = Steps(sem("pattn_act"), ["prTs0", "prTs1", "os0", "os1"], 4)

    def lambda_vector(dve):
        dve.wait_ge(consts_in, 16 * N_CONST_LOADS)
        nc.vector.tensor_tensor(lamw[:, 0:4:2, :], lamw[:, 0:4:2, :], lamw[:, 1:4:2, :], ALU.mult)
        dve.drain()
        nc.vector.tensor_reduce(lamt[:, 0:2], lamw[:, 0:4:2, :], AX.X, ALU.add).then_inc(lam_d, 1)
        dve.wait_ge(lam_a, 1)
        nc.vector.tensor_tensor(lam, lamt[:, 2:3], lamt[:, 3:4], ALU.subtract)
        dve.drain()
        nc.vector.tensor_scalar(lam, lam, LAM_INIT, None, ALU.add)
        dve.drain()
        nc.vector.tensor_scalar(coef, cst["map1"], lam, -1.0, ALU.mult, ALU.mult)
        dve.drain()
        nc.vector.tensor_tensor(coef, coef, cst["map0"], ALU.add).then_inc(lam_ready, 1)

    def lambda_scalar(act):
        act.wait_ge(lam_d, 1)
        nc.scalar.activation(lamt[:, 2:4], lamt[:, 0:2], ACT.Exp).then_inc(lam_a, 1)

    def vtok_tensor(pe):
        pe.wait_ge(proj_ready, 1)
        for n in range(2):
            for j in range(4):
                mm = nc.tensor.transpose(ps[:, n, j * P:j * P + P], projT[:, 8 + j, n * P:n * P + P],
                                         ident)
        mm.then_inc(vtok_pe, 1)

    def vtok_scalar(act):
        act.wait_ge(vtok_pe, 1)
        nc.scalar.activation(Vtok[:, :, :], ps[:, 0:2, :], ACT.Copy).then_inc(vtok_act, 1)

    def pattn_scores(pe, j):
        pe.wait_ge(pa_queries, j + 1)
        for b in range(2):
            for i in range(4):
                mm = nc.tensor.matmul(ps[:, 2 * b + i // 2, (i % 2) * TP:(i % 2) * TP + TP],
                                      Qm[:, i, b * P:b * P + P], projT[:, ds(j + 4, 1), 0:TP],
                                      start=True, stop=True)
            mm.then_inc(pa_scored, 1)

    def pattn_tensor(pe, j, more):
        pe.wait_ge(pa_act.sem, pa_act.at("os1", j) - 4)
        for b in range(2):
            pe.wait_ge(pa_dve.sem, pa_dve.at(f"pr{b}", j))
            for h2 in range(2):
                for kt in range(2):
                    mm = nc.tensor.transpose(ps[:, 4 + 3 * b, (2 * h2 + kt) * P:(2 * h2 + kt + 1) * P],
                                             prP[b][:, h2, kt * P:kt * P + P], ident)
            mm.then_inc(pa_pe.sem, 1)
        if more:
            pattn_scores(pe, j + 1)
        pe.wait_ge(pa_dve.sem, pa_dve.at("values", j))
        for b in range(2):
            pe.wait_ge(pa_act.sem, pa_act.at(f"prTs{b}", j))
            for h2 in range(2):
                for kt in range(b + 1):
                    mm = nc.tensor.matmul(ps[64 * h2:64 * h2 + 64, 4 + 3 * b, 0:P],
                                          Vst[:, kt, 64 * h2:64 * h2 + 64],
                                          prPT[b][:, 2 * h2 + kt, :], start=kt == 0, stop=kt == b)
            mm.then_inc(pa_pe.sem, 1)

    def pattn_queries(dve, j):
        for i in range(4):
            last = nc.vector.tensor_scalar(Qm[:, i:i + 1, :], projT[:, ds(j, 1), 0:TP],
                                           cst["rowmask"][:, i:i + 1], SCALE, ALU.mult, ALU.mult)
        last.then_inc(pa_queries, 1)

    def pattn_max(dve, j):
        for b in range(2):
            dve.wait_ge(pa_scored, 2 * j + (b + 1))
            for h2 in range(2):
                nc.vector.scalar_tensor_tensor(
                    sP[b][:, 2 * h2:2 * h2 + 2, :], dist[:, b, :].unsqueeze(1).to_broadcast([P, 2, TP]),
                    cst["slope"][:, ds(2 * j + h2, 1)],
                    ps[:, 2 * b + h2, :].rearrange("p (m k) -> p m k", m=2), ALU.mult, ALU.add)
            dve.drain()
            nc.vector.tensor_reduce(nmaxP[:, 4 * b:4 * b + 4], sP[b][:, :, :], AX.X, ALU.max)
            dve.drain()
            nc.vector.tensor_scalar(nmaxP[:, 4 * b:4 * b + 4], nmaxP[:, 4 * b:4 * b + 4], -1.0,
                                    None, ALU.mult).then_inc(pa_max, 1)

    def pattn_vector(dve, j, more):
        if more:
            dve.wait_ge(pa_scored, 2 * j + 2)
            pattn_queries(dve, j + 1)
        for b in range(2):
            dve.wait_ge(pa_exp, 2 * j + (b + 1))
            l = lP[:, 4 * b:4 * b + 4]
            nc.vector.reciprocal(l, l)
            dve.drain()
            nc.vector.tensor_scalar(l[:, 1:4:2], l[:, 1:4:2], lam, None, ALU.mult)
            dve.drain()
            for h2 in range(2):
                nc.vector.tensor_scalar(sP[b][:, 2 * h2 + 1, :], sP[b][:, 2 * h2 + 1, :],
                                        l[:, 2 * h2 + 1:2 * h2 + 2], None, ALU.mult)
            dve.drain()
            for h2 in range(2):
                last = nc.vector.scalar_tensor_tensor(
                    prP[b][:, h2, :], sP[b][:, 2 * h2, :], l[:, 2 * h2:2 * h2 + 1],
                    sP[b][:, 2 * h2 + 1, :], ALU.mult, ALU.subtract)
            last.then_inc(pa_dve.sem, 1)
        dve.wait_ge(pa_pe.sem, pa_pe.at("o1", j) - 4)
        nc.vector.tensor_copy(Vst[:, :, :], Vtok[:, :, ds(j * P, P)]).then_inc(pa_dve.sem, 1)
        if more:
            pattn_max(dve, j + 1)

    def pattn_exp(act, j):
        for b in range(2):
            act.wait_ge(pa_max, 2 * j + (b + 1))
            for i in range(4):
                last = nc.scalar.activation(sP[b][:, i, :], sP[b][:, i, :], ACT.Exp,
                                            bias=nmaxP[:, 4 * b + i:4 * b + i + 1],
                                            accum_out=lP[:, 4 * b + i:4 * b + i + 1])
            last.then_inc(pa_exp, 1)

    def pattn_scalar(act, j, more):
        for b in range(2):
            act.wait_ge(pa_pe.sem, pa_pe.at(f"prT{b}", j))
            nc.scalar.activation(prPT[b][:, :, :].rearrange("p a k -> p (a k)"),
                                 ps[:, 4 + 3 * b, :], ACT.Copy).then_inc(pa_act.sem, 1)
        for b in range(2):
            act.wait_ge(pa_pe.sem, pa_pe.at(f"o{b}", j))
            nc.scalar.activation(mixT[:, ds(j, 1), b * P:b * P + P],
                                 ps[:, 4 + 3 * b:5 + 3 * b, 0:P], ACT.Copy).then_inc(pa_act.sem, 1)
        if more:
            pattn_exp(act, j + 1)

    k_landed = [sem(f"k_pages{i}") for i in range(2)]
    v_landed = [sem(f"v_pages{i}") for i in range(2)]
    sa_queries = [sem(f"sattn_queries{i}") for i in range(2)]
    sa_dve = [Steps(sem(f"sattn_dve{i}"), ["smax", "cm", "om"]) for i in range(2)]
    sa_pe = [Steps(sem(f"sattn_pe{i}"), ["S", "PT", "O", "F"], 4) for i in range(2)]
    sa_act = [Steps(sem(f"sattn_act{i}"), ["vn", "exp", "pT", "ms"], 4) for i in range(2)]

    def sattn_load(pool):
        pool.wait_ge(consts_in, 16 * N_CONST_LOADS)
        k_h, v_h = a["cache_k"], a["cache_v"]
        pool.wait_ge(shift_done, 1)
        with pool.Fori(0, NB // 2) as i:
            for par in range(2):
                if par == 1:
                    pool.wait_ge(pa_pe.sem, pa_pe.at("o1", 3))
                for g in range(NPG):
                    page = pool.value_load(ptab[0:1, ds(i * (2 * NPG) + (par * NPG + g), 1)],
                                           min_val=0, max_val=N_POOL - 1)
                    if g == 0:
                        pool.wait_ge(sa_pe[par].sem, sa_pe[par].at("S", i) - 4)
                    pool.dma_start(Kp[par][:, g, :, :].rearrange("p j n -> p (j n)"),
                                   k_h[ds(page, 1)].rearrange("o p n -> p (o n)")
                                   ).then_inc(k_landed[par], 16)
                for g in range(NPG):
                    page = pool.value_load(ptab[0:1, ds(i * (2 * NPG) + (par * NPG + g), 1)],
                                           min_val=0, max_val=N_POOL - 1)
                    if g == 0:
                        pool.wait_ge(sa_pe[par].sem, sa_pe[par].at("O", i) - 4)
                    pool.dma_start(Vp[par][:, g, :],
                                   v_h[ds(page, 1)].rearrange("o p n -> p (o n)")
                                   ).then_inc(v_landed[par], 16)

    def sattn_queries(dve, par, i):
        tok = i * (2 * DS) + (TP + par * DS)
        dve.wait_ge(sa_pe[par].sem, sa_pe[par].at("S", i) - 4)
        for r in range(4):
            nc.vector.tensor_scalar(Qs[par][:, :, 8 * r:8 * r + 8], projT[:, 0:4, ds(tok, DS)],
                                    cst["rowmask"][:, r:r + 1], SCALE, ALU.mult, ALU.mult)
        nc.vector.tensor_copy(kvn[par][:, :, :], projT[:, 4:12, ds(tok, DS)]
                              ).then_inc(sa_queries[par], 1)

    def sattn_max(dve, par, i):
        dve.wait_ge(sa_pe[par].sem, sa_pe[par].at("S", i))
        s = sS[par]
        nc.vector.tensor_tensor(s[:, 0:PAST].rearrange("p (h k) -> p h k", h=2),
                                ps[:, 2 * par:2 * par + 2, :],
                                biasS[:, 0:PAST].rearrange("p (h k) -> p h k", h=2), ALU.add)
        nc.vector.tensor_tensor(s[:, PAST:PAST + DS], ps[:, 4, DS * par:DS * par + DS],
                                biasS[:, PAST:PAST + DS], ALU.add)
        dve.drain()
        nm = nmaxS[:, par:par + 1]
        nc.vector.tensor_reduce(nm, s, AX.X, ALU.max)
        dve.drain()
        nc.vector.tensor_scalar(nm, nm, -1.0, None, ALU.mult).then_inc(sa_dve[par].sem, 1)

    def sattn_weights(dve, par, i):
        dve.wait_ge(sa_act[par].sem, sa_act[par].at("exp", i))
        l = lS[:, par:par + 1]
        nc.vector.reciprocal(l, l)
        dve.drain()
        nc.vector.tensor_scalar(Cm[par], cst["pairsum"], l, coef, ALU.mult,
                                ALU.mult).then_inc(sa_dve[par].sem, 1)

    def sattn_vector(dve, i, more):
        for par in range(2):
            nxt = par == 0 or more
            if nxt:
                sattn_max(dve, 1 - par, i + par)
            if more:
                sattn_queries(dve, par, i + 1)
            dve.wait_ge(sa_pe[par].sem, sa_pe[par].at("O", i))
            nc.vector.tensor_tensor(om[par], ps[:, 6 + par, :], ownhead, ALU.mult
                                    ).then_inc(sa_dve[par].sem, 1)
            if nxt:
                sattn_weights(dve, 1 - par, i + par)

    def sattn_scores(pe, par, i, more_before=True):
        pe.wait_ge(sa_queries[par], i + 1)
        pe.wait_ge(k_landed[par], 16 * NPG * (i + 1))
        pe.wait_ge(sa_act[par].sem, sa_act[par].at("ms", i) - 4)
        if par or more_before:
            pe.wait_ge(sa_dve[1 - par].sem, sa_dve[1 - par].at("smax", i) - 3 * (1 - par))
        for hf in range(2):
            for j in range(4):
                nc.tensor.matmul(ps[32 * j:32 * j + 32, 2 * par + hf, :], Qs[par][:, j, :],
                                 Kp[par][:, 4 * hf:4 * hf + 4, j, :], start=True, stop=True)
        for j in range(4):
            nc.tensor.matmul(ps[32 * j:32 * j + 32, 4, DS * par:DS * par + DS], Qs[par][:, j, :],
                             kvn[par][:, j, :], start=True, stop=True)
        for j in range(4):
            mm = nc.tensor.transpose(ps[0:DS, 6 + par, j * P:j * P + P], kvn[par][:, 4 + j, :],
                                     ident)
        mm.then_inc(sa_pe[par].sem, 1)

    def sattn_tensor(pe, i, more):
        for par in range(2):
            if par == 0 or more:
                sattn_scores(pe, 1 - par, i + par)
            pe.wait_ge(sa_dve[par].sem, sa_dve[par].at("cm", i))
            for g in range(NPG):
                nc.tensor.matmul(ps[:, 2 * par, 64 * g:64 * g + 64], sS[par][:, g * P:g * P + P],
                                 Cm[par], start=True, stop=True)
            mm = nc.tensor.matmul(ps[0:DS, 2 * par + 1, 0:64], sS[par][:, PAST:PAST + DS], Cm[par],
                                  start=True, stop=True)
            mm.then_inc(sa_pe[par].sem, 1)
            pe.wait_ge(sa_act[par].sem, sa_act[par].at("pT", i))
            pe.wait_ge(v_landed[par], 16 * NPG * (i + 1))
            nc.tensor.matmul(ps[0:64, 6 + par, :], prn[par][0:DS, :], vn[par][0:DS, :],
                             start=True, stop=False)
            for g in range(NPG):
                half = 64 * (g % 2)
                mm = nc.tensor.matmul(ps[half:half + 64, 6 + par, :], prTs[par][:, g, :],
                                      Vp[par][:, g, :], start=g == 1, stop=g >= NPG - 2)
            mm.then_inc(sa_pe[par].sem, 1)
            pe.wait_ge(sa_dve[par].sem, sa_dve[par].at("om", i))
            for j in range(4):
                mm = nc.tensor.matmul(ps[:, 2 * par + 1, 64 + DS * j:64 + DS * j + DS],
                                      om[par][:, j * P:j * P + P], cst["sumheads"],
                                      start=True, stop=True)
            mm.then_inc(sa_pe[par].sem, 1)

    def sattn_newvalues(act, par, i):
        act.wait_ge(sa_pe[par].sem, sa_pe[par].at("S", i))
        nc.scalar.activation(vn[par][0:DS, :], ps[0:DS, 6 + par, :], ACT.Copy
                             ).then_inc(sa_act[par].sem, 1)

    def sattn_exp(act, par, i):
        act.wait_ge(sa_dve[par].sem, sa_dve[par].at("smax", i))
        nc.scalar.activation(sS[par], sS[par], ACT.Exp, bias=nmaxS[:, par:par + 1],
                             accum_out=lS[:, par:par + 1]).then_inc(sa_act[par].sem, 1)

    def sattn_scalar(act, i, more):
        for par in range(2):
            nxt = par == 0 or more
            if nxt:
                sattn_newvalues(act, 1 - par, i + par)
            act.wait_ge(sa_pe[par].sem, sa_pe[par].at("PT", i))
            nc.scalar.activation(prn[par][0:DS, :], ps[0:DS, 2 * par + 1, 0:64], ACT.Copy)
            nc.scalar.activation(prTs[par][:, :, :].rearrange("p g n -> p (g n)"),
                                 ps[:, 2 * par, :], ACT.Copy).then_inc(sa_act[par].sem, 1)
            if nxt:
                sattn_exp(act, 1 - par, i + par)
            act.wait_ge(sa_pe[par].sem, sa_pe[par].at("F", i))
            nc.scalar.activation(
                mixT[:, 0:4, ds(i * (2 * DS) + (TP + par * DS), DS)],
                ps[:, 2 * par + 1, 64:64 + 4 * DS].rearrange("p (j s) -> p j s", s=DS),
                ACT.Copy).then_inc(sa_act[par].sem, 1)

    sub_sq = arena[:, 26 * T:30 * T].rearrange("p (j t) -> p j t", t=T)
    sub = {n: sem(f"subnorm_{n}") for n in ("sq", "sum", "var", "root", "done")}

    def subnorm_scalar(act):
        act.drain()
        nc.scalar.activation(sub_sq[:, :, :], mixT[:, 0:4, :], ACT.Square).then_inc(sub["sq"], 1)
        act.wait_ge(sub["var"], 1)
        nc.scalar.activation(sub_sq[:, :, :], sub_sq[:, :, :], ACT.Sqrt).then_inc(sub["root"], 1)

    def subnorm_tensor(pe):
        pe.wait_ge(sub["sq"], 1)
        for j in range(4):
            mm = nc.tensor.matmul(ps[:, j, 0:T], block64, sub_sq[:, j, :], start=True, stop=True)
        mm.then_inc(sub["sum"], 1)

    def subnorm_vector(dve):
        dve.wait_ge(sub["sum"], 1)
        nc.vector.tensor_scalar(sub_sq[:, :, :], ps[:, 0:4, 0:T], 1.0 / DV, RMS_EPS, ALU.mult,
                                ALU.add).then_inc(sub["var"], 1)
        dve.wait_ge(sub["root"], 1)
        nc.vector.reciprocal(sub_sq[:, :, :], sub_sq[:, :, :])
        dve.drain()
        nc.vector.tensor_tensor(mixT[:, 0:4, :], mixT[:, 0:4, :], sub_sq[:, :, :], ALU.mult)
        dve.drain()
        nc.vector.tensor_scalar(mixT[:, 0:4, :], mixT[:, 0:4, :], sgc, 1.0 - LAM_INIT, ALU.mult,
                                ALU.mult).then_inc(sub["done"], 1)

    xr, xk, xv = xb[:, 0:4, :], xb[:, 4:8, :], xb[:, 8:12, :]
    aR1 = Area(0)
    cumprev = aR1.take(4, T)
    cum = aR1.take(4, T)
    kk = aR1.take(4, T)
    aR = Area(base_b)
    kmod = aR.take(4, T)
    nb = aR.take(4, T)
    gup = aR.take(512)
    st = aR.take(5, 4 * P)
    stR, stQ, stK, stB, stV = (st[:, n, :].rearrange("p (j t) -> p j t", t=P) for n in range(5))
    ATm = aR.take(2, 512)
    S9 = aR.take(9, 256)
    Cst = aR.take(2, 256)
    Sbd = aR.take(2, 512)
    T1 = aR.take(256)
    T2 = aR.take(256)
    RW = aR.take(4, P)
    Y0 = aR.take(4, P)
    tokK, tokB, tokV = (aR.take(512) for _ in range(3))
    mats_at = aR.at
    mats = [{n: aR.take(512) for n in ("A0", "A1", "A2", "G", "ET", "MT", "NT", "QT", "X")}
            for _ in range(2)]
    ZF = aR.take(1024)
    for x in range(2):
        mats[x]["A3"] = ZF[:, 512 * x:512 * x + 512]
    pend = aR.take(4, 4)
    ex1, ex2, ex3 = (mats[0][n].rearrange("p (j t) -> p j t", t=P) for n in ("A0", "A1", "A2"))
    aM = Area(mats_at)
    scan_keep = aM.take(4 * T)
    waup = aM.take(512)
    aval = aM.take(4, T)
    tmpR = aM.take(4, T)
    yT = mixT[:, 4:8, :]
    post_sq = tmpR
    gg, bonus = cumprev, kk
    aD = Area(base_b + 2 * TP + PAST + DS + 512)
    diff = aD.take(14, T)

    shift_done, shift_saved = sem("token_shift_done"), sem("shift_saved")
    kv_stored, ones_ready = sem("outputs_stored"), sem("ones_ready")
    rwkv_in, attn_over = sem("rwkv_loads"), sem("attention_over")
    mix_ready = sem("mix_ready")
    rw_over = sem("rwkv_over")

    def shift_vector(dve):
        pb = projT[:, 12:26, :]
        dve.wait_ge(proj_ready, 1)
        nc.vector.tensor_copy(shift_out[:, :, :], pb[:, :, TP - 1:T:DS]).then_inc(shift_saved, 1)
        nc.vector.tensor_tensor(diff[:, :, 1:T], pb[:, :, 0:T - 1], pb[:, :, 1:T], ALU.subtract)
        dve.drain()
        nc.vector.tensor_scalar(diff[:, :, 0:1], pb[:, :, 0:1], -1.0, None, ALU.mult)
        nc.vector.tensor_tensor(diff[:, :, TP:T:DS], shift_in[:, :, :], pb[:, :, TP:T:DS],
                                ALU.subtract)
        dve.drain()
        for m in range(14):
            last = nc.vector.scalar_tensor_tensor(pb[:, m, :], diff[:, m, :], mu[:, m:m + 1],
                                                  pb[:, m, :], ALU.mult, ALU.add)
        last.then_inc(shift_done, 1)

    rp = {n: sem("rwkv_" + n) for n in ("gates", "lora", "sig", "kk_sq", "kk_sum", "kk_root",
                                        "kk_read", "prep")}

    def rwkv_loads(pool):
        pool.wait_ge(sub["done"], 1)
        pool.wait_ge(attn_over, 1)
        pool.wait_ge(kv_stored, 32)
        for dst, src in ((waup, a["wa_up"]), (gup, a["g_up"]), (scan_keep, a["scan_keep"]),
                         (S9[:, 1:9, :], a["s_init"])):
            pool.dma_start(dst, src).then_inc(rwkv_in, 16)

    def rwkv_prep_scalar(act):
        act.drain().then_inc(attn_over, 1)
        act.wait_ge(shift_done, 1)
        nc.scalar.activation(xb[0:64, 12, :], xb[0:64, 12, :], ACT.Tanh)
        nc.scalar.activation(xb[:, 13, :], xb[:, 13, :], ACT.Sigmoid).then_inc(rp["gates"], 1)
        act.wait_ge(rp["lora"], 1)
        act.wait_ge(kv_stored, 32)
        for j in range(4):
            nc.scalar.activation(cumprev[:, j, :], ps[:, j, 0:T], ACT.Sigmoid, bias=w0c[:, j:j + 1])
        for j in range(4):
            last = nc.scalar.activation(aval[:, j, :], ps[:, 4 + j, 0:T], ACT.Sigmoid,
                                        bias=a0c[:, j:j + 1])
        last.then_inc(rp["sig"], 1)
        act.wait_ge(rp["kk_sum"], 1)
        nc.scalar.activation(tmpR[:, :, :], ps[:, 0:4, 0:T], ACT.Sqrt).then_inc(rp["kk_root"], 1)

    def rwkv_prep_tensor(pe):
        pe.wait_ge(rp["gates"], 1)
        pe.wait_ge(rwkv_in, 64)
        pe.wait_ge(sub["var"], 1)
        for j in range(4):
            nc.tensor.matmul(ps[:, j, 0:T], waup[0:64, j * P:j * P + P], xb[0:64, 12, :],
                             start=True, stop=True)
        for j in range(4):
            mm = nc.tensor.matmul(ps[:, 4 + j, 0:T], waup[64:P, j * P:j * P + P], xb[64:P, 12, :],
                                  start=True, stop=True)
        mm.then_inc(rp["lora"], 1)
        pe.wait_ge(rp["kk_sq"], 1)
        pe.wait_ge(rp["sig"], 1)
        for j in range(4):
            mm = nc.tensor.matmul(ps[:, j, 0:T], block64, tmpR[:, j, :], start=True, stop=True)
        mm.then_inc(rp["kk_sum"], 1)

    def rwkv_prep_vector(dve):
        dve.wait_ge(rwkv_in, 64)
        for j in range(4):
            nc.vector.tensor_scalar(kk[:, j, :], xk[:, j, :], kkc[:, j:j + 1], None, ALU.mult)
        nc.vector.memset(S9[:, 0, :], 0.0)
        nc.vector.memset(Sbd[:, :, :], 0.0)
        dve.drain()
        nc.vector.tensor_tensor(tmpR[:, :, :], kk[:, :, :], kk[:, :, :], ALU.mult
                                ).then_inc(rp["kk_sq"], 1)
        dve.wait_ge(rp["sig"], 1)
        flat = "p j t -> p (j t)"
        nc.vector.tensor_tensor_scan(cum[:, :, :].rearrange(flat), scan_keep,
                                     cumprev[:, :, :].rearrange(flat), 0.0, ALU.mult, ALU.add)
        dve.drain()
        nc.vector.tensor_tensor(cumprev[:, :, :], cum[:, :, :], cumprev[:, :, :], ALU.subtract)
        for j in range(4):
            nc.vector.tensor_scalar(kmod[:, j, :], aval[:, j, :], 1.0, kac[:, j:j + 1],
                                    ALU.subtract, ALU.mult)
        dve.drain()
        nc.vector.scalar_tensor_tensor(kmod[:, :, :].rearrange(flat), kmod[:, :, :].rearrange(flat),
                                       1.0, xk[:, :, :].rearrange(flat), ALU.add, ALU.mult)
        dve.wait_ge(rp["kk_root"], 1)
        nc.vector.tensor_scalar(tmpR[:, :, :], tmpR[:, :, :], 1e-12, None, ALU.max)
        dve.drain()
        nc.vector.reciprocal(tmpR[:, :, :], tmpR[:, :, :])
        dve.drain()
        nc.vector.tensor_tensor(kk[:, :, :], kk[:, :, :], tmpR[:, :, :], ALU.mult)
        dve.drain()
        nc.vector.scalar_tensor_tensor(nb[:, :, :].rearrange(flat), kk[:, :, :].rearrange(flat),
                                       -1.0, aval[:, :, :].rearrange(flat), ALU.mult, ALU.mult)
        dve.drain().then_inc(rp["prep"], 1)

    PER = ["turn"] + [f"{x}{h}" for x in ("s1", "s2", "s3", "s4", "s5", "s6", "s7", "s8")
                      for h in range(2)]
    PER += ["yr", "wc0", "wc1", "y0", "wc2", "y1", "wc3", "y2", "y3"]
    DVR = ["prod"] + [f"m1{h}" for h in range(2)] + [f"qx{h}" for h in range(2)]
    DVR += [f"g{n}{h}" for n in (1, 2, 3) for h in range(2)] + [f"zf{h}" for h in range(2)]
    DVR += ["rw", "ac0", "ac1", "s0", "ac2", "s1", "ac3", "s2", "s3", "yt"]
    ACR = ["exps", "tok"] + [f"{x}{h}" for x in ("sq2", "sq4", "sq8", "z", "ez") for h in range(2)]
    ACR += ["y0"] + [f"bd{c}" for c in range(4)]
    r_pe, r_dve, r_act = sem("rtile_pe"), sem("rtile_dve"), sem("rtile_act")
    rpe = [Steps(r_pe, PER, x * 2 * len(PER)) for x in range(2)]
    RD0 = 1
    rdve = [Steps(r_dve, DVR, x * 2 * len(DVR) + RD0) for x in range(2)]
    ract = [Steps(r_act, ACR, x * 2 * len(ACR)) for x in range(2)]

    UW = ZF.rearrange("p (j u h v) -> p j u h v", j=4, u=2, h=2)

    def heads4(m):
        return m.rearrange("p (h t) -> p h t", t=P)

    def tile_views(part, i):
        if part == 0:
            return (lambda x: x[:, :, ds(i * P, P)], lambda x: x, lambda x: x, P)
        four = "p j (b s) -> p j b s"
        return (lambda x: x[:, :, ds(i * 4 * DS + TP, 4 * DS)].rearrange(four, s=DS),
                lambda x: x.rearrange("p j (b s) -> p j b s", s=RC)[:, :, :, 0:DS],
                lambda x: x[:, :, 0:4 * DS].rearrange(four, s=DS), 4 * DS)

    def state(part, i, cc):
        return S9[:, 0:1, :] if part == 0 else S9[:, ds(i * 4 + (cc + 1), 1), :]

    def rtile_vector(dve, part, i):
        col, stg, comp, n = tile_views(part, i)
        D_, A_, P_ = rdve[part], ract[part], rpe[part]
        dve.wait_ge(r_act, A_.at("exps", i))
        for dst, x, e in ((stR, xr, ex1), (stQ, kk, ex3), (stK, kmod, ex2), (stB, nb, ex2)):
            nc.vector.tensor_tensor(stg(dst), col(x), comp(e), ALU.mult)
        nc.vector.tensor_copy(stg(stV), col(xv))
        step = n // 4
        nc.vector.tensor_copy(pend[:, :, :], ex1[:, :, step - 1:n:step]).then_inc(r_dve, 1)

        def masked(dst, b, mask):
            nc.vector.tensor_tensor(heads4(dst), heads4(ps[:, b, :]),
                                    cst[mask].unsqueeze(1).to_broadcast([P, 4, P]), ALU.mult)
        for h in range(2):
            m, b = mats[h], 4 * h
            dve.wait_ge(r_pe, P_.at(f"s1{h}", i))
            masked(m["A0"], b, "low16")
            masked(m["A1"], b + 1, "up16")
            masked(m["ET"], b + 1, "up32off")
            masked(m["MT"], b + 2, "up32")
            masked(m["NT"], b + 3, "up32incl")
            dve.drain()
            nc.vector.tensor_tensor(heads4(m["G"]), heads4(m["A1"]),
                                    ident.unsqueeze(1).to_broadcast([P, 4, P]), ALU.add
                                    ).then_inc(r_dve, 1)
        for h in range(2):
            m, b = mats[h], 4 * h
            dve.wait_ge(r_pe, P_.at(f"s2{h}", i))
            masked(m["QT"], b + 2, "up32incl")
            nc.vector.tensor_copy(heads4(m["X"])[:, :, 0:64],
                                  ps[:, b + 3, 0:256].rearrange("p (k v) -> p k v", v=64)
                                  ).then_inc(r_dve, 1)
        for s, src in (("s3", 2), ("s4", 3), ("s5", 1)):
            for h in range(2):
                m, b = mats[h], 4 * h
                dve.wait_ge(r_pe, P_.at(f"{s}{h}", i))
                nc.vector.tensor_tensor(m["G"], m["G"], ps[:, b + src, :], ALU.add
                                        ).then_inc(r_dve, 1)
        for h in range(2):
            m, b = mats[h], 4 * h
            dve.wait_ge(r_pe, P_.at(f"s8{h}", i))
            v = "p (k u v) -> p k u v"
            nc.vector.tensor_tensor(UW[:, :, :, h, :], m["A0"].rearrange(v, u=2, v=64),
                                    ps[:, b, :].rearrange(v, u=2, v=64), ALU.add
                                    ).then_inc(r_dve, 1)
        dve.wait_ge(r_pe, P_.at("yr", i))
        nc.vector.tensor_tensor(RW[:, :, :].rearrange("p j t -> p (j t)"), st[:, 0, :],
                                ps[:, 1, :], ALU.add).then_inc(r_dve, 1)

        def chunk_matrices(cc):
            dve.wait_ge(r_pe, P_.at(f"wc{cc}", i))
            t = cc % 2
            nc.vector.tensor_tensor(heads4(ATm[:, t, :]), heads4(ps[:, 2 + 2 * t, :]),
                                    block64.unsqueeze(1).to_broadcast([P, 4, P]), ALU.mult)
            for q in (0, 64):
                last = nc.vector.tensor_tensor(
                    Cst[q:q + 64, t, :].rearrange("p (j v) -> p j v", v=64),
                    heads4(ps[q:q + 64, 3 + 2 * t, :])[:, :, q:q + 64],
                    pend[q:q + 64, :, cc:cc + 1].to_broadcast([64, 4, 64]), ALU.mult)
            last.then_inc(r_dve, 1)

        def chunk_state(cc):
            s = state(part, i, cc)
            pe4 = pend[:, :, cc:cc + 1].to_broadcast([P, 4, 64])
            v4 = "p o (j v) -> p (o j) v"
            nc.vector.tensor_tensor(T1.rearrange("p (j v) -> p j v", v=64), s.rearrange(v4, v=64),
                                    pe4, ALU.mult)
            dve.drain()
            nc.vector.tensor_tensor(T1, T1, Cst[:, cc % 2, :], ALU.add)
            dve.wait_ge(r_pe, P_.at(f"y{cc}", i))
            nc.vector.tensor_tensor(T2.rearrange("p (j v) -> p j v", v=64),
                                    ps[:, 6, 0:256].rearrange("p (j v) -> p j v", v=64), pe4,
                                    ALU.mult)
            dve.drain()
            nc.vector.tensor_tensor(s, T1.unsqueeze(1), T2.unsqueeze(1), ALU.add
                                    ).then_inc(r_dve, 1)
            dve.drain()
        chunk_matrices(0)
        chunk_matrices(1)
        chunk_state(0)
        chunk_matrices(2)
        chunk_state(1)
        chunk_matrices(3)
        chunk_state(2)
        chunk_state(3)
        dve.wait_ge(r_act, A_.at("y0", i))
        nc.vector.tensor_tensor(col(yT), stg(ps[:, 7, :].rearrange("p (j t) -> p j t", t=P)),
                                stg(Y0), ALU.add).then_inc(r_dve, 1)

    def rtile_scalar(act, part, i):
        col, stg, comp, n = tile_views(part, i)
        D_, A_, P_ = rdve[part], ract[part], rpe[part]
        if part == 0:
            act.wait_ge(rp["prep"], 1)
        act.wait_ge(r_dve, D_.base + i * len(DVR))
        for dst, src, s in ((ex1, cum, -KAPPA), (ex2, cum, KAPPA), (ex3, cumprev, -KAPPA)):
            last = nc.scalar.activation(comp(dst), col(src), ACT.Exp, scale=s)
        last.then_inc(r_act, 1)
        act.wait_ge(r_pe, P_.at("turn", i))
        for dst, b in ((tokK, 1), (tokB, 2), (tokV, 3)):
            nc.scalar.activation(dst, ps[:, b, :], ACT.Copy)
        for h in range(2):
            last = nc.scalar.activation(
                heads4(mats[h]["X"])[:, :, 64:P],
                ps[:, 0, :].rearrange("p (k h v) -> p k h v", h=2, v=64)[:, :, h, :], ACT.Copy)
        last.then_inc(r_act, 1)
        for s, pairs in (("s2", (("A2", 0), ("A3", 1))), ("s3", (("A0", 0), ("A1", 1))),
                         ("s4", (("A2", 0),)), ("s6", (("A0", 2),)), ("s7", (("A1", 3),))):
            for h in range(2):
                act.wait_ge(r_pe, P_.at(f"{s}{h}", i))
                for dst, b in pairs:
                    last = nc.scalar.activation(mats[h][dst], ps[:, 4 * h + b, :], ACT.Copy)
                last.then_inc(r_act, 1)
        act.wait_ge(r_pe, P_.at("yr", i))
        nc.scalar.activation(Y0[:, :, :].rearrange("p j t -> p (j t)"), ps[:, 0, :], ACT.Copy
                             ).then_inc(r_act, 1)
        for cc in range(4):
            if cc:
                act.wait_ge(r_dve, D_.at(f"s{cc - 1}", i))
            if cc > 1:
                act.wait_ge(r_pe, P_.at(f"y{cc - 2}", i))
            s = state(part, i, cc)
            for q in (0, 64):
                last = nc.scalar.activation(
                    Sbd[q:q + 64, cc % 2, :].rearrange("p (o j v) -> p o j v", o=1, v=P)[:, :, :, q:q + 64],
                    s[q:q + 64, :, :].rearrange("p o (j v) -> p o j v", v=64), ACT.Copy)
            last.then_inc(r_act, 1)

    def rtile_tensor(pe, part, i):
        D_, A_, P_ = rdve[part], ract[part], rpe[part]
        mm_ = nc.tensor.matmul
        pe.wait_ge(r_dve, D_.at("prod", i))
        for b, src in ((0, stQ), (1, stK), (2, stB), (3, stV)):
            for j in range(4):
                last = nc.tensor.transpose(ps[:, b, j * P:j * P + P], src[:, j, :], ident)
        last.then_inc(r_pe, 1)

        def head(x, h, k):
            return x[64 * h:64 * h + 64, k, :]

        def four(b, f):
            for k in range(4):
                lhsT, rhs = f(k)
                n = rhs.free_size()
                last = mm_(ps[:, b, k * n:k * n + n], lhsT, rhs, start=True, stop=True)
            return last

        def mat(h, name):
            m = mats[h][name]
            return lambda k: m[:, k * P:k * P + P]
        for h in range(2):
            b = 4 * h
            if h == 0:
                pe.wait_ge(r_act, A_.at("tok", i))
            four(b, lambda k: (head(stQ, h, k), head(stB, h, k)))
            four(b + 1, lambda k: (head(stB, h, k), head(stQ, h, k)))
            four(b + 2, lambda k: (head(stK, h, k), head(stQ, h, k)))
            four(b + 3, lambda k: (head(stK, h, k), head(stR, h, k))).then_inc(r_pe, 1)
        for h in range(2):
            b = 4 * h
            pe.wait_ge(r_dve, D_.at(f"m1{h}", i))
            A0, A1, MT = mat(h, "A0"), mat(h, "A1"), mat(h, "MT")
            four(b, lambda k: (A1(k), A0(k)))
            four(b + 1, lambda k: (A0(k), A1(k)))
            four(b + 2, lambda k: (head(stB, h, k), head(stR, h, k)))
            four(b + 3, lambda k: (MT(k), tokV[:, (2 * k + h) * 64:(2 * k + h) * 64 + 64])
                 ).then_inc(r_pe, 1)
        for h in range(2):
            b = 4 * h
            A2, A3, G = mat(h, "A2"), mat(h, "A3"), mat(h, "G")
            pe.wait_ge(r_act, A_.at(f"sq2{h}", i))
            four(b, lambda k: (A3(k), A2(k)))
            four(b + 1, lambda k: (A2(k), A3(k)))
            pe.wait_ge(r_dve, D_.at(f"qx{h}", i))
            four(b + 2, lambda k: (A2(k), G(k))).then_inc(r_pe, 1)
        for h in range(2):
            b = 4 * h
            A0, A1, G = mat(h, "A0"), mat(h, "A1"), mat(h, "G")
            pe.wait_ge(r_act, A_.at(f"sq4{h}", i))
            four(b, lambda k: (A1(k), A0(k)))
            pe.wait_ge(r_dve, D_.at(f"g1{h}", i))
            four(b + 3, lambda k: (A0(k), G(k))).then_inc(r_pe, 1)
        for h in range(2):
            b = 4 * h
            A2, G = mat(h, "A2"), mat(h, "G")
            pe.wait_ge(r_act, A_.at(f"sq8{h}", i))
            pe.wait_ge(r_dve, D_.at(f"g2{h}", i))
            four(b + 1, lambda k: (A2(k), G(k))).then_inc(r_pe, 1)
        for h in range(2):
            b = 4 * h
            G = mat(h, "G")
            pe.wait_ge(r_dve, D_.at(f"g3{h}", i))
            X = mat(h, "X")
            four(b + 2, lambda k: (G(k), X(k))).then_inc(r_pe, 1)
        for h in range(2):
            b = 4 * h
            ET = mat(h, "ET")
            pe.wait_ge(r_act, A_.at(f"z{h}", i))
            A0 = mat(h, "A0")
            four(b + 3, lambda k: (ET(k), A0(k))).then_inc(r_pe, 1)
        for h in range(2):
            b = 4 * h
            G = mat(h, "G")
            pe.wait_ge(r_act, A_.at(f"ez{h}", i))
            A1 = mat(h, "A1")
            four(b, lambda k: (G(k), A1(k))).then_inc(r_pe, 1)
        pe.wait_ge(r_dve, D_.at("zf1", i))
        for q in range(8):
            h, k = q % 2, q // 2
            half, j = 64 * (q % 2), q // 2
            U0, W = UW[:, k, 0, h, :], UW[:, k, 1, h, :]
            QT, NT = mat(h, "QT")(k), mat(h, "NT")(k)
            y = ps[half:half + 64, 0, j * P:j * P + P]
            mm_(y, tokV[:, q * 64:q * 64 + 64], NT, start=True, stop=False)
            mm_(y, U0, QT, start=False, stop=True)
            last = mm_(ps[half:half + 64, 1, j * P:j * P + P], W, QT, start=True, stop=True)
        last.then_inc(r_pe, 1)

        def chunk_products(cc):
            t, r = cc % 2, slice(RC * cc, RC * cc + RC)
            for j in range(4):
                m = ZF[r, 2 * P * j:2 * P * j + 2 * P]
                B, K, V = (x[r, j * P:j * P + P] for x in (tokB, tokK, tokV))
                mm_(ps[:, 2 + 2 * t, j * P:j * P + P], m[:, P:2 * P], B, start=True, stop=True)
                c = ps[:, 3 + 2 * t, j * P:j * P + P]
                mm_(c, K, V, start=True, stop=False)
                last = mm_(c, B, m[:, 0:P], start=False, stop=True)
            last.then_inc(r_pe, 1)

        def chunk_step(cc):
            s = state(part, i, cc)
            pe.wait_ge(r_dve, D_.at(f"ac{cc}", i))
            if cc:
                pe.wait_ge(r_dve, D_.at(f"s{cc - 1}", i))
            for j in range(4):
                mm_(ps[:, 6, j * 64:j * 64 + 64], ATm[:, cc % 2, j * P:j * P + P],
                    s[:, :, j * 64:j * 64 + 64], start=True, stop=True)
            pe.wait_ge(r_act, A_.at(f"bd{cc}", i))
            for j in range(4):
                last = mm_(ps[:, 7, j * P + RC * cc:j * P + RC * cc + RC],
                           Sbd[:, cc % 2, j * P:j * P + P], RW[:, j, RC * cc:RC * cc + RC],
                           start=True, stop=True)
            last.then_inc(r_pe, 1)
        chunk_products(0)
        chunk_products(1)
        pe.wait_ge(r_dve, D_.at("rw", i))
        chunk_step(0)
        chunk_products(2)
        chunk_step(1)
        chunk_products(3)
        chunk_step(2)
        chunk_step(3)


    po = {n: sem("rwkv_post_" + n) for n in ("rk", "sums", "g", "mean", "cent", "sq", "var",
                                             "varr", "root", "over")}

    def rwkv_post_scalar(act):
        act.wait_ge(po["sums"], 1)
        nc.scalar.activation(gg[:, :, :], ps[:, 0:4, 0:T], ACT.Copy).then_inc(po["g"], 1)
        act.wait_ge(po["cent"], 1)
        nc.scalar.activation(post_sq[:, :, :], yT, ACT.Square).then_inc(po["sq"], 1)
        act.wait_ge(po["varr"], 1)
        nc.scalar.activation(post_sq[:, :, :], post_sq[:, :, :], ACT.Sqrt).then_inc(po["root"], 1)

    def rwkv_post_tensor(pe):
        pe.wait_ge(po["rk"], 1)
        for j in range(4):
            nc.tensor.matmul(ps[:, j, 0:T], gup[:, j * P:j * P + P], xb[:, 13, :], start=True,
                             stop=True)
        for j in range(4):
            mm = nc.tensor.matmul(ps[:, 4 + j, 0:T], block64, post_sq[:, j, :], start=True,
                                  stop=True)
        mm.then_inc(po["sums"], 1)
        pe.wait_ge(po["g"], 1)
        for j in range(4):
            mm = nc.tensor.matmul(ps[:, j, 0:T], block64, yT[:, j, :], start=True, stop=True)
        mm.then_inc(po["mean"], 1)
        pe.wait_ge(po["sq"], 1)
        for j in range(4):
            mm = nc.tensor.matmul(ps[:, 4 + j, 0:T], block64, post_sq[:, j, :], start=True,
                                  stop=True)
        mm.then_inc(po["var"], 1)

    def rwkv_post_vector(dve):
        dve.drain().then_inc(rw_over, 1)
        nc.vector.tensor_tensor(post_sq[:, :, :], xr, kmod[:, :, :], ALU.mult)
        dve.drain()
        for j in range(4):
            last = nc.vector.tensor_scalar(post_sq[:, j, :], post_sq[:, j, :], rkc[:, j:j + 1],
                                           None, ALU.mult)
        last.then_inc(po["rk"], 1)
        dve.wait_ge(po["sums"], 1)
        nc.vector.tensor_tensor(bonus[:, :, :], ps[:, 4:8, 0:T], xv, ALU.mult)
        dve.wait_ge(po["mean"], 1)
        nc.vector.scalar_tensor_tensor(yT, ps[:, 0:4, 0:T], -1.0 / 64, yT, ALU.mult, ALU.add
                                       ).then_inc(po["cent"], 1)
        dve.wait_ge(po["var"], 1)
        nc.vector.tensor_scalar(post_sq[:, :, :], ps[:, 4:8, 0:T], 1.0 / 64, LNX_EPS, ALU.mult,
                                ALU.add).then_inc(po["varr"], 1)
        dve.wait_ge(po["root"], 1)
        nc.vector.reciprocal(post_sq[:, :, :], post_sq[:, :, :])
        dve.drain()
        nc.vector.tensor_tensor(yT, yT, post_sq[:, :, :], ALU.mult)
        dve.drain()
        for j in range(4):
            nc.vector.tensor_scalar(yT[:, j, :], yT[:, j, :], lgc[:, j:j + 1], lbc[:, j:j + 1],
                                    ALU.mult, ALU.add)
        dve.drain()
        nc.vector.tensor_tensor(yT, yT, bonus[:, :, :], ALU.add)
        dve.drain()
        nc.vector.tensor_tensor(yT, yT, gg[:, :, :], ALU.mult).then_inc(mix_ready, 1)

    def rwkv_scalar(act):
        rwkv_prep_scalar(act)
        with act.Fori(0, 2) as i:
            rtile_scalar(act, 0, i)
            mod_scalar(act, G_MOD1, i + 8, i + 10)
        with act.Fori(0, 2) as i:
            rtile_scalar(act, 1, i)
        rwkv_post_scalar(act)

    def rwkv_vector(dve):
        rwkv_prep_vector(dve)
        dve.drain().then_inc(r_dve, RD0)
        with dve.Fori(0, 2) as i:
            rtile_vector(dve, 0, i)
            mod_vector(dve, i + 10)
        nc.vector.memset(st[:, :, :], 0.0)
        dve.drain()
        with dve.Fori(0, 2) as i:
            rtile_vector(dve, 1, i)
        rwkv_post_vector(dve)

    def rwkv_tensor(pe):
        rwkv_prep_tensor(pe)
        with pe.Fori(0, 2) as i:
            rtile_tensor(pe, 0, i)
            pe.wait_ge(r_dve, rdve[0].at("yt", i))
            mod_tensor(pe, G_MOD1, i + 8, i + 10)
        with pe.Fori(0, 2) as i:
            rtile_tensor(pe, 1, i)
        rwkv_post_tensor(pe)

    sgate = [arena[:, at_sgate + x * T:at_sgate + x * T + T] for x in range(2)]
    htmp = arena[:, at_htmp:at_htmp + 2 * T].rearrange("p (a t) -> p a t", t=T)
    hid_act, hid_ready = sem("gate_silu"), sem("hidden_ready")

    def gu_tensor(pe):
        pe.wait_ge(h_ready, 2)

        def body(c, k, i):
            pe.wait_ge(lo_ready, c + (S_GU + 1))
            wait_psum(pe, G_GU, c)
            w = parts(S_GU, k, 2 * KT, P)
            for t in range(2):
                for q in range(KT):
                    mm = three_passes(ps[:, pbank(G_GU, k) + t, 0:T],
                                      [v[:, t * KT + q, :] for v in w],
                                      [hx_hi[:, q, :], hx_lo[:, q, :]], q == 0, q == KT - 1)
            mm.then_inc(chunk_done, 1)
        by_four(pe, N_GU, body)

    def gu_split_first(act):
        act.wait_ge(mix_ready, 1)
        act.wait_ge(kv_stored, 16 * 4)
        split_hi(act, act_copy, G_GU, S_GU, 0, 0, 0, 2 * KT, P)

    def gu_scalar(act):
        def body(c, k, i):
            if not (isinstance(c, int) and c == N_GU - 1):
                c1, k1 = c + 1, k + 1
                split_hi(act, act_copy, G_GU, S_GU, c1, k1, i, 2 * KT, P)
            wait_done(act, G_GU, c)
            act.wait_ge(hid_ready, c + 1)
            nc.scalar.activation(sgate[k % 2], ps[:, pbank(G_GU, k), 0:T], ACT.Silu
                                 ).then_inc(hid_act, 1)
        by_four(act, N_GU, body)

    def gu_vector(dve):
        dve.drain().then_inc(hid_ready, 2)

        def body(c, k, i):
            h = htmp[:, k % 2:k % 2 + 1, :]
            hi = hid_hi[:, ds(c, 1), :]
            dve.wait_ge(hid_act, c + 1)
            nc.vector.tensor_tensor(h, sgate[k % 2].unsqueeze(1),
                                    ps[:, pbank(G_GU, k) + 1:pbank(G_GU, k) + 2, 0:T], ALU.mult
                                    ).then_inc(chunk_read, 1)
            dve.drain()
            nc.vector.tensor_copy(hi, h)
            dve.drain()
            nc.vector.tensor_tensor(hid_lo[:, ds(c, 1), :], h, hi.bitcast(F32), ALU.subtract)
            dve.drain().then_inc(hid_ready, 1)
        by_four(dve, N_GU, body)

    aO = Area(0)
    uT = aO.take(EC // P, T)
    vtk = aO.take(3, EC)
    bsB = aO.take(GC, T)
    stats = aO.take(3, 4, 6)
    aggr = aO.take(3, 2)
    assert aO.at <= at_split
    aU = Area(at_um)
    lnvg = aU.take(EC)
    lnvb = aU.take(EC)
    hflat = hT[:, :, :].rearrange("p k t -> p (k t)")
    wsT = hflat[:, 0:GC * CHUNK].rearrange("p (g t) -> p g t", t=CHUNK)
    wsS = hflat[:, GC * CHUNK:GC * (CHUNK + TS)].rearrange("p (g t) -> p g t", t=TS)
    mtmp = hflat[:, GC * (CHUNK + TS):GC * (CHUNK + TS) + 2 * T].rearrange("p (a t) -> p a t", a=2)
    odd_kn = (KT, 2 * P, KT * 256)
    out_o_kn = (EC // P, P, KT * 256)
    odd_in, odd_masked = sem("gmlp_loads"), sem("spatial_masked")
    u_ready, v_part = sem("u_ready"), sem("v_part")
    lnv_var, lnv_root, v_ready = sem("lnv_var"), sem("lnv_root"), sem("v_ready")
    mixed_mm, mixed_rd = sem("mixed_product"), sem("mixed_read")

    def odd_loads(pool):
        pool.wait_ge(x_ready, 3)
        for dst, src in ((lnvg, a["lnv_g"].partition_broadcast(P)),
                         (lnvb, a["lnv_b"].partition_broadcast(P)),
                         (bsB[:, :, :].rearrange("p g t -> p (g t)"), a["b_s"].partition_broadcast(P)),
                         (wsT[:, :, :], a["w_s"]), (wsS[0:TS, :, :], a["w_s8"])):
            if src is a["w_s"]:
                pool.wait_ge(h_ready, 3)
            pool.dma_start(dst, src).then_inc(odd_in, 16)

    def in_o_tensor(pe):
        columns_split(pe, G_IN_O, S_IN_O, 8, KT, 2, (hx_hi, hx_lo), lambda e: e.wait_ge(h_ready, 3),
                      KT * 256)

        def body(c, k, i):
            g0, s0 = G_IN_O + 8, S_IN_O + 8
            pe.wait_ge(lo_ready, c + (s0 + 1))
            wait_psum(pe, g0, c)
            w = parts(s0, k, KT, 2 * P, KT * 256)
            for n in range(3):
                rows = P if n < 2 else TS
                for q in range(KT):
                    mm = three_passes(
                        ps[0:rows, pbank(g0, k) + n // 2, (n % 2) * 256:(n % 2) * 256 + 256],
                        [v[:, q, n * P:n * P + rows] for v in (hx_hi, hx_lo)],
                        [v[:, q, :] for v in w], q == 0, q == KT - 1)
            mm.then_inc(chunk_done, 1)
        by_four(pe, 8, body)

    def in_o_scalar(act):
        def body_u(c, k, i):
            wait_done(act, G_IN_O, c)
            b = pbank(G_IN_O, k)
            nc.scalar.activation(uT[:, ds(2 * c, 2), :], ps[:, b:b + 2, 0:T], ACT.Gelu
                                 ).then_inc(chunk_read, 1)
        by_four(act, 8, body_u)
        act.drain().then_inc(u_ready, 1)

        def body_v(c, k, i):
            g0 = G_IN_O + 8
            wait_done(act, g0, c)
            b = pbank(g0, k)
            nc.scalar.activation(vtk[:, 0:2, ds(c * 256, 256)],
                                 ps[:, b, :].rearrange("p (n f) -> p n f", n=2), ACT.Gelu)
            nc.scalar.activation(vtk[0:TS, 2, ds(c * 256, 256)], ps[0:TS, b + 1, 0:256], ACT.Gelu
                                 ).then_inc(chunk_read, 1)
        by_four(act, 8, body_v)
        act.drain().then_inc(v_part, 1)
        act.wait_ge(lnv_var, 1)
        nc.scalar.activation(aggr[:, 0:2, 1:2], aggr[:, 0:2, 1:2], ACT.Sqrt)
        nc.scalar.activation(aggr[0:TS, 2, 1:2], aggr[0:TS, 2, 1:2], ACT.Sqrt
                             ).then_inc(lnv_root, 1)

    def v_norm_vector(dve):
        split_both(dve, G_IN_O, S_IN_O, 8, *odd_kn)
        dve.wait_ge(odd_in, 16 * 5)
        nc.vector.tensor_tensor(wsT[:, :, :], wsT[:, :, :],
                                cst["upincl"].unsqueeze(1).to_broadcast([P, GC, CHUNK]), ALU.mult)
        nc.vector.tensor_tensor(wsS[0:TS, :, :], wsS[0:TS, :, :],
                                cst["upincl8"][0:TS, 0:TS].unsqueeze(1).to_broadcast([TS, GC, TS]),
                                ALU.mult).then_inc(odd_masked, 1)
        split_both(dve, G_IN_O + 8, S_IN_O + 8, 8, *odd_kn)
        dve.wait_ge(v_part, 1)
        for n in range(3):
            rows = P if n < 2 else TS
            for q in range(4):
                nc.vector.bn_stats(stats[0:rows, n, q, :], vtk[0:rows, n, q * 512:q * 512 + 512])
        dve.drain()
        for n in range(3):
            rows = P if n < 2 else TS
            nc.vector.bn_aggr(aggr[0:rows, n, :], stats[0:rows, n, :, :])
        dve.drain()
        nc.vector.tensor_scalar(aggr[:, 0:2, 1:2], aggr[:, 0:2, 1:2], LN_EPS, None, ALU.add)
        nc.vector.tensor_scalar(aggr[0:TS, 2, 1:2], aggr[0:TS, 2, 1:2], LN_EPS, None, ALU.add
                                ).then_inc(lnv_var, 1)
        dve.wait_ge(lnv_root, 1)
        nc.vector.reciprocal(aggr[:, 0:2, 1:2], aggr[:, 0:2, 1:2])
        nc.vector.reciprocal(aggr[0:TS, 2, 1:2], aggr[0:TS, 2, 1:2])
        dve.drain()
        for n in range(3):
            rows = P if n < 2 else TS
            v = vtk[0:rows, n, :]
            nc.vector.tensor_scalar(v, v, aggr[0:rows, n, 0:1], aggr[0:rows, n, 1:2], ALU.subtract,
                                    ALU.mult)
            dve.drain()
            nc.vector.tensor_tensor(v, v, lnvg[0:rows, :], ALU.mult)
            dve.drain()
            last = nc.vector.tensor_tensor(v, v, lnvb[0:rows, :], ALU.add)
            last.then_inc(v_ready, 1)

    def mixed_tensor(pe):
        pe.wait_ge(odd_masked, 1)
        pe.wait_ge(v_ready, 3)
        for m in range(EC // P):
            g = m // 2
            if m >= 4:
                pe.wait_ge(mixed_rd, m - 3)
            for n in range(2):
                nc.tensor.matmul(ps[:, 4 + m % 4, n * P:n * P + P], vtk[:, n, m * P:m * P + P],
                                 wsT[:, g, :], start=True, stop=True)
            nc.tensor.matmul(ps[:, 4 + m % 4, TP:T], vtk[0:TS, 2, m * P:m * P + P],
                             wsS[0:TS, g, :], start=True, stop=True).then_inc(mixed_mm, 1)

    def mixed_vector(dve):
        dve.wait_ge(u_ready, 1)
        for m in range(EC // P):
            dve.wait_ge(mixed_mm, m + 1)
            nc.vector.tensor_tensor(mtmp[:, m % 2, :], ps[:, 4 + m % 4, 0:T], bsB[:, m // 2, :],
                                    ALU.add).then_inc(mixed_rd, 1)
            dve.drain()
            nc.vector.tensor_tensor(uT[:, m, :], uT[:, m, :], mtmp[:, m % 2, :], ALU.mult
                                    ).then_inc(gated, 1)

    def mixed_scalar(act):
        for m in range(EC // P):
            act.wait_ge(gated, m + 1)
            nc.scalar.activation(um_hi[:, m, :], uT[:, m, :], ACT.Copy).then_inc(gated_hi, 1)

    def mixed_pool(pool):
        for m in range(EC // P):
            pool.wait_ge(gated_hi, m + 1)
            pool.tensor_tensor(um_lo[:, m, :], uT[:, m, :], um_hi[:, m, :].bitcast(F32),
                               ALU.subtract).then_inc(gated_lo, 1)

    gated, gated_hi, gated_lo = sem("gated"), sem("gated_hi"), sem("gated_lo")

    aE = Area(0)
    h2tok = aE.take(3, D)
    acc = aE.take(KT, T)
    xg = aE.take(KT, CAP)
    hidE = aE.take(FE, CAP)
    sgE = [aE.take(CAP) for _ in range(2)]
    ye = aE.take(D)
    PgT = aE.take(T)
    Psel = aE.take(3, CAP)
    Pgat = aE.take(3, CAP)
    rw = aE.take(KT, NE)
    rbB = aE.take(NE)
    lgT = aE.take(T)
    lg = aE.take(3, NE)
    ex = aE.take(3, NE)
    cmpA = aE.take(3, 64)
    cmpB = aE.take(3, 64)
    beaten = aE.take(3, NE)
    sel = aE.take(3, NE + 1)
    gate = aE.take(3, NE + 1)
    rank = aE.take(3, NE + 1)
    tot = aE.take(NE)
    r1 = aE.take(3)
    r2 = aE.take(3)
    rounds_f = aE.take(2)
    router_in = sem("router_loads")
    rt_pe = Steps(sem("router_pe"), ["logits", "lgtok", "h2a", "h2b", "h2c", "rank"])
    rt_act = Steps(sem("router_act"), ["lgT", "h2a", "h2b", "h2c", "exp"])
    rt_dve = Steps(sem("router_dve"), ["max", "gate", "rounds"])
    EX0 = 1
    ex_pe = Steps(sem("expert_pe"), ["scatterA", "scatterB", "turned", "gather"], EX0)
    ex_dve = Steps(sem("expert_dve"), ["accA", "accB", "select"], EX0)
    ex_act = Steps(sem("expert_act"), ["PgT", "xg", "ye"], EX0)
    silu_e, hid_e = sem("expert_silu"), sem("expert_hidden")
    moe_over = sem("experts_over")

    def router_loads(pool):
        pool.wait_ge(x_ready, 4)
        pool.dma_start(rw[:, :, :], a["router_w"]).then_inc(router_in, 16)
        pool.dma_start(rbB, a["router_b"].partition_broadcast(P)).then_inc(router_in, 16)

    def router_tensor(pe):
        pe.wait_ge(router_in, 32)
        pe.wait_ge(h_ready, 4)
        for q in range(KT):
            mm = nc.tensor.matmul(ps[0:NE, 0, 0:T], rw[:, q, :], hT[:, q, :], start=q == 0,
                                  stop=q == KT - 1)
        mm.then_inc(rt_pe.sem, 1)
        pe.wait_ge(rt_act.sem, rt_act.at("lgT"))
        for n in range(3):
            rows = P if n < 2 else TS
            mm = nc.tensor.transpose(ps[0:rows, 1, n * NE:n * NE + NE], lgT[0:NE, n * P:n * P + rows],
                                     ident[0:NE, 0:NE])
        mm.then_inc(rt_pe.sem, 1)
        for n, name in enumerate("abc"):
            rows = P if n < 2 else TS
            for q in range(KT):
                mm = nc.tensor.transpose(ps[0:rows, 2 + 2 * n + q // 4, (q % 4) * P:(q % 4) * P + P],
                                         hT[:, q, n * P:n * P + rows], ident)
            mm.then_inc(rt_pe.sem, 1)
        pe.wait_ge(rt_dve.sem, rt_dve.at("gate"))
        up = cst["up"]
        for n in range(3):
            for m in range(n + 1):
                nc.tensor.matmul(ps[:, 0, n * NE:n * NE + NE], up if m == n else ones[:, :],
                                 sel[:, m, 0:NE], start=m == 0, stop=m == n)
        for m in range(3):
            mm = nc.tensor.matmul(ps[:, 0, 32:32 + NE], ones[:, :], sel[:, m, 0:NE], start=m == 0,
                                  stop=m == 2)
        mm.then_inc(rt_pe.sem, 1)

    def router_scalar(act):
        act.wait_ge(rt_pe.sem, rt_pe.at("logits"))
        nc.scalar.activation(lgT[0:NE, :], ps[0:NE, 0, 0:T], ACT.Copy).then_inc(rt_act.sem, 1)
        for n, name in enumerate("abc"):
            rows = P if n < 2 else TS
            act.wait_ge(rt_pe.sem, rt_pe.at("h2" + name))
            nc.scalar.activation(h2tok[0:rows, n, :].rearrange("p (a b) -> p a b", a=2),
                                 ps[0:rows, 2 + 2 * n:4 + 2 * n, :], ACT.Copy
                                 ).then_inc(rt_act.sem, 1)
        act.wait_ge(rt_dve.sem, rt_dve.at("max"))
        nc.scalar.activation(ex[:, :, :], ex[:, :, :], ACT.Exp).then_inc(rt_act.sem, 1)

    def router_vector(dve):
        dve.wait_ge(router_in, 32)
        nc.vector.memset(lg[:, :, :], 0.0)
        nc.vector.memset(acc[:, :, :], 0.0)
        dve.drain()
        dve.wait_ge(rt_pe.sem, rt_pe.at("lgtok"))
        b3 = rbB.unsqueeze(1)
        nc.vector.tensor_tensor(lg[:, 0:2, :], ps[:, 1, 0:2 * NE].rearrange("p (n e) -> p n e", e=NE),
                                b3.to_broadcast([P, 2, NE]), ALU.add)
        nc.vector.tensor_tensor(lg[0:TS, 2, :], ps[0:TS, 1, 2 * NE:3 * NE], rbB[0:TS, :], ALU.add)
        dve.drain()
        nc.vector.tensor_reduce(r1, lg[:, :, :], AX.X, ALU.max)
        dve.drain()
        nc.vector.tensor_tensor(ex[:, :, :], lg[:, :, :], r1.unsqueeze(2).to_broadcast([P, 3, NE]),
                                ALU.subtract).then_inc(rt_dve.sem, 1)
        full = [P, 3, NE, NE]
        mine = lg[:, :, :].unsqueeze(3).to_broadcast(full)
        other = lg[:, :, :].unsqueeze(2).to_broadcast(full)
        c4 = cmpA[:, :, :].rearrange("p n (e f) -> p n e f", f=NE)
        d4 = cmpB[:, :, :].rearrange("p n (e f) -> p n e f", f=NE)
        nc.vector.tensor_tensor(c4, other, mine, ALU.is_gt)
        nc.vector.tensor_tensor(d4, other, mine, ALU.is_equal)
        dve.drain()
        nc.vector.tensor_tensor(cmpB[:, :, :], cmpB[:, :, :],
                                cst["lower_e"].unsqueeze(1).to_broadcast([P, 3, 64]), ALU.mult)
        dve.drain()
        nc.vector.tensor_tensor(cmpA[:, :, :], cmpA[:, :, :], cmpB[:, :, :], ALU.add)
        dve.drain()
        nc.vector.tensor_reduce(beaten[:, :, :], c4, AX.X, ALU.add)
        dve.drain()
        nc.vector.tensor_scalar(sel[:, :, 0:NE], beaten[:, :, :], 1.5, None, ALU.is_lt)
        dve.drain()
        nc.vector.tensor_tensor(sel[:, :, 0:NE], sel[:, :, 0:NE],
                                cst["valid"].unsqueeze(2).to_broadcast([P, 3, NE]), ALU.mult)
        dve.wait_ge(rt_act.sem, rt_act.at("exp"))
        dve.drain()
        nc.vector.tensor_scalar(beaten[:, :, :], beaten[:, :, :], 1.5, None, ALU.is_lt)
        dve.drain()
        nc.vector.tensor_tensor(ex[:, :, :], ex[:, :, :], beaten[:, :, :], ALU.mult)
        dve.drain()
        nc.vector.tensor_reduce(r2, ex[:, :, :], AX.X, ALU.add)
        dve.drain()
        nc.vector.reciprocal(r2, r2)
        dve.drain()
        nc.vector.tensor_tensor(gate[:, :, 0:NE], ex[:, :, :], r2.unsqueeze(2).to_broadcast([P, 3, NE]),
                                ALU.mult).then_inc(rt_dve.sem, 1)
        dve.wait_ge(rt_pe.sem, rt_pe.at("rank"))
        nc.vector.tensor_copy(rank[:, :, 0:NE], ps[:, 0, 0:3 * NE].rearrange("p (n e) -> p n e", e=NE))
        nc.vector.tensor_reduce(tot[:, 0:1], ps[:, 0, 32:32 + NE], AX.X, ALU.max)
        dve.drain()
        nc.vector.tensor_copy(sel[:, :, NE:NE + 1], sel[:, :, 0:1])
        nc.vector.tensor_copy(gate[:, :, NE:NE + 1], gate[:, :, 0:1])
        nc.vector.tensor_scalar(rank[:, :, NE:NE + 1], rank[:, :, 0:1], -float(CAP), None, ALU.add)
        nc.vector.tensor_scalar(rounds_f[:, 0:1], tot[:, 0:1], CAP + 0.5, 1.0, ALU.is_gt, ALU.add)
        nc.vector.tensor_scalar(rounds_f[:, 1:2], tot[:, 0:1], 2 * CAP + 0.5, None, ALU.is_gt)
        dve.drain()
        nc.vector.tensor_tensor(rounds_i[:, 0:1], rounds_f[:, 0:1], rounds_f[:, 1:2], ALU.add
                                ).then_inc(rt_dve.sem, 1)

    def rounds(eng):
        eng.wait_ge(rt_dve.sem, rt_dve.at("rounds"))
        return eng.value_load(rounds_i[0:1, 0:1], min_val=1, max_val=3)

    def each_expert(eng, body, after_round=None):
        n = rounds(eng)
        with eng.Fori(0, n) as r:
            with eng.Fori(0, NE) as e:
                body(e, r * NE + e)
            if after_round is not None:
                after_round()

    S_BASE = [len([g for g in range(G_EXP) if g % RING == s]) for s in range(RING)]

    def expert_slot(j):
        return (G_EXP + j) % RING

    def expert_use(j, turn):
        s = expert_slot(j)
        per = len([q for q in range(N_EXP) if expert_slot(q) == s])
        before = len([q for q in range(j) if expert_slot(q) == s])
        return turn * per + (S_BASE[s] + before + 1)

    def gather_tensor(pe):
        for q in range(KT):
            for n in range(3):
                rows = P if n < 2 else TS
                mm = nc.tensor.matmul(ps[:, 4 + q // 4, (q % 4) * CAP:(q % 4) * CAP + CAP],
                                      h2tok[0:rows, n, q * P:q * P + P], Psel[0:rows, n, :],
                                      start=n == 0, stop=n == 2)
        mm.then_inc(ex_pe.sem, 1)

    def scatter_tensor(pe, hf, done):
        for q in range(4):
            m = 4 * hf + q
            mm = nc.tensor.matmul(ps[:, 4 + q, 0:T], ye[:, m * P:m * P + P], PgT, start=True,
                                  stop=True)
        mm.then_inc(done, 1)

    def expert_tensor(pe):
        pe.wait_ge(ex_dve.sem, EX0)
        gather_tensor(pe)

        def body(e, t):
            pe.wait_ge(ex_act.sem, 3 * t + EX0)
            for j in range(FE):
                g = G_EXP + j
                pe.wait_ge(landed[expert_slot(j)], 16 * expert_use(j, t))
                pe.wait_ge(chunk_read, N_EXP * t + (g + 1))
                w = ring[:, expert_slot(j), 0:2 * KT * P].rearrange("p (k n) -> p k n", n=P)
                for gu in range(2):
                    for q in range(KT):
                        mm = nc.tensor.matmul(ps[:, j % 2, gu * CAP:gu * CAP + CAP],
                                              w[:, gu * KT + q, :], xg[:, q, :], start=q == 0,
                                              stop=q == KT - 1)
                mm.then_inc(chunk_done, 1)
                if j == 0:
                    scatter_tensor(pe, 0, ex_pe.sem)
                if j == 1:
                    pe.wait_ge(ex_dve.sem, ex_dve.at("accA", t))
                    scatter_tensor(pe, 1, ex_pe.sem)
                if j == 2:
                    pe.wait_ge(ex_dve.sem, ex_dve.at("accB", t))
                    for n in range(3):
                        rows = P if n < 2 else TS
                        mm = nc.tensor.transpose(ps[:, 6, n * P:n * P + rows], Pgat[0:rows, n, :],
                                                 ident[0:rows, 0:rows])
                    mm.then_inc(ex_pe.sem, 1)
            pe.wait_ge(ex_dve.sem, ex_dve.at("select", t))
            gather_tensor(pe)
            pe.wait_ge(hid_e, FE * t + (FE + 2))
            for j in range(4):
                g = G_EXP + FE + j
                pe.wait_ge(landed[expert_slot(FE + j)], 16 * expert_use(FE + j, t))
                pe.wait_ge(chunk_read, N_EXP * t + (g + 1))
                w = ring[:, expert_slot(FE + j), 0:FE * 256].rearrange("p (k n) -> p k n", n=256)
                for q in range(FE):
                    mm = nc.tensor.matmul(ps[:, 2 + j % 2, 0:256], hidE[:, q, :], w[:, q, :],
                                          start=q == 0, stop=q == FE - 1)
                mm.then_inc(chunk_done, 1)
        each_expert(pe, body)
        pe.wait_ge(ye_zero, 1)
        pe.wait_ge(last_ye, 1)
        scatter_tensor(pe, 0, last_pe)
        pe.wait_ge(last_acc, 1)
        scatter_tensor(pe, 1, last_pe)

    ye_zero, last_ye, last_acc, last_pe = (sem("ye_zero"), sem("last_ye"), sem("last_acc"),
                                           sem("last_scatter"))

    def gathered_scalar(act):
        nc.scalar.activation(xg[:, :, :].rearrange("p (a k) c -> p a (k c)", a=2), ps[:, 4:6, :],
                             ACT.Copy).then_inc(ex_act.sem, 1)

    def expert_scalar(act):
        act.wait_ge(ex_pe.sem, EX0)
        act.wait_ge(ye_zero, 1)
        gathered_scalar(act)

        def body(e, t):
            for j in range(FE):
                act.wait_ge(chunk_done, N_EXP * t + (G_EXP + j + 1 + DONE0))
                act.wait_ge(hid_e, FE * t + (j + 1))
                nc.scalar.activation(sgE[j % 2], ps[:, j % 2, 0:CAP], ACT.Silu
                                     ).then_inc(silu_e, 1)
                if j == 3:
                    act.wait_ge(ex_pe.sem, ex_pe.at("turned", t))
                    nc.scalar.activation(PgT, ps[:, 6, 0:T], ACT.Copy).then_inc(ex_act.sem, 1)
            act.wait_ge(ex_pe.sem, ex_pe.at("gather", t))
            gathered_scalar(act)
            for j in range(4):
                act.wait_ge(chunk_done, N_EXP * t + (G_EXP + FE + j + 1 + DONE0))
                nc.scalar.activation(ye[:, j * 256:j * 256 + 256], ps[:, 2 + j % 2, 0:256],
                                     ACT.Copy).then_inc(chunk_read, 1)
            act.drain().then_inc(ex_act.sem, 1)
        each_expert(act, body)
        act.drain().then_inc(last_ye, 1)

    def select_vector(dve, e):
        for n in range(3):
            nc.vector.tensor_scalar(Psel[:, n, :], cst["iota"], rank[:, n, ds(e, 1)],
                                    sel[:, n, ds(e, 1)], ALU.is_equal, ALU.mult)
        dve.drain()
        for n in range(3):
            last = nc.vector.tensor_scalar(Pgat[:, n, :], Psel[:, n, :], gate[:, n, ds(e, 1)],
                                           None, ALU.mult)
        last.then_inc(ex_dve.sem, 1)

    def accumulate_vector(hf):
        return nc.vector.tensor_tensor(acc[:, 4 * hf:4 * hf + 4, :], acc[:, 4 * hf:4 * hf + 4, :],
                                       ps[:, 4:8, 0:T], ALU.add)

    def expert_vector(dve):
        nc.vector.memset(ye, 0.0)
        nc.vector.memset(PgT, 0.0)
        dve.drain().then_inc(ye_zero, 1)
        select_vector(dve, 0)
        dve.drain().then_inc(hid_e, 2)

        def body(e, t):
            for j in range(FE):
                dve.wait_ge(silu_e, FE * t + (j + 1))
                nc.vector.tensor_tensor(hidE[:, j, :], sgE[j % 2], ps[:, j % 2, CAP:2 * CAP],
                                        ALU.mult).then_inc(chunk_read, 1)
                dve.drain().then_inc(hid_e, 1)
                if j < 2:
                    dve.wait_ge(ex_pe.sem, ex_pe.at("scatterA" if j == 0 else "scatterB", t))
                    accumulate_vector(j).then_inc(ex_dve.sem, 1)
                if j == 3:
                    dve.wait_ge(ex_pe.sem, ex_pe.at("turned", t))
                    select_vector(dve, e + 1)

        def after_round():
            dve.drain()
            nc.vector.tensor_scalar(rank[:, :, :], rank[:, :, :], -float(CAP), None, ALU.add)
            dve.drain()
        each_expert(dve, body, after_round)
        dve.wait_ge(last_pe, 1)
        accumulate_vector(0).then_inc(last_acc, 1)
        dve.wait_ge(last_pe, 2)
        accumulate_vector(1)
        dve.drain()
        for m in range(KT):
            residual_tile(dve, acc[:, m:m + 1, :], 1, G2, m, None)
            dve.drain()
        dve.drain().then_inc(x_ready, 1)

    def load_weights(sp):
        def phase(g0, n, w, c0=0):
            size = w.shape[2]

            def body(c, k, i):
                sp.wait_ge(chunk_done, c + (g0 + 1))
                sp.dma_start(ring[:, slot(g0, k), 0:size],
                             w[ds(c + c0, 1)].rearrange("o p n -> p (o n)")
                             ).then_inc(landed[slot(g0, k)], 16)
            by_four(sp, n, body)
        phase(G_MOD0, N_MOD_A, a["w_mod"])
        phase(G_IN_E, N_IN_E, a["w_in_e"])
        phase(G_MOD1, N_MOD_B, a["w_mod"], N_MOD_A)
        phase(G_OUT_E, N_OUT_E, a["w_out_e"])
        phase(G_GU, N_GU, a["ffn_gu"])
        phase(G_DN, N_DN, a["ffn_down"])
        phase(G_IN_O, N_IN_O, a["w_in_o"])
        phase(G_OUT_O, N_OUT_O, a["w_out_o"])

        def body(e, t):
            for j in range(N_EXP):
                s = expert_slot(j)
                back = [q for q in range(j) if expert_slot(q) == s]
                if back:
                    need = back[-1] + 1
                else:
                    need = max([q for q in range(N_EXP) if expert_slot(q) == s][-1] + 1 - N_EXP,
                               j - RING + 1)
                sp.wait_ge(chunk_done, N_EXP * t + (G_EXP + DONE0 + need))
                if j < FE:
                    src, size = a["exp_gu"][ds(e * FE + j, 1)], 2 * KT * P
                else:
                    src, size = a["exp_down"][ds(e * 4 + (j - FE), 1)], FE * 256
                sp.dma_start(ring[:, s, 0:size], src.rearrange("o p n -> p (o n)")
                             ).then_inc(landed[s], 16)
        each_expert(sp, body)

    CONST_LOADS = [
        (gains[:, :, :], a["gains"]), (bmod[:, :, :], a["b_mod"]), (colsE[:, :], a["colsE"]),
        (attc, a["attc"]), (lamw[:, :, :].rearrange("p a k -> p (a k)"), a["lamv"].partition_broadcast(P)),
        (ptab[:, :], a["page_table"])]
    N_CONST_LOADS = len(CONST_LOADS) + 1

    block = ctx.enter_context(nc.Block())

    @block.sync
    def _(sp):
        sp.dma_start(cT[:, :, :], a["c_t"]).then_inc(inputs_in, 16)
        sp.dma_start(consts[:, :], a["consts"]).then_inc(inputs_in, 16)
        sp.dma_start(xT[:, :, :], a["x_t"]).then_inc(inputs_in, 16)
        load_weights(sp)
        sp.wait_ge(h_ready, 5)
        sp.dma_start(o["y"], hT[:, :, :]).then_inc(stores, 16)
        sp.wait_ge(stores, 16)

    @block.gpsimd
    def _(pool):
        for dst, src in CONST_LOADS:
            pool.dma_start(dst, src).then_inc(consts_in, 16)
        pool.dma_start(shift_in[:, :, :], a["shift"]).then_inc(consts_in, 16)
        pool.wait_ge(proj_ready, 1)
        pool.dma_start(o["k"], projT[:, 4:8, :]).then_inc(kv_stored, 16)
        pool.dma_start(o["v"], projT[:, 8:12, :]).then_inc(kv_stored, 16)
        pool.wait_ge(shift_saved, 1)
        sattn_load(pool)
        pool.dma_start(o["shift"], shift_out[:, :, :]).then_inc(kv_stored, 16)
        rwkv_loads(pool)
        pool.wait_ge(rw_over, 1)
        pool.dma_start(o["wkv"], S9[:, :, :]).then_inc(kv_stored, 16)
        pool.wait_ge(kv_stored, 16 * 4)
        pool.wait_ge(mix_ready, 1)
        split_lo_all(pool, G_GU, S_GU, N_GU, 2 * KT, P)
        split_lo_all(pool, G_DN, S_DN, N_DN, FT, P)
        odd_loads(pool)
        pool.wait_ge(v_ready, 3)
        pool.dma_start(o["cv"], vtk[0:TS, 2, :]).then_inc(kv_stored, 16)
        split_lo_all(pool, G_OUT_O, S_OUT_O, 2, *out_o_kn)
        mixed_pool(pool)
        split_lo_all(pool, G_OUT_O + 2, S_OUT_O + 2, N_OUT_O - 2, *out_o_kn)
        pool.wait_ge(kv_stored, 16 * 5)
        router_loads(pool)

    @block.scalar
    def _(act):
        act.wait_ge(inputs_in, 48)
        nc.scalar.activation(cT[:, :, :], cT[:, :, :], ACT.Silu).then_inc(silu_ready, 1)
        norm0 = norm_scalar
        with act.Fori(0, 2) as u:
            mod_scalar(act, G_MOD0, u, u)
        norm0(act, 0)
        in_e_scalar(act)
        lambda_scalar(act)
        vtok_scalar(act)
        for par in range(2):
            act.drain().then_inc(sa_act[par].sem, 4)
        act.drain().then_inc(pa_act.sem, 4)
        pattn_exp(act, 0)
        with act.Fori(0, 3) as j:
            pattn_scalar(act, j, True)
            mod_scalar(act, G_MOD1, j, j + 2)
        pattn_scalar(act, 3, False)
        mod_scalar(act, G_MOD1, 3, 5)
        sattn_newvalues(act, 0, 0)
        sattn_exp(act, 0, 0)
        with act.Fori(0, NB // 2 - 1) as i:
            sattn_scalar(act, i, True)
            mod_scalar(act, G_MOD1, i + 4, i + 6)
        sattn_scalar(act, NB // 2 - 1, False)
        mod_scalar(act, G_MOD1, NB // 2 + 3, NB // 2 + 5)
        subnorm_scalar(act)
        rwkv_scalar(act)
        gu_split_first(act)
        norm_scalar(act, 1)
        gu_scalar(act)
        split_hi_all(act, G_DN, S_DN, N_DN, FT, P)
        norm_scalar(act, 2)
        in_o_scalar(act)
        split_hi_all(act, G_OUT_O, S_OUT_O, 2, *out_o_kn)
        mixed_scalar(act)
        split_hi_all(act, G_OUT_O + 2, S_OUT_O + 2, N_OUT_O - 2, *out_o_kn)
        norm_scalar(act, 3)
        router_scalar(act)
        expert_scalar(act)
        norm_scalar(act, 4)

    @block.vector
    def _(dve):
        nc.vector.memset(ones[:, :], 1.0).then_inc(ones_ready, 1)
        dve.drain().then_inc(mod_ready, 1)
        dve.drain().then_inc(chunk_read, READ0)
        dve.wait_ge(inputs_in, 48)
        dve.drain().then_inc(x_ready, 1)
        dve.wait_ge(consts_in, 16 * N_CONST_LOADS)
        with dve.Fori(0, 2) as u:
            mod_vector(dve, u)
        split_both(dve, G_IN_E, S_IN_E, 2, KT, 2 * P)
        norm_vector(dve, 0, 0, SC1, SH1, 2)
        split_both(dve, G_IN_E + 2, S_IN_E + 2, N_IN_E - 2, KT, 2 * P)
        lambda_vector(dve)
        shift_vector(dve)
        pattn_queries(dve, 0)
        dve.wait_ge(vtok_act, 1)
        pattn_max(dve, 0)
        with dve.Fori(0, 3) as j:
            pattn_vector(dve, j, True)
            mod_vector(dve, j + 2)
        pattn_vector(dve, 3, False)
        for par in range(2):
            sattn_queries(dve, par, 0)
        mod_vector(dve, 5)
        sattn_max(dve, 0, 0)
        sattn_weights(dve, 0, 0)
        with dve.Fori(0, NB // 2 - 1) as i:
            sattn_vector(dve, i, True)
            mod_vector(dve, i + 6)
        sattn_vector(dve, NB // 2 - 1, False)
        mod_vector(dve, NB // 2 + 5)
        subnorm_vector(dve)
        rwkv_vector(dve)
        residual_vector(dve, G_OUT_E, N_OUT_E, 2, 0, G1)
        norm_vector(dve, 1, 0, SC2, SH2, 12)
        gu_vector(dve)
        residual_vector(dve, G_DN, N_DN, 1, 0, G2)
        norm_vector(dve, 2, 1, SC1, SH1, 12)
        v_norm_vector(dve)
        mixed_vector(dve)
        residual_vector(dve, G_OUT_O, N_OUT_O, 1, 1, G1)
        norm_vector(dve, 3, 1, SC2, SH2, 12)
        router_vector(dve)
        expert_vector(dve)
        norm_vector(dve, 4, None, 0, 0, 12)

    @block.tensor
    def _(pe):
        pe.drain().then_inc(chunk_done, DONE0)
        pe.drain().then_inc(pa_pe.sem, 4)
        for par in range(2):
            pe.drain().then_inc(sa_pe[par].sem, 4)
        pe.wait_ge(ones_ready, 1)
        pe.wait_ge(inputs_in, 48)
        with pe.Fori(0, 2) as u:
            mod_tensor(pe, G_MOD0, u, u)
        norm_tensor(pe, 0)
        columns_split(pe, G_IN_E, S_IN_E, N_IN_E, KT, 2, (hx_hi, hx_lo),
                      lambda e: e.wait_ge(h_ready, 1))
        vtok_tensor(pe)
        pe.wait_ge(vtok_act, 1)
        pattn_scores(pe, 0)
        with pe.Fori(0, 3) as j:
            pattn_tensor(pe, j, True)
            mod_tensor(pe, G_MOD1, j, j + 2)
        pattn_tensor(pe, 3, False)
        mod_tensor(pe, G_MOD1, 3, 5)
        sattn_scores(pe, 0, 0, False)
        with pe.Fori(0, NB // 2 - 1) as i:
            sattn_tensor(pe, i, True)
            mod_tensor(pe, G_MOD1, i + 4, i + 6)
        sattn_tensor(pe, NB // 2 - 1, False)
        mod_tensor(pe, G_MOD1, NB // 2 + 3, NB // 2 + 5)
        subnorm_tensor(pe)
        rwkv_tensor(pe)
        columns_tensor(pe, G_OUT_E, N_OUT_E, KT, 2, mixT, lambda e: (e.wait_ge(mix_ready, 1)))
        norm_tensor(pe, 1)
        gu_tensor(pe)
        columns_split(pe, G_DN, S_DN, N_DN, FT, 1, (hid_hi, hid_lo),
                      lambda e: e.wait_ge(hid_ready, N_GU + 2))
        norm_tensor(pe, 2)
        in_o_tensor(pe)
        mixed_tensor(pe)
        columns_split(pe, G_OUT_O, S_OUT_O, N_OUT_O, EC // P, 1, (um_hi, um_lo),
                      lambda e: e.wait_ge(gated_lo, EC // P), KT * 256)
        norm_tensor(pe, 3)
        router_tensor(pe)
        expert_tensor(pe)
        norm_tensor(pe, 4)


def kernel(**inputs):
    import concourse.bacc as _bacc
    from concourse.bass_utils import run_bass_kernel_spmd as _run

    n = {k: np.asarray(v) for k, v in inputs.items()}

    def tiles(w, cols):
        k, m = w.shape
        return w.reshape(k // P, P, m // cols, cols).transpose(2, 1, 0, 3).reshape(m // cols, P, -1)

    def columns(v):
        return v.reshape(-1, P).T

    x = np.concatenate([n["x_prompt"].reshape(TP, D), n["x_sample"].reshape(TS, D)])
    c = np.concatenate([n["c_prompt"], n["c_sample"], np.zeros((32 - NC_, D), np.float32)])
    k, v = n["cache_k"][0], n["cache_v"][0]
    wo = n["w_in_o"][0]
    ws = n["w_s"][0].transpose(2, 0, 1)
    gu = np.stack([tiles(n["ffn_gate"][0], P), tiles(n["ffn_up"][0], P)], 2)
    eg = np.stack([np.stack([tiles(n[w][0][e], P) for e in range(NE)]) for w in ("exp_gate", "exp_up")], 3)
    given = {
        "x_t": x.reshape(T, KT, P).transpose(2, 1, 0),
        "c_t": c.reshape(32, KT, P).transpose(2, 1, 0),
        "consts": np.concatenate(list(const_columns().values()), 1),
        "attc": attention_constants(),
        "scan_keep": scan_mask(),
        "gains": np.stack([columns(g) for g in (n["norm1_g"][0], n["norm2_g"][0], n["norm1_g"][1],
                                                n["norm2_g"][1], n["final_g"])], 1),
        "b_mod": n["b_mod"].reshape(2, 48, P).transpose(2, 0, 1),
        "colsE": np.concatenate(
            [columns(n["mu_b"][0])] + [columns(n[q].reshape(-1)) for q in
             ("w0", "a0", "k_k", "k_a", "r_k", "lnx_g", "lnx_b")]
            + [np.tile(n["subln_g"][0], 2)[:, None]] + [np.zeros((P, 31), np.float32)], 1),
        "lamv": np.stack([n[q][0] for q in ("lam_q1", "lam_k1", "lam_q2", "lam_k2")]).reshape(-1),
        "page_table": n["page_table"].reshape(1, -1),
        "shift": n["state_shift"][0].reshape(NB, 14, P).transpose(2, 1, 0),
        "s_init": n["state_wkv"][0].reshape(NB, 4, 2, 64, 64).transpose(2, 4, 0, 1, 3).reshape(P, NB, 256),
        "cache_k": k.reshape(N_POOL, PAGE, 4, P).transpose(0, 3, 2, 1).reshape(N_POOL, P, -1),
        "cache_v": v.reshape(N_POOL, PAGE, 512),
        "wa_up": np.concatenate([n["w_up"][0], n["a_up"][0]]),
        "g_up": n["g_up"][0],
        "w_mod": n["w_mod"].reshape(2, 4, 2, P, 6, D).transpose(0, 4, 1, 3, 2, 5).reshape(48, P, -1),
        "w_in_e": tiles(n["w_in_e"][0], 256),
        "w_out_e": tiles(n["w_out_e"][0], 256),
        "ffn_gu": gu.reshape(FT, P, -1),
        "ffn_down": tiles(n["ffn_down"][0], P),
        "w_in_o": tiles(wo, 256),
        "lnv_g": n["lnv_g"][0], "lnv_b": n["lnv_b"][0],
        "b_s": np.concatenate([n["b_s"][0], n["b_s"][0], np.tile(n["b_s"][0][:, :DS], (1, NB))], 1).reshape(-1),
        "w_s": ws,
        "w_s8": np.tile(ws[:DS, :, :DS], (NB, 1, NB)),
        "w_out_o": tiles(n["w_out_o"][0], P),
        "router_w": n["router_w"][0].reshape(KT, P, NE).transpose(1, 0, 2),
        "router_b": n["router_b"][0],
        "exp_gu": eg.reshape(NE * FE, P, -1),
        "exp_down": np.concatenate([tiles(n["exp_down"][0][e], 256) for e in range(NE)]),
    }
    returned = {"y": [P, KT, T], "k": [P, 4, T], "v": [P, 4, T], "shift": [P, 14, NC_],
                "wkv": [P, NC_, 256], "cv": [TS, EC]}
    nc = _bacc.Bacc("TRN2", target_bir_lowering=False, num_devices=1)
    arrays, a, o = {}, {}, {}
    for name, array in given.items():
        array = np.ascontiguousarray(array)
        arrays["in_" + name] = array
        a[name] = nc.dram_tensor("in_" + name, array.shape, mybir.dt.from_np(array.dtype),
                                 kind="ExternalInput").ap()
    for name, shape in returned.items():
        o[name] = nc.dram_tensor("out_" + name, shape, F32, kind="ExternalOutput").ap()
    build(nc, a, o)
    r = _run(nc, [arrays], core_ids=[0]).results[0]
    r = {name: np.asarray(r["out_" + name]) for name in returned}

    def rows(v):
        return v.transpose(2, 1, 0).reshape(v.shape[2], -1)
    y, kn, vn, sh = rows(r["y"]), rows(r["k"]), rows(r["v"]), rows(r["shift"])
    s = r["wkv"].reshape(2, 64, NC_, 4, 64).transpose(2, 3, 0, 4, 1).reshape(NC_, H, 64, 64)
    return (y[:TP].reshape(1, TP, D), y[TP:].reshape(NB, DS, D),
            kn[:TP].reshape(1, 1, TP, H, 2 * DK), vn[:TP].reshape(1, 1, TP, H, DV),
            s[:1][None], sh[:1][None],
            kn[TP:].reshape(1, NB, DS, H, 2 * DK), vn[TP:].reshape(1, NB, DS, H, DV),
            s[1:][None], sh[1:][None], r["cv"].reshape(1, NB, DS, EC))
```

```python
import math
from contextlib import ExitStack

import concourse.bass as bass
import numpy as np
from concourse import mybir

F32 = mybir.dt.float32
F32R = mybir.dt.float32r
I32 = mybir.dt.int32
ALU = mybir.AluOpType
ACT = mybir.ActivationFunctionType
AX = mybir.AxisListType
ds = bass.ds

P = 128
D = 1024
KT = D // P
TP, NB, DS = 256, 8, 8
TS = NB * DS
T = TP + TS
NC_ = 1 + NB
PAST, PAGE = 1024, 128
NPG = PAST // PAGE
N_POOL = 80
H = 8
DK, DV = 32, 64
EC, GC, CHUNK = 2048, 8, 128
DFF, DFE, NE = 2816, 1408, 8
FT, FE = DFF // P, DFE // P
RING = 4
SLOT = 22 * P
CAP = 128
LAM_INIT = 0.8 - 0.6 * math.exp(0.0)
KAPPA = math.exp(-0.5)
SCALE = DK ** -0.5
RMS_EPS, LN_EPS, LNX_EPS = 1e-6, 1e-5, 64e-5
RC = 32
SH1, SC1, G1, SH2, SC2, G2 = (KT * i for i in range(6))

N_MOD_A, N_MOD_B = 2 * 4, 10 * 4
N_MOD_ATTN = 5 * 4
N_IN_E, N_OUT_E, N_GU, N_DN = 13, 4, FT, 8
N_IN_O, N_OUT_O, N_EXP = 16, 8, FE + 4
G_MOD0 = 0
G_IN_E = G_MOD0 + N_MOD_A
G_MOD1 = G_IN_E + N_IN_E
G_OUT_E = G_MOD1 + N_MOD_B
G_GU = G_OUT_E + N_OUT_E
G_DN = G_GU + N_GU
G_IN_O = G_DN + N_DN
G_OUT_O = G_IN_O + N_IN_O
G_EXP = G_OUT_O + N_OUT_O
DONE0 = RING
READ0 = 2
S_IN_E = 0
S_GU = S_IN_E + N_IN_E
S_DN = S_GU + N_GU
S_IN_O = S_DN + N_DN
S_OUT_O = S_IN_O + N_IN_O
S_EXP = S_OUT_O + N_OUT_O
N_ED = 4


class Steps:

    def __init__(self, sem, names, base=0):
        self.sem, self.names, self.base = sem, names, base

    def at(self, name, turn=0):
        return turn * len(self.names) + (self.base + self.names.index(name) + 1)


def by_four(eng, n, body):
    full = n // RING
    if full > 1:
        with eng.Fori(0, full) as i:
            for k in range(RING):
                body(i * RING + k, k, i)
    elif full:
        for k in range(RING):
            body(k, k, 0)
    for k in range(n % RING):
        body(full * RING + k, k, full)


def const_columns():
    p = np.arange(P)[:, None]
    f = np.arange(P)[None, :]
    c = {}
    c["ident"] = (p == f)
    c["block64"] = (p // 64 == f // 64)
    c["low16"] = (f < p) & (f // 16 == p // 16)
    c["up16"] = (p < f) & (f // 16 == p // 16)
    c["up32off"] = (p < f) & (f // 32 == p // 32) & (f // 16 != p // 16)
    c["up32"] = (p < f) & (f // 32 == p // 32)
    c["up32incl"] = (p <= f) & (f // 32 == p // 32)
    c["up"] = (p < f)
    c["upincl"] = (p <= f)
    c["upincl8"] = (p <= f) & (p // DS == f // DS)
    c["iota"] = f + 0 * p
    c["halfsum"] = (f[:, 0:32] == p // 64)
    c["halfcast"] = (f // 64 == p % 32)
    e = np.arange(64)[None, :]
    c["lower_e"] = (e % 8 < e // 8) & (p >= 0)
    c["slope"] = np.exp2(-8.0 * np.arange(1, H + 1) / H)[None, :] + 0 * p
    c["rowmask"] = (p // 32 == np.arange(4)[None, :])
    c["map0"] = ((p // DS) % 2 == 0)
    c["map1"] = ((p // DS) % 2 == 1)
    c["valid"] = np.stack([np.ones(P), np.ones(P), np.arange(P) < TS], 1)
    hq = (p // 16) * DS + p % DS
    c["pairsum"] = (hq == np.arange(64)[None, :])
    c["sumheads"] = (p % DS == np.arange(DS)[None, :])
    return {k: np.ascontiguousarray(v.astype(np.float32)) for k, v in c.items()}


def attention_constants():
    q = np.arange(P)[:, None]
    k = np.arange(TP)[None, :]
    dist = np.stack([np.where(k <= q + P * b, k - (q + P * b), -1e30) for b in range(2)], 1)
    r = np.arange(P)
    head, qs = r // 16, r % DS
    slope = np.exp2(-8.0 * (head + 1) / H)[:, None]
    pos = np.arange(PAST + DS)[None, :]
    qp = (PAST + qs)[:, None]
    bias = np.where(pos <= qp, -slope * np.abs(qp - pos), -1e30)
    rows = np.arange(P) % 64
    own = (rows[:, None] // DS == np.arange(512)[None, :] // DV)
    return np.concatenate([dist.reshape(P, -1), bias, own], 1).astype(np.float32)


def scan_mask():
    t = np.arange(T)
    keep = np.where(t < TP, t % RC != 0, (t - TP) % DS != 0)
    return np.ascontiguousarray(np.broadcast_to(np.tile(keep, 4), (P, 4 * T)).astype(np.float32))


def build(nc, a, o):
    ctx = ExitStack()
    with ctx:
        program(nc, ctx, a, o)


def program(nc, ctx, a, o):
    def sb(name, shape, dt=F32):
        return ctx.enter_context(nc.sbuf_tensor(name, shape, dt))

    def sem(name):
        return ctx.enter_context(nc.semaphore(name))

    ring = sb("ring", [P, RING, SLOT])
    xT = sb("xT", [P, KT, T])
    hT = sb("hT", [P, KT, T])
    modT = sb("modT", [P, 2, 48, NC_])
    bmod = sb("bmod", [P, 2, 48])
    gains = sb("gains", [P, 5, KT])
    const_cols = const_columns()
    n_const = sum(v.shape[1] for v in const_cols.values())
    consts = sb("consts", [P, n_const])
    cst, at = {}, 0
    for name, v in const_cols.items():
        cst[name] = consts[:, at:at + v.shape[1]]
        at += v.shape[1]
    ones = sb("ones", [P, P])
    cT = sb("cT", [P, KT, 32])
    gsc = sb("gsc", [P, KT, NC_])
    rstd = sb("rstd", [P, T])
    ptab = sb("ptab", [1, NB * NPG], I32)
    small = sb("small", [P, 64])
    colsE = sb("colsE", [P, 74])
    modrow = sb("modrow", [P, 2 * P])
    gtmp = sb("gtmp", [P, TS])
    lamw = sb("lamw", [P, 4, DK])
    shift_out = sb("shift_out", [P, 14, NC_])
    rounds_i = sb("rounds_i", [P, 2], I32)
    n_arena = nc.sbuf_bytes_remaining // 4 - 8
    with nc.sbuf_tensor("arena", [P, n_arena], F32) as arena:
        pass

    def split_tensor(name, at, *shape):
        assert at + int(np.prod(shape)) <= n_arena
        with ExitStack() as place:
            if at:
                place.enter_context(nc.sbuf_tensor(f"below_{name}", [P, at], F32))
            return place.enter_context(nc.sbuf_tensor(name, [P, *shape], F32R))

    hid_hi, hid_lo = (split_tensor(n, x * FT * T, FT, T) for x, n in enumerate(("hid_hi", "hid_lo")))
    at_split = 2 * FT * T
    wsplit = split_tensor("wsplit", at_split, 4 * SLOT)
    at_um = at_split + 4 * KT * 256
    at_sgate = at_split + 4 * SLOT
    at_hx = at_um + 2 * EC
    assert at_hx >= at_sgate + 2 * T
    hx_hi, hx_lo = (split_tensor(n, at_hx + x * KT * T, KT, T) for x, n in enumerate(("hx_hi", "hx_lo")))
    shift_in = arena[:, at_sgate:at_sgate + 14 * NB].rearrange("p (m b) -> p m b", b=NB)
    at_htmp = at_hx + 2 * KT * T
    um_hi, um_lo = (split_tensor(n, at_um + x * (EC // P) * T, EC // P, T)
                    for x, n in enumerate(("um_hi", "um_lo")))
    ps = ctx.enter_context(nc.psum_tensor("ps", [P, 8, 512], F32))

    class Area:

        def __init__(self, at=0):
            self.at = at

        def take(self, *shape):
            n = int(np.prod(shape))
            v = arena[:, self.at:self.at + n]
            self.at += n
            assert self.at <= n_arena, (self.at, n_arena)
            if len(shape) == 2:
                v = v.rearrange("p (a b) -> p a b", b=shape[1])
            elif len(shape) == 3:
                v = v.rearrange("p (a b c) -> p a b c", b=shape[1], c=shape[2])
            return v

    ident, block64 = cst["ident"], cst["block64"]
    mu, w0c, a0c, kkc, kac, rkc, lgc, lbc, sgc, lamv = (
        colsE[:, 0:14], colsE[:, 14:18], colsE[:, 18:22], colsE[:, 22:26], colsE[:, 26:30],
        colsE[:, 30:34], colsE[:, 34:38], colsE[:, 38:42], colsE[:, 42:43], colsE[:, 43:44])

    landed = [sem(f"weights_landed{s}") for s in range(RING)]
    chunk_done, chunk_read = sem("chunk_done"), sem("chunk_read")
    inputs_in, consts_in = sem("inputs_in"), sem("consts_in")
    attn_consts_in = sem("attention_constants_in")
    stores = sem("stores")

    def slot(g0, k):
        return (g0 + k) % RING

    def use(g0, k, i):
        return i + (g0 + k) // RING

    def wait_weights(eng, g0, k, i):
        eng.wait_ge(landed[slot(g0, k)], 16 * (use(g0, k, i) + 1))

    def wait_psum(eng, g0, c):
        eng.wait_ge(chunk_read, c + (g0 + 1))

    def wait_done(eng, g0, c):
        eng.wait_ge(chunk_done, c + (g0 + 1 + DONE0))

    def pbank(g0, k):
        return 2 * ((g0 + k) % 2)

    def slot_view(g0, k, kt, n):
        return ring[:, slot(g0, k), 0:kt * n].rearrange("p (k n) -> p k n", n=n)

    hi_ready, lo_ready = sem("weights_hi"), sem("weights_lo")

    def parts(s0, k, kt, n, stride=SLOT):
        at = ((s0 + k) % 2) * stride
        return [wsplit[:, x + at:x + at + kt * n].rearrange("p (k n) -> p k n", n=n)
                for x in (0, 2 * stride)]

    def split_hi(eng, copy, g0, s0, c, k, i, kt, n, stride=SLOT):
        wait_weights(eng, g0, k, i)
        eng.wait_ge(chunk_done, c + (g0 - 1 + DONE0))
        copy(parts(s0, k, kt, n, stride)[0], slot_view(g0, k, kt, n)).then_inc(hi_ready, 1)

    def split_lo(eng, g0, s0, c, k, i, kt, n, stride=SLOT):
        eng.wait_ge(hi_ready, c + (s0 + 1))
        hi, lo = parts(s0, k, kt, n, stride)
        eng.tensor_tensor(lo, slot_view(g0, k, kt, n), hi.bitcast(F32), ALU.subtract
                          ).then_inc(lo_ready, 1)

    def split_both(dve, g0, s0, n_chunks, kt, n, stride=SLOT):
        def body(c, k, i):
            split_hi(dve, nc.vector.tensor_copy, g0, s0, c, k, i, kt, n, stride)
            split_lo(dve, g0, s0, c, k, i, kt, n, stride)
        by_four(dve, n_chunks, body)

    def act_copy(out, in_):
        return nc.scalar.activation(out, in_, ACT.Copy)

    def split_hi_all(act, g0, s0, n_chunks, kt, n, stride=SLOT):
        by_four(act, n_chunks, lambda c, k, i: split_hi(act, act_copy, g0, s0, c, k, i, kt, n, stride))

    def split_lo_all(pool, g0, s0, n_chunks, kt, n, stride=SLOT):
        by_four(pool, n_chunks, lambda c, k, i: split_lo(pool, g0, s0, c, k, i, kt, n, stride))

    def three_passes(out, w, x, first, last):
        for p, (u, v) in enumerate(((w[0], x[0]), (w[0], x[1]), (w[1], x[0]))):
            mm = nc.tensor.matmul(out, u, v, start=first and p == 0, stop=last and p == 2)
        return mm

    silu_ready, modrow_ready, mod_turned, mod_ready = (
        sem("silu_ready"), sem("modrow_ready"), sem("mod_turned"), sem("mod_ready"))

    def mod_tensor(pe, g0, u, unit):
        pe.wait_ge(silu_ready, 1)
        pe.wait_ge(mod_ready, unit + 1)
        for k in range(4):
            wait_weights(pe, g0, k, u)
            if k == 0:
                pe.wait_ge(chunk_read, RING * u + (g0 + READ0))
            w = slot_view(g0, k, 2, D)
            for q in range(2):
                for c in range(4):
                    mm = nc.tensor.matmul(ps[32 * c:32 * c + 32, 5, 0:2 * P], cT[:, 2 * k + q, :],
                                          w[:, q, 256 * c:256 * c + 256],
                                          start=k + q == 0, stop=k + q == 4)
            mm.then_inc(chunk_done, 1)
        pe.wait_ge(modrow_ready, unit + 1)
        for hh in range(2):
            mm = nc.tensor.transpose(ps[:, 5, (2 + hh) * P:(3 + hh) * P], modrow[:, hh * P:hh * P + P], ident)
        mm.then_inc(mod_turned, 1)

    def mod_scalar(act, g0, u, unit):
        act.wait_ge(chunk_done, RING * u + (g0 + RING + DONE0))
        act.wait_ge(mod_ready, unit + 1)
        nc.scalar.activation(modrow[:, :], ps[:, 5, 0:2 * P], ACT.Copy).then_inc(chunk_read, 4)
        act.drain().then_inc(modrow_ready, 1)

    def mod_vector(dve, unit):
        dve.wait_ge(mod_turned, unit + 1)
        flat = modT[:, :, :, :].rearrange("p l m c -> p (l m) c")
        fb = bmod[:, :, :].rearrange("p l m -> p (l m)")
        for hh in range(2):
            for c in range(4):
                m = 8 * unit + (hh + 2 * c)
                last = nc.vector.tensor_scalar(
                    flat[:, ds(m, 1), :], ps[:, 5:6, (2 + hh) * P + 32 * c:(2 + hh) * P + 32 * c + NC_],
                    fb[:, ds(m, 1)], None, ALU.add)
        last.then_inc(mod_ready, 1)

    area0 = Area(n_arena - KT * T)
    sq = area0.take(KT, T)
    sq_ready, ssum_ready, var_ready, root_ready, h_ready, x_ready = (
        sem("sq_ready"), sem("ssum_ready"), sem("var_ready"), sem("root_ready"), sem("h_ready"),
        sem("x_ready"))

    def norm_scalar(act, n):
        act.wait_ge(x_ready, n + 1)
        if n:
            act.wait_ge(ssum_ready, n)
        nc.scalar.activation(sq[:, :, :], xT[:, :, :], ACT.Square).then_inc(sq_ready, 1)
        act.wait_ge(var_ready, n + 1)
        nc.scalar.activation(rstd[:, :], rstd[:, :], ACT.Sqrt).then_inc(root_ready, 1)

    h_half, h_high = sem("h_half"), sem("h_high_part")

    def norm_tensor(pe, n):
        pe.wait_ge(sq_ready, n + 1)
        for kt in range(KT):
            mm = nc.tensor.matmul(ps[:, 7, 0:T], ones[:, :], sq[:, kt, :], start=kt == 0,
                                  stop=kt == KT - 1)
        mm.then_inc(ssum_ready, 1)

    def norm_gain(dve, n, layer, sc, mod_count):
        dve.wait_ge(mod_ready, mod_count + 1)
        dve.drain()
        nc.vector.scalar_tensor_tensor(
            gsc[:, :, :], modT[:, layer, sc:sc + KT, :], 1.0,
            gains[:, n, :].unsqueeze(2).to_broadcast([P, KT, NC_]), ALU.add, ALU.mult)

    def norm_scale(dve, n, gain=None):
        dve.wait_ge(ssum_ready, n + 1)
        nc.vector.tensor_scalar(rstd[:, :], ps[:, 7, 0:T], 1.0 / D, RMS_EPS, ALU.mult,
                                ALU.add).then_inc(var_ready, 1)
        if gain is not None:
            gain()
        dve.wait_ge(root_ready, n + 1)
        nc.vector.reciprocal(rstd[:, :], rstd[:, :])
        dve.drain()
        nc.vector.tensor_tensor(hT[:, :, :], xT[:, :, :],
                                rstd[:, :].unsqueeze(1).to_broadcast([P, KT, T]), ALU.mult)
        dve.drain()

    def norm_vector(dve, n, layer, sc, sh, mod_count):
        norm_scale(dve, n, None if layer is None else lambda: norm_gain(dve, n, layer, sc, mod_count))
        norm_shift(dve, n, layer, sh)

    def norm_shift(dve, n, layer, sh):
        if layer is None:
            for kt in range(KT):
                last = nc.vector.tensor_scalar(hT[:, kt, :], hT[:, kt, :], gains[:, n, kt:kt + 1],
                                               None, ALU.mult)
            last.then_inc(h_ready, 1)
            return
        for half in range(2):
            k4 = slice(4 * half, 4 * half + 4)
            for kt in range(4 * half, 4 * half + 4):
                nc.vector.tensor_scalar(hT[:, kt, 0:TP], hT[:, kt, 0:TP], gsc[:, kt, 0:1],
                                        modT[:, layer, sh + kt, 0:1], ALU.mult, ALU.add)
            hs = hT[:, k4, TP:T].rearrange("p k (b s) -> p k b s", s=DS)
            full = [P, 4, NB, DS]
            nc.vector.tensor_tensor(hs, hs, gsc[:, k4, 1:NC_].unsqueeze(3).to_broadcast(full),
                                    ALU.mult)
            dve.drain()
            last = nc.vector.tensor_tensor(
                hs, hs, modT[:, layer, sh + 4 * half:sh + 4 * half + 4, 1:NC_].unsqueeze(3)
                .to_broadcast(full), ALU.add)
            if n < 3:
                dve.drain().then_inc(h_half, 1)
        if n < 3:
            for half in range(2):
                k4 = slice(4 * half, 4 * half + 4)
                dve.wait_ge(h_high, 2 * n + half + 1)
                last = nc.vector.tensor_tensor(hx_lo[:, k4, :], hT[:, k4, :],
                                               hx_hi[:, k4, :].bitcast(F32), ALU.subtract)
        last.then_inc(h_ready, 1)

    def norm_split(act, n):
        for half in range(2):
            k4 = slice(4 * half, 4 * half + 4)
            act.wait_ge(h_half, 2 * n + half + 1)
            act_copy(hx_hi[:, k4, :], hT[:, k4, :]).then_inc(h_high, 1)


    def residual_tile(dve, src, layer, gate, m, inc):
        flat = modT[:, :, :, :].rearrange("p l m c -> p (l m) c")
        row = flat[:, ds(m + (layer * 48 + gate), 1), :]
        x = xT[:, ds(m, 1), :]
        nc.vector.scalar_tensor_tensor(x[:, :, 0:TP], src[:, :, 0:TP], row[:, 0, 0:1],
                                       x[:, :, 0:TP], ALU.mult, ALU.add)
        g = row[:, 0, 1:NC_].unsqueeze(2).to_broadcast([P, NB, DS])
        t3 = gtmp[:, :].rearrange("p (b s) -> p b s", s=DS)
        dve.drain()
        nc.vector.tensor_tensor(t3, src[:, 0, TP:T].rearrange("p (b s) -> p b s", s=DS), g,
                                ALU.mult)
        dve.drain()
        ins = nc.vector.tensor_tensor(x[:, 0, TP:T], x[:, 0, TP:T], gtmp[:, :], ALU.add)
        if inc is not None:
            ins.then_inc(inc, 1)

    def columns_tensor(pe, g0, n, kt, tiles, rhs, first_wait):
        first_wait(pe)

        def body(c, k, i):
            wait_weights(pe, g0, k, i)
            wait_psum(pe, g0, c)
            w = slot_view(g0, k, kt, tiles * P)
            for t in range(tiles):
                for q in range(kt):
                    mm = nc.tensor.matmul(ps[:, pbank(g0, k) + t, 0:T], w[:, q, t * P:t * P + P],
                                          rhs[:, q, :], start=q == 0, stop=q == kt - 1)
            mm.then_inc(chunk_done, 1)
        by_four(pe, n, body)

    def columns_split(pe, g0, s0, n, kt, tiles, x, first_wait, stride=SLOT):
        first_wait(pe)

        def body(c, k, i):
            pe.wait_ge(lo_ready, c + (s0 + 1))
            wait_psum(pe, g0, c)
            w = parts(s0, k, kt, tiles * P, stride)
            for t in range(tiles):
                for q in range(kt):
                    mm = three_passes(ps[:, pbank(g0, k) + t, 0:T],
                                      [v[:, q, t * P:t * P + P] for v in w],
                                      [v[:, q, :] for v in x], q == 0, q == kt - 1)
            mm.then_inc(chunk_done, 1)
        by_four(pe, n, body)

    def residual_vector(dve, g0, n, tiles, layer, gate):
        def body(c, k, i):
            dve.drain()
            wait_done(dve, g0, c)
            for t in range(tiles):
                if t:
                    dve.drain()
                residual_tile(dve, ps[:, pbank(g0, k) + t:pbank(g0, k) + t + 1, :], layer, gate,
                              c * tiles + t, chunk_read if t == tiles - 1 else None)
        by_four(dve, n, body)
        dve.drain().then_inc(x_ready, 1)

    aA = Area(0)
    projT = aA.take(26, T)
    xb = projT[:, 12:26, :]
    base_b = aA.at
    proj_ready = sem("proj_ready")
    mixT = hT

    def in_e_scalar(act):
        def body(c, k, i):
            wait_done(act, G_IN_E, c)
            nc.scalar.activation(projT[:, ds(2 * c, 2), :],
                                 ps[:, pbank(G_IN_E, k):pbank(G_IN_E, k) + 2, 0:T],
                                 ACT.Copy).then_inc(chunk_read, 1)
        by_four(act, N_IN_E, body)
        act.drain().then_inc(proj_ready, 1)

    aB = Area(base_b)
    attc = aB.take(2 * TP + PAST + DS + 512)
    dist = attc[:, 0:2 * TP].rearrange("p (b k) -> p b k", b=2)
    biasS = attc[:, 2 * TP:2 * TP + PAST + DS]
    ownhead = attc[:, 2 * TP + PAST + DS:]
    Kp, Vp = [], []
    for _ in range(2):
        kv_at = aB.at
        Kp.append(aB.take(NPG, 4, P))
        Vp.append(aB.take(NPG, 512))
    Kp_pages = [v.rearrange("p g j n -> p g (j n)") for v in Kp]
    sS = [aB.take(PAST + DS) for _ in range(2)]
    Qs = [aB.take(4, 32) for _ in range(2)]
    kvn = [aB.take(8, DS) for _ in range(2)]
    vn = [aB.take(512) for _ in range(2)]
    Cm = [aB.take(64) for _ in range(2)]
    prTs = [aB.take(NPG, 64) for _ in range(2)]
    prn = [aB.take(64) for _ in range(2)]
    om = [sS[par][:, 0:512] for par in range(2)]
    aP = Area(kv_at)
    Vtok = aP.take(2, 512)
    Qm = aP.take(4, TP)
    Vst = aP.take(2, P)
    sP = [aP.take(4, TP) for _ in range(2)]
    prP = [aP.take(2, TP) for _ in range(2)]
    prPT = [aP.take(4, P) for _ in range(2)]
    lam = small[:, 0:1]
    nmaxP, lP = small[:, 2:10], small[:, 10:18]
    nmaxS, lS = small[:, 18:20], small[:, 20:22]
    coef = small[:, 22:23]
    lamt = small[:, 24:28]

    vtok_pe, vtok_act = sem("vtok_turned"), sem("vtok_ready")
    lam_d, lam_a, lam_ready = sem("lam_dots"), sem("lam_exps"), sem("lam_ready")
    pa_scored = sem("pattn_scored")
    pa_queries = sem("pattn_queries")
    pa_pe = Steps(sem("pattn_pe"), ["prT0", "prT1", "o0", "o1"], 4)
    pa_dve = Steps(sem("pattn_dve"), ["pr0", "pr1", "values"])
    pa_max, pa_exp = sem("pattn_max"), sem("pattn_exp")
    pa_act = Steps(sem("pattn_act"), ["prTs0", "prTs1", "os0", "os1"], 4)

    def lambda_vector(dve):
        dve.wait_ge(consts_in, 16 * N_CONST_LOADS)
        nc.vector.tensor_tensor(lamw[:, 0:4:2, :], lamw[:, 0:4:2, :], lamw[:, 1:4:2, :], ALU.mult)
        dve.drain()
        nc.vector.tensor_reduce(lamt[:, 0:2], lamw[:, 0:4:2, :], AX.X, ALU.add).then_inc(lam_d, 1)
        dve.wait_ge(lam_a, 1)
        nc.vector.tensor_tensor(lam, lamt[:, 2:3], lamt[:, 3:4], ALU.subtract)
        dve.drain()
        nc.vector.tensor_scalar(lam, lam, LAM_INIT, None, ALU.add)
        dve.drain()
        nc.vector.tensor_scalar(coef, cst["map1"], lam, -1.0, ALU.mult, ALU.mult)
        dve.drain()
        nc.vector.tensor_tensor(coef, coef, cst["map0"], ALU.add).then_inc(lam_ready, 1)

    def lambda_scalar(act):
        act.wait_ge(lam_d, 1)
        nc.scalar.activation(lamt[:, 2:4], lamt[:, 0:2], ACT.Exp).then_inc(lam_a, 1)

    def vtok_tensor(pe):
        pe.wait_ge(proj_ready, 1)
        for n in range(2):
            for j in range(4):
                mm = nc.tensor.transpose(ps[:, n, j * P:j * P + P], projT[:, 8 + j, n * P:n * P + P],
                                         ident)
        mm.then_inc(vtok_pe, 1)

    def vtok_scalar(act):
        act.wait_ge(vtok_pe, 1)
        nc.scalar.activation(Vtok[:, :, :], ps[:, 0:2, :], ACT.Copy).then_inc(vtok_act, 1)

    def pattn_scores(pe, j):
        pe.wait_ge(pa_queries, j + 1)
        for b in range(2):
            for i in range(4):
                mm = nc.tensor.matmul(ps[:, 2 * b + i // 2, (i % 2) * TP:(i % 2) * TP + TP],
                                      Qm[:, i, b * P:b * P + P], projT[:, ds(j + 4, 1), 0:TP],
                                      start=True, stop=True)
            mm.then_inc(pa_scored, 1)

    def pattn_tensor(pe, j, more):
        pe.wait_ge(pa_act.sem, pa_act.at("os1", j) - 4)
        for b in range(2):
            pe.wait_ge(pa_dve.sem, pa_dve.at(f"pr{b}", j))
            for h2 in range(2):
                for kt in range(2):
                    mm = nc.tensor.transpose(ps[:, 4 + 3 * b, (2 * h2 + kt) * P:(2 * h2 + kt + 1) * P],
                                             prP[b][:, h2, kt * P:kt * P + P], ident)
            mm.then_inc(pa_pe.sem, 1)
        if more:
            pattn_scores(pe, j + 1)
        pe.wait_ge(pa_dve.sem, pa_dve.at("values", j))
        for b in range(2):
            pe.wait_ge(pa_act.sem, pa_act.at(f"prTs{b}", j))
            for h2 in range(2):
                for kt in range(b + 1):
                    mm = nc.tensor.matmul(ps[64 * h2:64 * h2 + 64, 4 + 3 * b, 0:P],
                                          Vst[:, kt, 64 * h2:64 * h2 + 64],
                                          prPT[b][:, 2 * h2 + kt, :], start=kt == 0, stop=kt == b)
            mm.then_inc(pa_pe.sem, 1)

    def pattn_queries(dve, j):
        for i in range(4):
            last = nc.vector.tensor_scalar(Qm[:, i:i + 1, :], projT[:, ds(j, 1), 0:TP],
                                           cst["rowmask"][:, i:i + 1], SCALE, ALU.mult, ALU.mult)
        last.then_inc(pa_queries, 1)

    def pattn_max(dve, j):
        for b in range(2):
            dve.wait_ge(pa_scored, 2 * j + (b + 1))
            for h2 in range(2):
                nc.vector.scalar_tensor_tensor(
                    sP[b][:, 2 * h2:2 * h2 + 2, :], dist[:, b, :].unsqueeze(1).to_broadcast([P, 2, TP]),
                    cst["slope"][:, ds(2 * j + h2, 1)],
                    ps[:, 2 * b + h2, :].rearrange("p (m k) -> p m k", m=2), ALU.mult, ALU.add)
            dve.drain()
            nc.vector.tensor_reduce(nmaxP[:, 4 * b:4 * b + 4], sP[b][:, :, :], AX.X, ALU.max)
            dve.drain()
            nc.vector.tensor_scalar(nmaxP[:, 4 * b:4 * b + 4], nmaxP[:, 4 * b:4 * b + 4], -1.0,
                                    None, ALU.mult).then_inc(pa_max, 1)

    def pattn_vector(dve, j, more):
        if more:
            dve.wait_ge(pa_scored, 2 * j + 2)
            pattn_queries(dve, j + 1)
        for b in range(2):
            dve.wait_ge(pa_exp, 2 * j + (b + 1))
            l = lP[:, 4 * b:4 * b + 4]
            nc.vector.reciprocal(l, l)
            dve.drain()
            nc.vector.tensor_scalar(l[:, 1:4:2], l[:, 1:4:2], lam, None, ALU.mult)
            dve.drain()
            for h2 in range(2):
                nc.vector.tensor_scalar(sP[b][:, 2 * h2 + 1, :], sP[b][:, 2 * h2 + 1, :],
                                        l[:, 2 * h2 + 1:2 * h2 + 2], None, ALU.mult)
            dve.drain()
            for h2 in range(2):
                last = nc.vector.scalar_tensor_tensor(
                    prP[b][:, h2, :], sP[b][:, 2 * h2, :], l[:, 2 * h2:2 * h2 + 1],
                    sP[b][:, 2 * h2 + 1, :], ALU.mult, ALU.subtract)
            last.then_inc(pa_dve.sem, 1)
        dve.wait_ge(pa_pe.sem, pa_pe.at("o1", j) - 4)
        nc.vector.tensor_copy(Vst[:, :, :], Vtok[:, :, ds(j * P, P)]).then_inc(pa_dve.sem, 1)
        if more:
            pattn_max(dve, j + 1)

    def pattn_exp(act, j):
        for b in range(2):
            act.wait_ge(pa_max, 2 * j + (b + 1))
            for i in range(4):
                last = nc.scalar.activation(sP[b][:, i, :], sP[b][:, i, :], ACT.Exp,
                                            bias=nmaxP[:, 4 * b + i:4 * b + i + 1],
                                            accum_out=lP[:, 4 * b + i:4 * b + i + 1])
            last.then_inc(pa_exp, 1)

    def pattn_scalar(act, j, more):
        for b in range(2):
            act.wait_ge(pa_pe.sem, pa_pe.at(f"prT{b}", j))
            nc.scalar.activation(prPT[b][:, :, :].rearrange("p a k -> p (a k)"),
                                 ps[:, 4 + 3 * b, :], ACT.Copy).then_inc(pa_act.sem, 1)
        for b in range(2):
            act.wait_ge(pa_pe.sem, pa_pe.at(f"o{b}", j))
            nc.scalar.activation(mixT[:, ds(j, 1), b * P:b * P + P],
                                 ps[:, 4 + 3 * b:5 + 3 * b, 0:P], ACT.Copy).then_inc(pa_act.sem, 1)
        if more:
            pattn_exp(act, j + 1)

    k_landed = [sem(f"k_pages{i}") for i in range(2)]
    v_landed = [sem(f"v_pages{i}") for i in range(2)]
    sa_queries = [sem(f"sattn_queries{i}") for i in range(2)]
    sa_dve = [Steps(sem(f"sattn_dve{i}"), ["smax", "cm", "om"]) for i in range(2)]
    sa_pe = [Steps(sem(f"sattn_pe{i}"), ["S", "PT", "O", "F"], 4) for i in range(2)]
    sa_act = [Steps(sem(f"sattn_act{i}"), ["vn", "exp", "pT", "ms"], 4) for i in range(2)]

    def sattn_pages(eng, pages, place, step, done, par, i):
        for g in range(NPG):
            page = eng.value_load(ptab[0:1, ds(i * (2 * NPG) + (par * NPG + g), 1)],
                                  min_val=0, max_val=N_POOL - 1)
            if g == 0:
                eng.wait_ge(sa_pe[par].sem, sa_pe[par].at(step, i) - 4)
            eng.dma_start(place[par][:, g], pages[ds(page, 1)].rearrange("o p n -> p (o n)")
                          ).then_inc(done[par], 16)

    def sattn_keys(sp, par, i):
        sattn_pages(sp, a["cache_k"], Kp_pages, "S", k_landed, par, i)

    def first_keys(sp):
        sp.wait_ge(consts_in, 16 * N_CONST_LOADS)
        sp.wait_ge(shift_done, 1)
        sattn_keys(sp, 0, 0)

    def other_keys(sp):
        sp.wait_ge(pa_pe.sem, pa_pe.at("o1", 3))
        sattn_keys(sp, 1, 0)
        with sp.Fori(1, NB // 2) as i:
            for par in range(2):
                sattn_keys(sp, par, i)

    def values_load(pool):
        pool.wait_ge(consts_in, 16 * N_CONST_LOADS)
        pool.wait_ge(shift_done, 1)
        with pool.Fori(0, NB // 2) as i:
            for par in range(2):
                if par == 1:
                    pool.wait_ge(pa_pe.sem, pa_pe.at("o1", 3))
                sattn_pages(pool, a["cache_v"], Vp, "O", v_landed, par, i)

    def sattn_queries(dve, par, i):
        tok = i * (2 * DS) + (TP + par * DS)
        dve.wait_ge(sa_pe[par].sem, sa_pe[par].at("S", i) - 4)
        for r in range(4):
            nc.vector.tensor_scalar(Qs[par][:, :, 8 * r:8 * r + 8], projT[:, 0:4, ds(tok, DS)],
                                    cst["rowmask"][:, r:r + 1], SCALE, ALU.mult, ALU.mult)
        nc.vector.tensor_copy(kvn[par][:, :, :], projT[:, 4:12, ds(tok, DS)]
                              ).then_inc(sa_queries[par], 1)

    def sattn_max(dve, par, i):
        dve.wait_ge(sa_pe[par].sem, sa_pe[par].at("S", i))
        s = sS[par]
        nc.vector.tensor_tensor(s[:, 0:PAST].rearrange("p (h k) -> p h k", h=2),
                                ps[:, 2 * par:2 * par + 2, :],
                                biasS[:, 0:PAST].rearrange("p (h k) -> p h k", h=2), ALU.add)
        nc.vector.tensor_tensor(s[:, PAST:PAST + DS], ps[:, 4, DS * par:DS * par + DS],
                                biasS[:, PAST:PAST + DS], ALU.add)
        dve.drain()
        nm = nmaxS[:, par:par + 1]
        nc.vector.tensor_reduce(nm, s, AX.X, ALU.max)
        dve.drain()
        nc.vector.tensor_scalar(nm, nm, -1.0, None, ALU.mult).then_inc(sa_dve[par].sem, 1)

    def sattn_weights(dve, par, i):
        dve.wait_ge(sa_act[par].sem, sa_act[par].at("exp", i))
        l = lS[:, par:par + 1]
        nc.vector.reciprocal(l, l)
        dve.drain()
        nc.vector.tensor_scalar(Cm[par], cst["pairsum"], l, coef, ALU.mult,
                                ALU.mult).then_inc(sa_dve[par].sem, 1)

    def sattn_vector(dve, i, more):
        for par in range(2):
            nxt = par == 0 or more
            if nxt:
                sattn_max(dve, 1 - par, i + par)
            if more:
                sattn_queries(dve, par, i + 1)
            if nxt:
                sattn_weights(dve, 1 - par, i + par)
            dve.wait_ge(sa_pe[par].sem, sa_pe[par].at("O", i))
            nc.vector.tensor_tensor(om[par], ps[:, 6 + par, :], ownhead, ALU.mult
                                    ).then_inc(sa_dve[par].sem, 1)

    def sattn_scores(pe, par, i):
        pe.wait_ge(sa_queries[par], i + 1)
        pe.wait_ge(k_landed[par], 16 * NPG * (i + 1))
        first = isinstance(i, int) and i == 0
        if not first:
            pe.wait_ge(sa_dve[par].sem, sa_dve[par].at("om", i) - 3)
        if par or not first:
            pe.wait_ge(sa_dve[1 - par].sem, sa_dve[1 - par].at("smax", i) - 3 * (1 - par))
        for hf in range(2):
            for j in range(4):
                nc.tensor.matmul(ps[32 * j:32 * j + 32, 2 * par + hf, :], Qs[par][:, j, :],
                                 Kp[par][:, 4 * hf:4 * hf + 4, j, :], start=True, stop=True)
        for j in range(4):
            nc.tensor.matmul(ps[32 * j:32 * j + 32, 4, DS * par:DS * par + DS], Qs[par][:, j, :],
                             kvn[par][:, j, :], start=True, stop=True)
        for j in range(4):
            mm = nc.tensor.transpose(ps[0:DS, 6 + par, j * P:j * P + P], kvn[par][:, 4 + j, :],
                                     ident)
        mm.then_inc(sa_pe[par].sem, 1)

    def sattn_values(pe, par, i):
        pe.wait_ge(sa_act[par].sem, sa_act[par].at("pT", i))
        pe.wait_ge(v_landed[par], 16 * NPG * (i + 1))
        nc.tensor.matmul(ps[0:64, 6 + par, :], prn[par][0:DS, :], vn[par][0:DS, :],
                         start=True, stop=False)
        for g in range(NPG):
            half = 64 * (g % 2)
            mm = nc.tensor.matmul(ps[half:half + 64, 6 + par, :], prTs[par][:, g, :],
                                  Vp[par][:, g, :], start=g == 1, stop=g >= NPG - 2)
        mm.then_inc(sa_pe[par].sem, 1)

    def sattn_outputs(pe, par, i):
        pe.wait_ge(sa_dve[par].sem, sa_dve[par].at("om", i))
        if par or not (isinstance(i, int) and i == 0):
            pe.wait_ge(sa_act[1 - par].sem, sa_act[1 - par].at("ms", i) - 4 * (1 - par))
        for j in range(4):
            mm = nc.tensor.matmul(ps[:, 5, 64 * par + DS * j:64 * par + DS * j + DS],
                                  om[par][:, j * P:j * P + P], cst["sumheads"],
                                  start=True, stop=True)
        mm.then_inc(sa_pe[par].sem, 1)

    def before(par, i):
        return 1 - par, i - (1 - par)

    def sattn_tensor(pe, i, first, more):
        for par in range(2):
            pe.wait_ge(sa_dve[par].sem, sa_dve[par].at("cm", i))
            for g in range(NPG):
                nc.tensor.matmul(ps[:, 2 * par, 64 * g:64 * g + 64], sS[par][:, g * P:g * P + P],
                                 Cm[par], start=True, stop=True)
            mm = nc.tensor.matmul(ps[0:DS, 2 * par + 1, 0:64], sS[par][:, PAST:PAST + DS], Cm[par],
                                  start=True, stop=True)
            mm.then_inc(sa_pe[par].sem, 1)
            if par or not first:
                sattn_outputs(pe, *before(par, i))
            if par == 0 or more:
                sattn_scores(pe, 1 - par, i + par)
            sattn_values(pe, par, i)

    def sattn_newvalues(act, par, i):
        act.wait_ge(sa_pe[par].sem, sa_pe[par].at("S", i))
        nc.scalar.activation(vn[par][0:DS, :], ps[0:DS, 6 + par, :], ACT.Copy
                             ).then_inc(sa_act[par].sem, 1)

    def sattn_exp(act, par, i):
        act.wait_ge(sa_dve[par].sem, sa_dve[par].at("smax", i))
        nc.scalar.activation(sS[par], sS[par], ACT.Exp, bias=nmaxS[:, par:par + 1],
                             accum_out=lS[:, par:par + 1]).then_inc(sa_act[par].sem, 1)

    def sattn_mix(act, par, i):
        act.wait_ge(sa_pe[par].sem, sa_pe[par].at("F", i))
        nc.scalar.activation(
            mixT[:, 0:4, ds(i * (2 * DS) + (TP + par * DS), DS)],
            ps[:, 5, 64 * par:64 * par + 4 * DS].rearrange("p (j s) -> p j s", s=DS),
            ACT.Copy).then_inc(sa_act[par].sem, 1)

    def sattn_scalar(act, i, first, more):
        for par in range(2):
            act.wait_ge(sa_pe[par].sem, sa_pe[par].at("PT", i))
            nc.scalar.activation(prn[par][0:DS, :], ps[0:DS, 2 * par + 1, 0:64], ACT.Copy)
            nc.scalar.activation(prTs[par][:, :, :].rearrange("p g n -> p (g n)"),
                                 ps[:, 2 * par, :], ACT.Copy).then_inc(sa_act[par].sem, 1)
            if par or not first:
                sattn_mix(act, *before(par, i))
            if par == 0 or more:
                sattn_newvalues(act, 1 - par, i + par)
                sattn_exp(act, 1 - par, i + par)

    sub = {n: sem(f"subnorm_{n}") for n in ("sq", "sum", "var", "root", "scale", "cast", "done")}

    def head_sums(sq, bank):
        for j in range(4):
            mm = nc.tensor.matmul(ps[32 * j:32 * j + 32, bank, 0:T], cst["halfsum"], sq[:, j, :],
                                  start=True, stop=True)
        return mm

    def head_cast(rows, bank):
        for j in range(4):
            r = slice(32 * j, 32 * j + 32)
            mm = nc.tensor.matmul(ps[:, bank + j, 0:T], cst["halfcast"][r, :], rows[r, :],
                                  start=True, stop=True)
        return mm

    xr, xk, xv = xb[:, 0:4, :], xb[:, 4:8, :], xb[:, 8:12, :]
    aR1 = Area(0)
    cumprev = aR1.take(4, T)
    cum = aR1.take(4, T)
    kk = aR1.take(4, T)
    aR = Area(base_b)
    kmod = aR.take(4, T)
    nb = aR.take(4, T)
    gup = aR.take(512)
    st = aR.take(5, 4 * P)
    stR, stQ, stK, stB, stV = (st[:, n, :].rearrange("p (j t) -> p j t", t=P) for n in range(5))
    ATm = aR.take(2, 512)
    S9 = aR.take(9, 256)
    Cst = aR.take(2, 256)
    Sbd = aR.take(2, 512)
    T1 = aR.take(256)
    T2 = aR.take(256)
    RW = aR.take(4, P)
    Y0 = aR.take(4, P)
    tokK, tokB, tokV = (aR.take(512) for _ in range(3))
    mats_at = aR.at
    mats = [{n: aR.take(512) for n in ("A0", "A1", "A2", "G", "ET", "MT", "NT", "QT", "X")}
            for _ in range(2)]
    ZF = aR.take(1024)
    for x in range(2):
        mats[x]["A3"] = ZF[:, 512 * x:512 * x + 512]
    pend = aR.take(4, 4)
    ex1, ex2, ex3 = (mats[0][n].rearrange("p (j t) -> p j t", t=P) for n in ("A0", "A1", "A2"))
    aM = Area(mats_at)
    aval = aM.take(4, T)
    tmpR = aM.take(4, T)
    sub_sq = aM.take(4, T)
    sub_rows = aM.take(T)
    kk_rows = aM.take(T)
    scan_keep = st[:, :, :].rearrange("p n t -> p (n t)")[:, 0:4 * T]
    waup = st[:, :, :].rearrange("p n t -> p (n t)")[:, 4 * T:4 * T + 512]
    yT = mixT[:, 4:8, :]
    post_sq, post_rk, post_rows = aval, tmpR, sub_rows
    gg, bonus = cumprev, kk
    aD = Area(base_b + 2 * TP + PAST + DS + 512)
    diff = aD.take(14, T)

    shift_done, shift_saved = sem("token_shift_done"), sem("shift_saved")
    kv_stored, ones_ready = sem("outputs_stored"), sem("ones_ready")
    rwkv_in = sem("rwkv_loads")
    mix_ready = sem("mix_ready")
    rw_over = sem("rwkv_over")

    def shift_pool(pool):
        pb = projT[:, 12:26, :]
        nc.gpsimd.tensor_tensor(diff[:, :, 1:T], pb[:, :, 0:T - 1], pb[:, :, 1:T], ALU.subtract
                                ).then_inc(shift_diff, 1)

    def shift_vector(dve):
        pb = projT[:, 12:26, :]
        nc.vector.tensor_copy(shift_out[:, :, :], pb[:, :, TP - 1:T:DS]).then_inc(shift_saved, 1)
        dve.wait_ge(shift_diff, 1)
        nc.vector.tensor_scalar(diff[:, :, 0:1], pb[:, :, 0:1], -1.0, None, ALU.mult)
        nc.vector.tensor_tensor(diff[:, :, TP:T:DS], shift_in[:, :, :], pb[:, :, TP:T:DS],
                                ALU.subtract)
        dve.drain()
        for m in range(14):
            last = nc.vector.scalar_tensor_tensor(pb[:, m, :], diff[:, m, :], mu[:, m:m + 1],
                                                  pb[:, m, :], ALU.mult, ALU.add)
        last.then_inc(shift_done, 1)

    shift_stored = sem("shift_rows_stored")
    shift_diff = sem("token_differences")
    rp = {n: sem("rwkv_" + n) for n in ("gates", "lora", "sig", "kk_sq", "kk_sum", "kk_root",
                                        "kk_scale", "kk_cast", "kk_read", "prep")}

    def rwkv_loads(pool):
        pool.wait_ge(sa_pe[0].sem, sa_pe[0].at("O", NB // 2 - 1))
        pool.wait_ge(kv_stored, 32)
        for dst, src in ((waup, a["wa_up"]), (gup, a["g_up"]), (scan_keep, a["scan_keep"]),
                         (S9[:, 1:9, :], a["s_init"])):
            pool.dma_start(dst, src).then_inc(rwkv_in, 16)

    def rwkv_gates_scalar(act):
        act.wait_ge(shift_done, 1)
        nc.scalar.activation(xb[0:64, 12, :], xb[0:64, 12, :], ACT.Tanh)
        nc.scalar.activation(xb[:, 13, :], xb[:, 13, :], ACT.Sigmoid).then_inc(rp["gates"], 1)

    def rwkv_prep_scalar(act):
        act.drain()
        nc.scalar.activation(sub_sq[:, :, :], mixT[:, 0:4, :], ACT.Square).then_inc(sub["sq"], 1)
        act.wait_ge(rp["lora"], 1)
        act.wait_ge(kv_stored, 32)
        for j in range(4):
            nc.scalar.activation(cumprev[:, j, :], ps[:, j, 0:T], ACT.Sigmoid, bias=w0c[:, j:j + 1])
        for j in range(4):
            last = nc.scalar.activation(aval[:, j, :], ps[:, 4 + j, 0:T], ACT.Sigmoid,
                                        bias=a0c[:, j:j + 1])
        last.then_inc(rp["sig"], 1)
        act.wait_ge(rp["kk_sum"], 1)
        nc.scalar.activation(kk_rows, ps[:, 0, 0:T], ACT.Sqrt).then_inc(rp["kk_root"], 1)
        act.wait_ge(sub["var"], 1)
        nc.scalar.activation(sub_rows, sub_rows, ACT.Sqrt).then_inc(sub["root"], 1)
        mod_scalar(act, G_MOD1, 5, 7)

    def rwkv_prep_tensor(pe):
        pe.wait_ge(rp["gates"], 1)
        pe.wait_ge(rwkv_in, 64)
        pe.wait_ge(mod_ready, 7 + 1)
        for par in range(2):
            pe.wait_ge(sa_act[par].sem, sa_act[par].at("ms", NB // 2 - 1))
        for j in range(4):
            nc.tensor.matmul(ps[:, j, 0:T], waup[0:64, j * P:j * P + P], xb[0:64, 12, :],
                             start=True, stop=True)
        for j in range(4):
            mm = nc.tensor.matmul(ps[:, 4 + j, 0:T], waup[64:P, j * P:j * P + P], xb[64:P, 12, :],
                                  start=True, stop=True)
        mm.then_inc(rp["lora"], 1)
        pe.wait_ge(rp["kk_sq"], 1)
        pe.wait_ge(rp["sig"], 1)
        head_sums(tmpR, 0).then_inc(rp["kk_sum"], 1)
        pe.wait_ge(sub["sq"], 1)
        head_sums(sub_sq, 4).then_inc(sub["sum"], 1)
        mod_tensor(pe, G_MOD1, 5, 7)
        pe.wait_ge(rp["kk_scale"], 1)
        head_cast(kk_rows, 0).then_inc(rp["kk_cast"], 1)
        pe.wait_ge(sub["scale"], 1)
        pe.wait_ge(rp["kk_read"], 1)
        head_cast(sub_rows, 0).then_inc(sub["cast"], 1)

    def rwkv_prep_vector(dve):
        dve.wait_ge(rwkv_in, 64)
        dve.wait_ge(sa_pe[1].sem, sa_pe[1].at("F", NB // 2 - 1))
        for j in range(4):
            nc.vector.tensor_scalar(kk[:, j, :], xk[:, j, :], kkc[:, j:j + 1], None, ALU.mult)
        dve.drain()
        nc.vector.tensor_tensor(tmpR[:, :, :], kk[:, :, :], kk[:, :, :], ALU.mult
                                ).then_inc(rp["kk_sq"], 1)
        nc.vector.memset(S9[:, 0, :], 0.0)
        nc.vector.memset(Sbd[:, :, :], 0.0)
        nc.vector.memset(ATm[:, :, :], 0.0)
        dve.wait_ge(rp["sig"], 1)
        flat = "p j t -> p (j t)"
        for j in range(4):
            nc.vector.tensor_scalar(kmod[:, j, :], aval[:, j, :], 1.0, kac[:, j:j + 1],
                                    ALU.subtract, ALU.mult)
        dve.wait_ge(rp["kk_root"], 1)
        nc.vector.tensor_scalar(kk_rows, kk_rows, 1e-12, None, ALU.max)
        dve.drain()
        nc.vector.reciprocal(kk_rows, kk_rows).then_inc(rp["kk_scale"], 1)
        dve.wait_ge(sub["sum"], 1)
        nc.vector.tensor_scalar(sub_rows, ps[:, 4, 0:T], 1.0 / DV, RMS_EPS, ALU.mult,
                                ALU.add).then_inc(sub["var"], 1)
        nc.vector.tensor_tensor_scan(cum[:, :, :].rearrange(flat), scan_keep,
                                     cumprev[:, :, :].rearrange(flat), 0.0, ALU.mult, ALU.add)
        dve.drain()
        nc.vector.tensor_tensor(cumprev[:, :, :], cum[:, :, :], cumprev[:, :, :], ALU.subtract)
        nc.vector.scalar_tensor_tensor(kmod[:, :, :].rearrange(flat), kmod[:, :, :].rearrange(flat),
                                       1.0, xk[:, :, :].rearrange(flat), ALU.add, ALU.mult)
        dve.wait_ge(sub["root"], 1)
        nc.vector.reciprocal(sub_rows, sub_rows).then_inc(sub["scale"], 1)
        dve.wait_ge(rp["kk_cast"], 1)
        nc.vector.tensor_tensor(kk[:, :, :], kk[:, :, :], ps[:, 0:4, 0:T], ALU.mult
                                ).then_inc(rp["kk_read"], 1)
        dve.drain()
        nc.vector.scalar_tensor_tensor(nb[:, :, :].rearrange(flat), kk[:, :, :].rearrange(flat),
                                       -1.0, aval[:, :, :].rearrange(flat), ALU.mult, ALU.mult)
        dve.wait_ge(sub["cast"], 1)
        nc.vector.tensor_tensor(mixT[:, 0:4, :], mixT[:, 0:4, :], ps[:, 0:4, 0:T], ALU.mult
                                ).then_inc(sub["done"], 1)
        dve.drain().then_inc(rp["prep"], 1)
        nc.vector.tensor_scalar(mixT[:, 0:4, :], mixT[:, 0:4, :], sgc, 1.0 - LAM_INIT, ALU.mult,
                                ALU.mult)
        mod_vector(dve, 7)

    PER = ["turn"] + [f"{x}{h}" for x in ("s1", "s2", "s3", "s4", "s5", "s6", "s7", "s8")
                      for h in range(2)]
    PER += ["yr", "wc0", "wc1", "y0", "wc2", "y1", "wc3", "y2", "y3"]
    DVR = ["prod"] + [f"m1{h}" for h in range(2)] + [f"qx{h}" for h in range(2)]
    DVR += [f"g{n}{h}" for n in (1, 2, 3) for h in range(2)] + [f"zf{h}" for h in range(2)]
    DVR += ["rw", "ac0", "ac1", "s0", "ac2", "s1", "ac3", "s2", "s3", "yt"]
    ACR = ["exps", "tok"] + [f"{x}{h}" for x in ("sq2", "sq4", "sq8", "z", "ez") for h in range(2)]
    ACR += ["y0"] + [f"bd{c}" for c in range(4)]
    LONG = ("s50", "s51", "s70", "s71", "s80", "s81", "g30", "g31", "sq80", "sq81", "ez0", "ez1")
    PERS, DVRS, ACRS = ([[n for n in names if n not in ("bd1", "bd2", "bd3")],
                         [n for n in names if n not in LONG]] for names in (PER, DVR, ACR))
    r_pe, r_dve, r_act = sem("rtile_pe"), sem("rtile_dve"), sem("rtile_act")
    rpe = [Steps(r_pe, PERS[x], x * 2 * len(PER)) for x in range(2)]
    RD0 = 1
    rdve = [Steps(r_dve, DVRS[x], x * 2 * len(DVR) + RD0) for x in range(2)]
    ract = [Steps(r_act, ACRS[x], x * 2 * len(ACRS[0])) for x in range(2)]

    UW = ZF.rearrange("p (j u h v) -> p j u h v", j=4, u=2, h=2)

    def heads4(m):
        return m.rearrange("p (h t) -> p h t", t=P)

    def tile_views(part, i):
        if part == 0:
            return (lambda x: x[:, :, ds(i * P, P)], lambda x: x, lambda x: x, P)
        four = "p j (b s) -> p j b s"
        return (lambda x: x[:, :, ds(i * 4 * DS + TP, 4 * DS)].rearrange(four, s=DS),
                lambda x: x.rearrange("p j (b s) -> p j b s", s=RC)[:, :, :, 0:DS],
                lambda x: x[:, :, 0:4 * DS].rearrange(four, s=DS), 4 * DS)

    def state(part, i, cc):
        return S9[:, 0:1, :] if part == 0 else S9[:, ds(i * 4 + (cc + 1), 1), :]

    def rtile_vector(dve, part, i):
        col, stg, comp, n = tile_views(part, i)
        D_, A_, P_ = rdve[part], ract[part], rpe[part]
        dve.wait_ge(r_act, A_.at("exps", i))
        for dst, x, e in ((stR, xr, ex1), (stQ, kk, ex3), (stK, kmod, ex2), (stB, nb, ex2)):
            nc.vector.tensor_tensor(stg(dst), col(x), comp(e), ALU.mult)
        nc.vector.tensor_copy(stg(stV), col(xv))
        step = n // 4
        nc.vector.tensor_copy(pend[:, :, :], ex1[:, :, step - 1:n:step]).then_inc(r_dve, 1)

        def masked(dst, b, mask):
            nc.vector.tensor_tensor(heads4(dst), heads4(ps[:, b, :]),
                                    cst[mask].unsqueeze(1).to_broadcast([P, 4, P]), ALU.mult)
        for h in range(2):
            m, b = mats[h], 4 * h
            dve.wait_ge(r_pe, P_.at(f"s1{h}", i))
            masked(m["A0"], b, "low16")
            masked(m["A1"], b + 1, "up16")
            masked(m["ET"], b + 1, "up32off")
            masked(m["MT"], b + 2, "up32")
            masked(m["NT"], b + 3, "up32incl")
            dve.drain()
            nc.vector.tensor_tensor(heads4(m["G"]), heads4(m["A1"]),
                                    ident.unsqueeze(1).to_broadcast([P, 4, P]), ALU.add
                                    ).then_inc(r_dve, 1)
        for h in range(2):
            m, b = mats[h], 4 * h
            dve.wait_ge(r_pe, P_.at(f"s2{h}", i))
            masked(m["QT"], b + 2, "up32incl")
            nc.vector.tensor_copy(heads4(m["X"])[:, :, 0:64],
                                  ps[:, b + 3, 0:256].rearrange("p (k v) -> p k v", v=64)
                                  ).then_inc(r_dve, 1)
        for s, src in (("s3", 2), ("s4", 3), ("s5", 1))[:3 - part]:
            for h in range(2):
                m, b = mats[h], 4 * h
                dve.wait_ge(r_pe, P_.at(f"{s}{h}", i))
                nc.vector.tensor_tensor(m["G"], m["G"], ps[:, b + src, :], ALU.add
                                        ).then_inc(r_dve, 1)
        for h in range(2):
            m, b = mats[h], 4 * h
            v = "p (k u v) -> p k u v"
            if part:
                dve.wait_ge(r_act, A_.at(f"z{h}", i))
                nc.vector.tensor_copy(UW[:, :, :, h, :], m["A0"].rearrange(v, u=2, v=64)
                                      ).then_inc(r_dve, 1)
                continue
            dve.wait_ge(r_pe, P_.at(f"s8{h}", i))
            nc.vector.tensor_tensor(UW[:, :, :, h, :], m["A0"].rearrange(v, u=2, v=64),
                                    ps[:, b, :].rearrange(v, u=2, v=64), ALU.add
                                    ).then_inc(r_dve, 1)
        dve.wait_ge(r_pe, P_.at("yr", i))
        nc.vector.tensor_tensor(RW[:, :, :].rearrange("p j t -> p (j t)"), st[:, 0, :],
                                ps[:, 1, :], ALU.add).then_inc(r_dve, 1)

        def chunk_matrices(cc):
            dve.wait_ge(r_pe, P_.at(f"wc{cc}", i))
            t = cc % 2
            for q in (0, 64):
                nc.vector.tensor_copy(heads4(ATm[q:q + 64, t, :])[:, :, q:q + 64],
                                      heads4(ps[q:q + 64, 2 + 2 * t, :])[:, :, q:q + 64])
            for q in (0, 64):
                last = nc.vector.tensor_tensor(
                    Cst[q:q + 64, t, :].rearrange("p (j v) -> p j v", v=64),
                    heads4(ps[q:q + 64, 3 + 2 * t, :])[:, :, q:q + 64],
                    pend[q:q + 64, :, cc:cc + 1].to_broadcast([64, 4, 64]), ALU.mult)
            last.then_inc(r_dve, 1)

        def chunk_state(cc):
            s = state(part, i, cc)
            pe4 = pend[:, :, cc:cc + 1].to_broadcast([P, 4, 64])
            v4 = "p o (j v) -> p (o j) v"
            nc.vector.tensor_tensor(T1.rearrange("p (j v) -> p j v", v=64), s.rearrange(v4, v=64),
                                    pe4, ALU.mult)
            dve.drain()
            nc.vector.tensor_tensor(T1, T1, Cst[:, cc % 2, :], ALU.add)
            dve.wait_ge(r_pe, P_.at(f"y{cc}", i))
            nc.vector.tensor_tensor(T2.rearrange("p (j v) -> p j v", v=64),
                                    ps[:, 6, 0:256].rearrange("p (j v) -> p j v", v=64), pe4,
                                    ALU.mult)
            dve.drain()
            if part == 0 and cc < 3:
                for q in (0, 64):
                    h = slice(q, q + 64)
                    last = nc.vector.tensor_tensor(
                        heads4(Sbd[h, (cc + 1) % 2, :])[:, :, q:q + 64],
                        *(x[h, :].rearrange("p (j v) -> p j v", v=64) for x in (T1, T2)), ALU.add)
                last.then_inc(r_dve, 1)
            last = nc.vector.tensor_tensor(s, T1.unsqueeze(1), T2.unsqueeze(1), ALU.add)
            if part or cc == 3:
                last.then_inc(r_dve, 1)
            dve.drain()
        chunk_matrices(0)
        chunk_matrices(1)
        chunk_state(0)
        chunk_matrices(2)
        chunk_state(1)
        chunk_matrices(3)
        chunk_state(2)
        chunk_state(3)
        dve.wait_ge(r_act, A_.at("y0", i))
        nc.vector.tensor_tensor(col(yT), stg(ps[:, 7, :].rearrange("p (j t) -> p j t", t=P)),
                                stg(Y0), ALU.add).then_inc(r_dve, 1)

    def rtile_scalar(act, part, i):
        col, stg, comp, n = tile_views(part, i)
        D_, A_, P_ = rdve[part], ract[part], rpe[part]
        if part == 0:
            act.wait_ge(rp["prep"], 1)
        act.wait_ge(r_dve, D_.base + i * len(D_.names))
        for dst, src, s in ((ex1, cum, -KAPPA), (ex2, cum, KAPPA), (ex3, cumprev, -KAPPA)):
            last = nc.scalar.activation(comp(dst), col(src), ACT.Exp, scale=s)
        last.then_inc(r_act, 1)
        act.wait_ge(r_pe, P_.at("turn", i))
        for dst, b in ((tokK, 1), (tokB, 2), (tokV, 3)):
            nc.scalar.activation(dst, ps[:, b, :], ACT.Copy)
        for h in range(2):
            last = nc.scalar.activation(
                heads4(mats[h]["X"])[:, :, 64:P],
                ps[:, 0, :].rearrange("p (k h v) -> p k h v", h=2, v=64)[:, :, h, :], ACT.Copy)
        last.then_inc(r_act, 1)
        for s, pairs in (("s2", (("A2", 0), ("A3", 1))), ("s3", (("A0", 0), ("A1", 1))),
                         ("s4", (("A2", 0),)), ("s6", (("A0", 2),)), ("s7", (("A1", 3),))):
            if part and s in ("s4", "s7"):
                continue
            for h in range(2):
                act.wait_ge(r_pe, P_.at(f"{s}{h}", i))
                for dst, b in pairs:
                    last = nc.scalar.activation(mats[h][dst], ps[:, 4 * h + b, :], ACT.Copy)
                last.then_inc(r_act, 1)
        act.wait_ge(r_pe, P_.at("yr", i))
        nc.scalar.activation(Y0[:, :, :].rearrange("p j t -> p (j t)"), ps[:, 0, :], ACT.Copy
                             ).then_inc(r_act, 1)
        for cc in range(4 if part else 1):
            if cc > 1:
                act.wait_ge(r_pe, P_.at(f"y{cc - 2}", i))
            s = state(part, i, cc)
            for q in (0, 64):
                last = nc.scalar.activation(
                    Sbd[q:q + 64, cc % 2, :].rearrange("p (o j v) -> p o j v", o=1, v=P)[:, :, :, q:q + 64],
                    s[q:q + 64, :, :].rearrange("p o (j v) -> p o j v", v=64), ACT.Copy)
            last.then_inc(r_act, 1)

    def rtile_tensor(pe, part, i):
        D_, A_, P_ = rdve[part], ract[part], rpe[part]
        mm_ = nc.tensor.matmul
        pe.wait_ge(r_dve, D_.at("prod", i))
        pe.wait_ge(sub["done"], 1)
        for b, src in ((0, stQ), (1, stK), (2, stB), (3, stV)):
            for j in range(4):
                last = nc.tensor.transpose(ps[:, b, j * P:j * P + P], src[:, j, :], ident)
        last.then_inc(r_pe, 1)

        def head(x, h, k):
            return x[64 * h:64 * h + 64, k, :]

        def four(b, f):
            for k in range(4):
                lhsT, rhs = f(k)
                n = rhs.free_size()
                last = mm_(ps[:, b, k * n:k * n + n], lhsT, rhs, start=True, stop=True)
            return last

        def mat(h, name):
            m = mats[h][name]
            return lambda k: m[:, k * P:k * P + P]
        for h in range(2):
            b = 4 * h
            if h == 0:
                pe.wait_ge(r_act, A_.at("tok", i))
            four(b, lambda k: (head(stQ, h, k), head(stB, h, k)))
            four(b + 1, lambda k: (head(stB, h, k), head(stQ, h, k)))
            four(b + 2, lambda k: (head(stK, h, k), head(stQ, h, k)))
            four(b + 3, lambda k: (head(stK, h, k), head(stR, h, k))).then_inc(r_pe, 1)
        for h in range(2):
            b = 4 * h
            pe.wait_ge(r_dve, D_.at(f"m1{h}", i))
            A0, A1, MT = mat(h, "A0"), mat(h, "A1"), mat(h, "MT")
            four(b, lambda k: (A1(k), A0(k)))
            four(b + 1, lambda k: (A0(k), A1(k)))
            four(b + 2, lambda k: (head(stB, h, k), head(stR, h, k)))
            four(b + 3, lambda k: (MT(k), tokV[:, (2 * k + h) * 64:(2 * k + h) * 64 + 64])
                 ).then_inc(r_pe, 1)
        for h in range(2):
            b = 4 * h
            A2, A3, G = mat(h, "A2"), mat(h, "A3"), mat(h, "G")
            pe.wait_ge(r_act, A_.at(f"sq2{h}", i))
            four(b, lambda k: (A3(k), A2(k)))
            four(b + 1, lambda k: (A2(k), A3(k)))
            pe.wait_ge(r_dve, D_.at(f"qx{h}", i))
            four(b + 2, lambda k: (A2(k), G(k))).then_inc(r_pe, 1)
        for h in range(2):
            b = 4 * h
            A0, A1, G = mat(h, "A0"), mat(h, "A1"), mat(h, "G")
            pe.wait_ge(r_act, A_.at(f"sq4{h}", i))
            if part == 0:
                four(b, lambda k: (A1(k), A0(k)))
            pe.wait_ge(r_dve, D_.at(f"g1{h}", i))
            four(b + 3, lambda k: (A0(k), G(k))).then_inc(r_pe, 1)
        for h in range(2 if part == 0 else 0):
            b = 4 * h
            A2, G = mat(h, "A2"), mat(h, "G")
            pe.wait_ge(r_act, A_.at(f"sq8{h}", i))
            pe.wait_ge(r_dve, D_.at(f"g2{h}", i))
            four(b + 1, lambda k: (A2(k), G(k))).then_inc(r_pe, 1)
        for h in range(2):
            b = 4 * h
            G = mat(h, "G")
            pe.wait_ge(r_dve, D_.at(f"g{3 - part}{h}", i))
            X = mat(h, "X")
            four(b + 2, lambda k: (G(k), X(k))).then_inc(r_pe, 1)
        for h in range(2 if part == 0 else 0):
            b = 4 * h
            ET = mat(h, "ET")
            pe.wait_ge(r_act, A_.at(f"z{h}", i))
            A0 = mat(h, "A0")
            four(b + 3, lambda k: (ET(k), A0(k))).then_inc(r_pe, 1)
        for h in range(2 if part == 0 else 0):
            b = 4 * h
            G = mat(h, "G")
            pe.wait_ge(r_act, A_.at(f"ez{h}", i))
            A1 = mat(h, "A1")
            four(b, lambda k: (G(k), A1(k))).then_inc(r_pe, 1)
        pe.wait_ge(r_dve, D_.at("zf1", i))
        for k in range(4):
            for n in range(3):
                for h in range(2):
                    half = 64 * h
                    U0, W = UW[:, k, 0, h, :], UW[:, k, 1, h, :]
                    QT, NT = mat(h, "QT")(k), mat(h, "NT")(k)
                    y = ps[half:half + 64, 0, k * P:k * P + P]
                    if n == 0:
                        mm_(y, tokV[:, k * P + half:k * P + half + 64], NT, start=True, stop=False)
                    elif n == 1:
                        mm_(y, U0, QT, start=False, stop=True)
                    else:
                        last = mm_(ps[half:half + 64, 1, k * P:k * P + P], W, QT, start=True,
                                   stop=True)
        last.then_inc(r_pe, 1)

        def chunk_products(cc):
            t, r = cc % 2, slice(RC * cc, RC * cc + RC)
            for j in range(4):
                for n in range(3):
                    for h in range(2):
                        q = 64 * h
                        own = slice(j * P + q, j * P + q + 64)
                        U, W = (ZF[r, 2 * P * j + x + q:2 * P * j + x + q + 64] for x in (0, P))
                        B, K, V = (x[r, own] for x in (tokB, tokK, tokV))
                        a_, c_ = (ps[q:q + 64, x + 2 * t, own] for x in (2, 3))
                        if n == 0:
                            mm_(a_, W, B, start=True, stop=True)
                        elif n == 1:
                            mm_(c_, K, V, start=True, stop=False)
                        else:
                            last = mm_(c_, B, U, start=False, stop=True)
            last.then_inc(r_pe, 1)

        def chunk_step(cc):
            pe.wait_ge(r_dve, D_.at(f"ac{cc}", i))
            if cc:
                pe.wait_ge(r_dve, D_.at(f"s{cc - 1}", i))
            if part or cc == 0:
                pe.wait_ge(r_act, A_.at(f"bd{cc}", i))
            for j in range(4):
                for q in (0, 64):
                    mm_(ps[q:q + 64, 6, j * 64:j * 64 + 64],
                        ATm[:, cc % 2, j * P + q:j * P + q + 64],
                        Sbd[:, cc % 2, j * P + q:j * P + q + 64], start=True, stop=True)
            for j in range(4):
                for q in (0, 64):
                    last = mm_(ps[q:q + 64, 7, j * P + RC * cc:j * P + RC * cc + RC],
                               Sbd[:, cc % 2, j * P + q:j * P + q + 64],
                               RW[:, j, RC * cc:RC * cc + RC], start=True, stop=True)
            last.then_inc(r_pe, 1)
        chunk_products(0)
        chunk_products(1)
        pe.wait_ge(r_dve, D_.at("rw", i))
        chunk_step(0)
        chunk_products(2)
        chunk_step(1)
        chunk_products(3)
        chunk_step(2)
        chunk_step(3)


    po = {n: sem("rwkv_post_" + n) for n in ("rk", "rk_sum", "bonus", "g", "g_read", "mean", "cent",
                                             "sq", "sum", "var", "root", "scale", "cast")}

    def rwkv_post_scalar(act):
        act.wait_ge(po["cent"], 1)
        nc.scalar.activation(post_sq[:, :, :], yT, ACT.Square).then_inc(po["sq"], 1)
        act.wait_ge(po["g"], 1)
        nc.scalar.activation(gg[:, :, :], ps[:, 0:4, 0:T], ACT.Copy).then_inc(po["g_read"], 1)
        act.wait_ge(po["var"], 1)
        nc.scalar.activation(post_rows, post_rows, ACT.Sqrt).then_inc(po["root"], 1)

    def rwkv_post_tensor(pe):
        pe.wait_ge(r_dve, rdve[1].at("yt", 1))
        for j in range(4):
            mm = nc.tensor.matmul(ps[:, j, 0:T], block64, yT[:, j, :], start=True, stop=True)
        mm.then_inc(po["mean"], 1)
        pe.wait_ge(po["rk"], 1)
        for j in range(4):
            mm = nc.tensor.matmul(ps[:, 4 + j, 0:T], block64, post_rk[:, j, :], start=True,
                                  stop=True)
        mm.then_inc(po["rk_sum"], 1)
        pe.wait_ge(po["cent"], 1)
        for j in range(4):
            mm = nc.tensor.matmul(ps[:, j, 0:T], gup[:, j * P:j * P + P], xb[:, 13, :], start=True,
                                  stop=True)
        mm.then_inc(po["g"], 1)
        pe.wait_ge(po["sq"], 1)
        pe.wait_ge(po["bonus"], 1)
        head_sums(post_sq, 4).then_inc(po["sum"], 1)
        pe.wait_ge(po["scale"], 1)
        head_cast(post_rows, 4).then_inc(po["cast"], 1)

    def rwkv_post_vector(dve):
        dve.drain().then_inc(rw_over, 1)
        nc.vector.tensor_tensor(post_rk[:, :, :], xr, kmod[:, :, :], ALU.mult)
        dve.drain()
        for j in range(4):
            last = nc.vector.tensor_scalar(post_rk[:, j, :], post_rk[:, j, :], rkc[:, j:j + 1],
                                           None, ALU.mult)
        last.then_inc(po["rk"], 1)
        dve.wait_ge(po["mean"], 1)
        nc.vector.scalar_tensor_tensor(yT, ps[:, 0:4, 0:T], -1.0 / 64, yT, ALU.mult, ALU.add
                                       ).then_inc(po["cent"], 1)
        dve.wait_ge(po["rk_sum"], 1)
        nc.vector.tensor_tensor(bonus[:, :, :], ps[:, 4:8, 0:T], xv, ALU.mult
                                ).then_inc(po["bonus"], 1)
        dve.wait_ge(po["sum"], 1)
        nc.vector.tensor_scalar(post_rows, ps[:, 4, 0:T], 1.0 / 64, LNX_EPS, ALU.mult,
                                ALU.add).then_inc(po["var"], 1)
        dve.wait_ge(po["root"], 1)
        nc.vector.reciprocal(post_rows, post_rows).then_inc(po["scale"], 1)
        dve.wait_ge(po["g_read"], 1)
        dve.wait_ge(po["cast"], 1)
        nc.vector.tensor_tensor(yT, yT, ps[:, 4:8, 0:T], ALU.mult)
        dve.drain()
        for j in range(4):
            nc.vector.tensor_scalar(yT[:, j, :], yT[:, j, :], lgc[:, j:j + 1], lbc[:, j:j + 1],
                                    ALU.mult, ALU.add)
        dve.drain()
        nc.vector.tensor_tensor(yT, yT, bonus[:, :, :], ALU.add)
        dve.drain()
        nc.vector.tensor_tensor(yT, yT, gg[:, :, :], ALU.mult).then_inc(mix_ready, 1)

    def rwkv_scalar(act):
        rwkv_prep_scalar(act)
        for part in range(2):
            with act.Fori(0, 2) as i:
                rtile_scalar(act, part, i)
                mod_scalar(act, G_MOD1, i + (6 + 2 * part), i + (8 + 2 * part))
        rwkv_post_scalar(act)

    def rwkv_vector(dve):
        rwkv_prep_vector(dve)
        dve.drain().then_inc(r_dve, RD0)
        with dve.Fori(0, 2) as i:
            rtile_vector(dve, 0, i)
            mod_vector(dve, i + 8)
        nc.vector.memset(st[:, :, :], 0.0)
        dve.drain()
        with dve.Fori(0, 2) as i:
            rtile_vector(dve, 1, i)
            mod_vector(dve, i + 10)
        rwkv_post_vector(dve)

    def rwkv_tensor(pe):
        rwkv_prep_tensor(pe)
        for part in range(2):
            with pe.Fori(0, 2) as i:
                rtile_tensor(pe, part, i)
                pe.wait_ge(r_dve, rdve[part].at("yt", i))
                mod_tensor(pe, G_MOD1, i + (6 + 2 * part), i + (8 + 2 * part))
        rwkv_post_tensor(pe)

    sgate = [arena[:, at_sgate + x * T:at_sgate + x * T + T] for x in range(2)]
    htmp = arena[:, at_htmp:at_htmp + 2 * T].rearrange("p (a t) -> p a t", t=T)
    hid_act, hid_ready = sem("gate_silu"), sem("hidden_ready")

    def gu_tensor(pe):
        pe.wait_ge(h_ready, 2)

        def body(c, k, i):
            pe.wait_ge(lo_ready, c + (S_GU + 1))
            wait_psum(pe, G_GU, c)
            w = parts(S_GU, k, 2 * KT, P)
            for t in range(2):
                for q in range(KT):
                    mm = three_passes(ps[:, pbank(G_GU, k) + t, 0:T],
                                      [v[:, t * KT + q, :] for v in w],
                                      [hx_hi[:, q, :], hx_lo[:, q, :]], q == 0, q == KT - 1)
            mm.then_inc(chunk_done, 1)
        by_four(pe, N_GU, body)

    def gu_split_first(act):
        act.wait_ge(mix_ready, 1)
        act.wait_ge(kv_stored, 16 * 3)
        split_hi(act, act_copy, G_GU, S_GU, 0, 0, 0, 2 * KT, P)

    def gu_scalar(act):
        def body(c, k, i):
            if not (isinstance(c, int) and c == N_GU - 1):
                c1, k1 = c + 1, k + 1
                split_hi(act, act_copy, G_GU, S_GU, c1, k1, i, 2 * KT, P)
            wait_done(act, G_GU, c)
            act.wait_ge(hid_ready, c + 1)
            nc.scalar.activation(sgate[k % 2], ps[:, pbank(G_GU, k), 0:T], ACT.Silu
                                 ).then_inc(hid_act, 1)
        by_four(act, N_GU, body)

    def gu_vector(dve):
        dve.drain().then_inc(hid_ready, 2)

        def body(c, k, i):
            h = htmp[:, k % 2:k % 2 + 1, :]
            hi = hid_hi[:, ds(c, 1), :]
            dve.wait_ge(hid_act, c + 1)
            nc.vector.tensor_tensor(h, sgate[k % 2].unsqueeze(1),
                                    ps[:, pbank(G_GU, k) + 1:pbank(G_GU, k) + 2, 0:T], ALU.mult
                                    ).then_inc(chunk_read, 1)
            dve.drain()
            nc.vector.tensor_copy(hi, h)
            dve.drain()
            nc.vector.tensor_tensor(hid_lo[:, ds(c, 1), :], h, hi.bitcast(F32), ALU.subtract)
            dve.drain().then_inc(hid_ready, 1)
        by_four(dve, N_GU, body)

    aO = Area(0)
    uT = aO.take(EC // P, T)
    vtk = aO.take(3, EC)
    bsB = aO.take(GC, T)
    stats = aO.take(3, 8, 6)
    aggr = aO.take(3, 3)
    assert aO.at <= at_split
    aU = Area(at_um)
    lnvg = aU.take(EC)
    lnvb = aU.take(EC)
    hflat = hT[:, :, :].rearrange("p k t -> p (k t)")
    wsT = hflat[:, 0:GC * CHUNK].rearrange("p (g t) -> p g t", t=CHUNK)
    wsS = hflat[:, GC * CHUNK:GC * (CHUNK + TS)].rearrange("p (g t) -> p g t", t=TS)
    mtmp = hflat[:, GC * (CHUNK + TS):GC * (CHUNK + TS) + 2 * T].rearrange("p (a t) -> p a t", a=2)
    odd_kn = (KT, 2 * P, KT * 256)
    out_o_kn = (EC // P, P, KT * 256)
    odd_in, odd_masked = sem("gmlp_loads"), sem("spatial_masked")
    u_ready = sem("u_ready")
    lnv_var, lnv_root, lnv_scale = sem("lnv_var"), sem("lnv_root"), sem("lnv_scale")
    v_centred, v_ready, v_ready_sample = sem("v_centred"), sem("v_ready"), sem("v_ready_sample")
    mixed_mm, mixed_rd = sem("mixed_product"), sem("mixed_read")

    def odd_loads(pool):
        pool.wait_ge(x_ready, 3)
        for dst, src in ((lnvg, a["lnv_g"].partition_broadcast(P)),
                         (lnvb, a["lnv_b"].partition_broadcast(P)),
                         (bsB[:, :, :].rearrange("p g t -> p (g t)"), a["b_s"].partition_broadcast(P)),
                         (wsT[:, :, :], a["w_s"]), (wsS[0:TS, :, :], a["w_s8"])):
            if src is a["w_s"]:
                split_lo_all(pool, G_IN_O, S_IN_O, 2, *odd_kn)
                pool.wait_ge(h_ready, 3)
            pool.dma_start(dst, src).then_inc(odd_in, 16)

    def in_o_tensor(pe):
        columns_split(pe, G_IN_O, S_IN_O, 8, KT, 2, (hx_hi, hx_lo), lambda e: e.wait_ge(h_ready, 3),
                      KT * 256)

        def body(c, k, i):
            g0, s0 = G_IN_O + 8, S_IN_O + 8
            pe.wait_ge(lo_ready, c + (s0 + 1))
            wait_psum(pe, g0, c)
            w = parts(s0, k, KT, 2 * P, KT * 256)
            for n in range(3):
                rows = P if n < 2 else TS
                for q in range(KT):
                    mm = three_passes(
                        ps[0:rows, pbank(g0, k) + n // 2, (n % 2) * 256:(n % 2) * 256 + 256],
                        [v[:, q, n * P:n * P + rows] for v in (hx_hi, hx_lo)],
                        [v[:, q, :] for v in w], q == 0, q == KT - 1)
            mm.then_inc(chunk_done, 1)
        by_four(pe, 8, body)

    def in_o_scalar(act):
        def body_u(c, k, i):
            wait_done(act, G_IN_O, c)
            b = pbank(G_IN_O, k)
            nc.scalar.activation(uT[:, ds(2 * c, 2), :], ps[:, b:b + 2, 0:T], ACT.Gelu
                                 ).then_inc(chunk_read, 1)
        by_four(act, 8, body_u)
        act.drain().then_inc(u_ready, 1)

        def body_v(c, k, i):
            g0 = G_IN_O + 8
            wait_done(act, g0, c)
            b = pbank(g0, k)
            nc.scalar.activation(vtk[:, 0:2, ds(c * 256, 256)],
                                 ps[:, b, :].rearrange("p (n f) -> p n f", n=2), ACT.Gelu)
            nc.scalar.activation(vtk[0:TS, 2, ds(c * 256, 256)], ps[0:TS, b + 1, 0:256], ACT.Gelu
                                 ).then_inc(chunk_read, 1)
        by_four(act, 8, body_v)
        act.wait_ge(lnv_var, 1)
        nc.scalar.activation(aggr[:, 0:2, 1:2], aggr[:, 0:2, 1:2], ACT.Sqrt)
        nc.scalar.activation(aggr[0:TS, 2, 1:2], aggr[0:TS, 2, 1:2], ACT.Sqrt
                             ).then_inc(lnv_root, 1)
        act.wait_ge(lnv_scale, 1)
        for half in range(2):
            for n in range(3):
                rows = P if n < 2 else TS
                v = vtk[0:rows, n, half * (EC // 2):(half + 1) * (EC // 2)]
                nc.scalar.activation(v, v, ACT.Identity, bias=aggr[0:rows, n, 2:3],
                                     scale=aggr[0:rows, n, 1:2]).then_inc(v_centred, 1)

    def v_norm_vector(dve):
        dve.wait_ge(lo_ready, S_IN_O + 2)
        split_both(dve, G_IN_O + 2, S_IN_O + 2, 6, *odd_kn)
        dve.wait_ge(odd_in, 16 * 5)
        nc.vector.tensor_tensor(wsT[:, :, :], wsT[:, :, :],
                                cst["upincl"].unsqueeze(1).to_broadcast([P, GC, CHUNK]), ALU.mult)
        nc.vector.tensor_tensor(wsS[0:TS, :, :], wsS[0:TS, :, :],
                                cst["upincl8"][0:TS, 0:TS].unsqueeze(1).to_broadcast([TS, GC, TS]),
                                ALU.mult).then_inc(odd_masked, 1)

        def statistics(c):
            dve.wait_ge(chunk_read, G_IN_O + 8 + c + 1 + READ0)
            for n in range(3):
                rows = P if n < 2 else TS
                nc.vector.bn_stats(stats[0:rows, n, c, :], vtk[0:rows, n, c * 256:c * 256 + 256])
        g0, s0 = G_IN_O + 8, S_IN_O + 8
        split_both(dve, g0, s0, 2, *odd_kn)
        for c in range(2, 8):
            split_both(dve, g0 + c, s0 + c, 1, *odd_kn)
            statistics(c - 2)
        statistics(6)
        statistics(7)
        dve.drain()
        for n in range(3):
            rows = P if n < 2 else TS
            nc.vector.bn_aggr(aggr[0:rows, n, 0:2], stats[0:rows, n, :, :])
        dve.drain()
        parts_ = ((slice(0, P), slice(0, 2)), (slice(0, TS), slice(2, 3)))
        for rows, n in parts_:
            last = nc.vector.tensor_scalar(aggr[rows, n, 1:2], aggr[rows, n, 1:2], LN_EPS, None,
                                           ALU.add)
        last.then_inc(lnv_var, 1)
        dve.wait_ge(lnv_root, 1)
        for rows, n in parts_:
            nc.vector.reciprocal(aggr[rows, n, 1:2], aggr[rows, n, 1:2])
        dve.drain()
        for rows, n in parts_:
            last = nc.vector.scalar_tensor_tensor(aggr[rows, n, 2:3], aggr[rows, n, 0:1], -1.0,
                                                  aggr[rows, n, 1:2], ALU.mult, ALU.mult)
        last.then_inc(lnv_scale, 1)
        for half in range(2):
            cols = slice(half * (EC // 2), (half + 1) * (EC // 2))
            for n in range(2):
                dve.wait_ge(v_centred, 3 * half + n + 1)
                nc.vector.tensor_tensor(vtk[:, n, cols], vtk[:, n, cols], lnvg[:, cols], ALU.mult)
            dve.drain()
            for n in range(2):
                last = nc.vector.tensor_tensor(vtk[:, n, cols], vtk[:, n, cols], lnvb[:, cols],
                                               ALU.add)
            last.then_inc(v_ready, 1)

    def v_norm_sample(pool):
        for half in range(2):
            cols = slice(half * (EC // 2), (half + 1) * (EC // 2))
            v = vtk[0:TS, 2, cols]
            pool.wait_ge(v_centred, 3 * half + 3)
            nc.gpsimd.tensor_tensor(v, v, lnvg[0:TS, cols], ALU.mult)
            pool.drain()
            nc.gpsimd.tensor_tensor(v, v, lnvb[0:TS, cols], ALU.add).then_inc(v_ready_sample, 1)

    def mixed_tensor(pe):
        pe.wait_ge(odd_masked, 1)
        for m in range(EC // P):
            g = m // 2
            if m % (EC // P // 2) == 0:
                pe.wait_ge(v_ready, 1 + m // (EC // P // 2))
                pe.wait_ge(v_ready_sample, 1 + m // (EC // P // 2))
            if m >= 4:
                pe.wait_ge(mixed_rd, m - 3)
            for n in range(2):
                nc.tensor.matmul(ps[:, 4 + m % 4, n * P:n * P + P], vtk[:, n, m * P:m * P + P],
                                 wsT[:, g, :], start=True, stop=True)
            nc.tensor.matmul(ps[:, 4 + m % 4, TP:T], vtk[0:TS, 2, m * P:m * P + P],
                             wsS[0:TS, g, :], start=True, stop=True).then_inc(mixed_mm, 1)

    def mixed_vector(dve):
        dve.wait_ge(u_ready, 1)
        for m in range(EC // P):
            dve.wait_ge(mixed_mm, m + 1)
            nc.vector.tensor_tensor(mtmp[:, m % 2, :], ps[:, 4 + m % 4, 0:T], bsB[:, m // 2, :],
                                    ALU.add).then_inc(mixed_rd, 1)
            dve.drain()
            nc.vector.tensor_tensor(uT[:, m, :], uT[:, m, :], mtmp[:, m % 2, :], ALU.mult
                                    ).then_inc(gated, 1)
        mixed_lo(nc.vector, range(LO_POOL, EC // P), gated_lo_v)

    def mixed_scalar(act):
        act.wait_ge(v_ready_sample, 2)
        for m in range(EC // P):
            act.wait_ge(gated, m + 1)
            nc.scalar.activation(um_hi[:, m, :], uT[:, m, :], ACT.Copy).then_inc(gated_hi, 1)

    def mixed_lo(eng, tiles, done):
        for m in tiles:
            eng.wait_ge(gated_hi, m + 1)
            eng.tensor_tensor(um_lo[:, m, :], uT[:, m, :], um_hi[:, m, :].bitcast(F32),
                              ALU.subtract).then_inc(done, 1)

    gated, gated_hi = sem("gated"), sem("gated_hi")
    gated_lo, gated_lo_v = sem("gated_lo_pool"), sem("gated_lo_vector")
    LO_POOL = 9

    ESLOTS = 3
    wexp = split_tensor("wexp", 0, 2 * ESLOTS * SLOT)
    he_hi, he_lo = (split_tensor(n, 2 * ESLOTS * SLOT + x * FE * CAP, FE, CAP)
                    for x, n in enumerate(("he_hi", "he_lo")))
    aE = Area(2 * ESLOTS * SLOT + 2 * FE * CAP)
    rw = aE.take(KT, NE)
    rbB = aE.take(NE)
    h2tok = aE.take(3, D)
    acc = aE.take(KT, T)
    xg = aE.take(KT, CAP)
    htE = [aE.take(1, CAP) for _ in range(2)]
    sgE = [aE.take(CAP) for _ in range(2)]
    ye = aE.take(D)
    PgT = aE.take(T)
    Psel = aE.take(3, CAP)
    Pgat = aE.take(3, CAP)
    lgT = aE.take(T)
    lg = aE.take(3, NE)
    ex = aE.take(3, NE)
    cmpA = aE.take(3, 64)
    cmpB = aE.take(3, 64)
    beaten = aE.take(3, NE)
    sel = aE.take(3, NE + 1)
    gate = aE.take(3, NE + 1)
    rank = aE.take(3, NE + 1)
    tot = aE.take(NE)
    r1 = aE.take(3)
    r2 = aE.take(3)
    rounds_f = aE.take(2)
    router_in = sem("router_loads")
    rt_pe = Steps(sem("router_pe"), ["logits", "lgtok", "h2a", "h2b", "h2c", "rank"])
    rt_act = Steps(sem("router_act"), ["lgT", "h2a", "h2b", "h2c", "exp"])
    rt_dve = Steps(sem("router_dve"), ["max", "gate", "rounds"])
    EX0 = 1
    ex_pe = Steps(sem("expert_pe"), ["scatterA", "scatterB", "turned", "gather"], EX0)
    ex_dve = Steps(sem("expert_dve"), ["accA", "accB", "select"], EX0)
    ex_act = Steps(sem("expert_act"), ["PgT", "xg", "ye"], EX0)
    silu_e, hid_e = sem("expert_silu"), sem("expert_hidden")

    def router_loads(pool):
        pool.wait_ge(x_ready, 4)
        pool.dma_start(rw[:, :, :], a["router_w"]).then_inc(router_in, 16)
        pool.dma_start(rbB, a["router_b"].partition_broadcast(P)).then_inc(router_in, 16)

    def router_tensor(pe):
        pe.wait_ge(router_in, 32)
        pe.wait_ge(h_ready, 4)
        for q in range(KT):
            mm = nc.tensor.matmul(ps[0:NE, 0, 0:T], rw[:, q, :], hT[:, q, :], start=q == 0,
                                  stop=q == KT - 1)
        mm.then_inc(rt_pe.sem, 1)
        pe.wait_ge(rt_act.sem, rt_act.at("lgT"))
        for n in range(3):
            rows = P if n < 2 else TS
            mm = nc.tensor.transpose(ps[0:rows, 1, n * NE:n * NE + NE], lgT[0:NE, n * P:n * P + rows],
                                     ident[0:NE, 0:NE])
        mm.then_inc(rt_pe.sem, 1)
        for n, name in enumerate("abc"):
            rows = P if n < 2 else TS
            for q in range(KT):
                mm = nc.tensor.transpose(ps[0:rows, 2 + 2 * n + q // 4, (q % 4) * P:(q % 4) * P + P],
                                         hT[:, q, n * P:n * P + rows], ident)
            mm.then_inc(rt_pe.sem, 1)
        pe.wait_ge(rt_dve.sem, rt_dve.at("gate"))
        up = cst["up"]
        for n in range(3):
            for m in range(n + 1):
                nc.tensor.matmul(ps[:, 0, n * NE:n * NE + NE], up if m == n else ones[:, :],
                                 sel[:, m, 0:NE], start=m == 0, stop=m == n)
        for m in range(3):
            mm = nc.tensor.matmul(ps[:, 0, 32:32 + NE], ones[:, :], sel[:, m, 0:NE], start=m == 0,
                                  stop=m == 2)
        mm.then_inc(rt_pe.sem, 1)

    def router_scalar(act):
        act.wait_ge(rt_pe.sem, rt_pe.at("logits"))
        nc.scalar.activation(lgT[0:NE, :], ps[0:NE, 0, 0:T], ACT.Copy).then_inc(rt_act.sem, 1)
        for n, name in enumerate("abc"):
            rows = P if n < 2 else TS
            act.wait_ge(rt_pe.sem, rt_pe.at("h2" + name))
            nc.scalar.activation(h2tok[0:rows, n, :].rearrange("p (a b) -> p a b", a=2),
                                 ps[0:rows, 2 + 2 * n:4 + 2 * n, :], ACT.Copy
                                 ).then_inc(rt_act.sem, 1)
        act.wait_ge(rt_dve.sem, rt_dve.at("max"))
        nc.scalar.activation(ex[:, :, :], ex[:, :, :], ACT.Exp).then_inc(rt_act.sem, 1)

    def router_vector(dve):
        dve.wait_ge(router_in, 32)
        nc.vector.memset(lg[:, :, :], 0.0)
        nc.vector.memset(acc[:, :, :], 0.0)
        dve.drain()
        dve.wait_ge(rt_pe.sem, rt_pe.at("lgtok"))
        b3 = rbB.unsqueeze(1)
        nc.vector.tensor_tensor(lg[:, 0:2, :], ps[:, 1, 0:2 * NE].rearrange("p (n e) -> p n e", e=NE),
                                b3.to_broadcast([P, 2, NE]), ALU.add)
        nc.vector.tensor_tensor(lg[0:TS, 2, :], ps[0:TS, 1, 2 * NE:3 * NE], rbB[0:TS, :], ALU.add)
        dve.drain()
        nc.vector.tensor_reduce(r1, lg[:, :, :], AX.X, ALU.max)
        dve.drain()
        nc.vector.tensor_tensor(ex[:, :, :], lg[:, :, :], r1.unsqueeze(2).to_broadcast([P, 3, NE]),
                                ALU.subtract).then_inc(rt_dve.sem, 1)
        full = [P, 3, NE, NE]
        mine = lg[:, :, :].unsqueeze(3).to_broadcast(full)
        other = lg[:, :, :].unsqueeze(2).to_broadcast(full)
        c4 = cmpA[:, :, :].rearrange("p n (e f) -> p n e f", f=NE)
        d4 = cmpB[:, :, :].rearrange("p n (e f) -> p n e f", f=NE)
        nc.vector.tensor_tensor(c4, other, mine, ALU.is_gt)
        nc.vector.tensor_tensor(d4, other, mine, ALU.is_equal)
        dve.drain()
        nc.vector.tensor_tensor(cmpB[:, :, :], cmpB[:, :, :],
                                cst["lower_e"].unsqueeze(1).to_broadcast([P, 3, 64]), ALU.mult)
        dve.drain()
        nc.vector.tensor_tensor(cmpA[:, :, :], cmpA[:, :, :], cmpB[:, :, :], ALU.add)
        dve.drain()
        nc.vector.tensor_reduce(beaten[:, :, :], c4, AX.X, ALU.add)
        dve.drain()
        nc.vector.tensor_scalar(sel[:, :, 0:NE], beaten[:, :, :], 1.5, None, ALU.is_lt)
        dve.drain()
        nc.vector.tensor_tensor(sel[:, :, 0:NE], sel[:, :, 0:NE],
                                cst["valid"].unsqueeze(2).to_broadcast([P, 3, NE]), ALU.mult)
        dve.wait_ge(rt_act.sem, rt_act.at("exp"))
        dve.drain()
        nc.vector.tensor_scalar(beaten[:, :, :], beaten[:, :, :], 1.5, None, ALU.is_lt)
        dve.drain()
        nc.vector.tensor_tensor(ex[:, :, :], ex[:, :, :], beaten[:, :, :], ALU.mult)
        dve.drain()
        nc.vector.tensor_reduce(r2, ex[:, :, :], AX.X, ALU.add)
        dve.drain()
        nc.vector.reciprocal(r2, r2)
        dve.drain()
        nc.vector.tensor_tensor(gate[:, :, 0:NE], ex[:, :, :], r2.unsqueeze(2).to_broadcast([P, 3, NE]),
                                ALU.mult).then_inc(rt_dve.sem, 1)
        dve.wait_ge(rt_pe.sem, rt_pe.at("rank"))
        nc.vector.tensor_copy(rank[:, :, 0:NE], ps[:, 0, 0:3 * NE].rearrange("p (n e) -> p n e", e=NE))
        nc.vector.tensor_reduce(tot[:, 0:1], ps[:, 0, 32:32 + NE], AX.X, ALU.max)
        dve.drain()
        nc.vector.tensor_copy(sel[:, :, NE:NE + 1], sel[:, :, 0:1])
        nc.vector.tensor_copy(gate[:, :, NE:NE + 1], gate[:, :, 0:1])
        nc.vector.tensor_scalar(rank[:, :, NE:NE + 1], rank[:, :, 0:1], -float(CAP), None, ALU.add)
        nc.vector.tensor_scalar(rounds_f[:, 0:1], tot[:, 0:1], CAP + 0.5, 1.0, ALU.is_gt, ALU.add)
        nc.vector.tensor_scalar(rounds_f[:, 1:2], tot[:, 0:1], 2 * CAP + 0.5, None, ALU.is_gt)
        dve.drain()
        nc.vector.tensor_tensor(rounds_i[:, 0:1], rounds_f[:, 0:1], rounds_f[:, 1:2], ALU.add
                                ).then_inc(rt_dve.sem, 1)

    def rounds(eng):
        eng.wait_ge(rt_dve.sem, rt_dve.at("rounds"))
        return eng.value_load(rounds_i[0:1, 0:1], min_val=1, max_val=3)

    def each_expert(eng, body, after_round=None):
        n = rounds(eng)
        with eng.Fori(0, n) as r:
            with eng.Fori(0, NE) as e:
                body(e, r * NE + e)
            if after_round is not None:
                after_round()

    S_BASE = [len([g for g in range(G_EXP) if g % RING == s]) for s in range(RING)]

    def expert_slot(j):
        return (G_EXP + j) % RING

    def expert_use(j, turn):
        s = expert_slot(j)
        per = len([q for q in range(N_EXP) if expert_slot(q) == s])
        before = len([q for q in range(j) if expert_slot(q) == s])
        return turn * per + (S_BASE[s] + before + 1)

    def expert_parts(j):
        at = (j % ESLOTS) * SLOT
        return [wexp[:, x + at:x + at + FE * 256].rearrange("p (k n) -> p k n", n=256)
                for x in (0, ESLOTS * SLOT)]

    def expert_raw(j):
        return ring[:, expert_slot(FE + j), 0:FE * 256].rearrange("p (k n) -> p k n", n=256)

    def down_hi(act, j, t):
        act.wait_ge(landed[expert_slot(FE + j)], 16 * expert_use(FE + j, t))
        back = j - ESLOTS if j >= ESLOTS else N_ED - 1 - N_EXP
        act.wait_ge(chunk_done, N_EXP * t + (G_EXP + FE + back + 1 + DONE0))
        act_copy(expert_parts(j)[0], expert_raw(j)).then_inc(hi_ready, 1)

    def down_lo(dve, j, t):
        dve.wait_ge(hi_ready, N_ED * t + (S_EXP + j + 1))
        hi, lo = expert_parts(j)
        nc.vector.tensor_tensor(lo, expert_raw(j), hi.bitcast(F32), ALU.subtract
                                ).then_inc(lo_ready, 1)

    def gather_tensor(pe):
        for q in range(KT):
            for n in range(3):
                rows = P if n < 2 else TS
                mm = nc.tensor.matmul(ps[:, 4 + q // 4, (q % 4) * CAP:(q % 4) * CAP + CAP],
                                      h2tok[0:rows, n, q * P:q * P + P], Psel[0:rows, n, :],
                                      start=n == 0, stop=n == 2)
        mm.then_inc(ex_pe.sem, 1)

    def scatter_tensor(pe, hf, done):
        for q in range(4):
            m = 4 * hf + q
            mm = nc.tensor.matmul(ps[:, 4 + q, 0:T], ye[:, m * P:m * P + P], PgT, start=True,
                                  stop=True)
        mm.then_inc(done, 1)

    def expert_tensor(pe):
        pe.wait_ge(ex_dve.sem, EX0)
        gather_tensor(pe)

        def body(e, t):
            pe.wait_ge(ex_act.sem, 3 * t + EX0)
            for j in range(FE):
                g = G_EXP + j
                pe.wait_ge(landed[expert_slot(j)], 16 * expert_use(j, t))
                pe.wait_ge(chunk_read, N_EXP * t + (g + 1))
                w = ring[:, expert_slot(j), 0:2 * KT * P].rearrange("p (k n) -> p k n", n=P)
                for gu in range(2):
                    for q in range(KT):
                        mm = nc.tensor.matmul(ps[:, j % 2, gu * CAP:gu * CAP + CAP],
                                              w[:, gu * KT + q, :], xg[:, q, :], start=q == 0,
                                              stop=q == KT - 1)
                mm.then_inc(chunk_done, 1)
                if j == 0:
                    scatter_tensor(pe, 0, ex_pe.sem)
                if j == 1:
                    pe.wait_ge(ex_dve.sem, ex_dve.at("accA", t))
                    scatter_tensor(pe, 1, ex_pe.sem)
                if j == 2:
                    pe.wait_ge(ex_dve.sem, ex_dve.at("accB", t))
                    for n in range(3):
                        rows = P if n < 2 else TS
                        mm = nc.tensor.transpose(ps[:, 6, n * P:n * P + rows], Pgat[0:rows, n, :],
                                                 ident[0:rows, 0:rows])
                    mm.then_inc(ex_pe.sem, 1)
            pe.wait_ge(ex_dve.sem, ex_dve.at("select", t))
            gather_tensor(pe)
            pe.wait_ge(hid_e, FE * t + (FE + 2))
            for j in range(4):
                g = G_EXP + FE + j
                pe.wait_ge(lo_ready, N_ED * t + (S_EXP + j + 1))
                pe.wait_ge(chunk_read, N_EXP * t + (g + 1))
                w = expert_parts(j)
                for q in range(FE):
                    mm = three_passes(ps[:, 2 + j % 2, 0:256], (he_hi[:, q, :], he_lo[:, q, :]),
                                      [v[:, q, :] for v in w], q == 0, q == FE - 1)
                mm.then_inc(chunk_done, 1)
        each_expert(pe, body)
        pe.wait_ge(ye_zero, 1)
        pe.wait_ge(last_ye, 1)
        scatter_tensor(pe, 0, last_pe)
        pe.wait_ge(last_acc, 1)
        scatter_tensor(pe, 1, last_pe)

    ye_zero, last_ye, last_acc, last_pe = (sem("ye_zero"), sem("last_ye"), sem("last_acc"),
                                           sem("last_scatter"))

    def gathered_scalar(act):
        nc.scalar.activation(xg[:, :, :].rearrange("p (a k) c -> p a (k c)", a=2), ps[:, 4:6, :],
                             ACT.Copy).then_inc(ex_act.sem, 1)

    def expert_scalar(act):
        act.wait_ge(ex_pe.sem, EX0)
        act.wait_ge(ye_zero, 1)
        gathered_scalar(act)

        def body(e, t):
            for j in range(FE):
                act.wait_ge(chunk_done, N_EXP * t + (G_EXP + j + 1 + DONE0))
                act.wait_ge(hid_e, FE * t + (j + 1))
                nc.scalar.activation(sgE[j % 2], ps[:, j % 2, 0:CAP], ACT.Silu
                                     ).then_inc(silu_e, 1)
                if j >= FE - ESLOTS:
                    down_hi(act, j - (FE - ESLOTS), t)
                if j == 3:
                    act.wait_ge(ex_pe.sem, ex_pe.at("turned", t))
                    nc.scalar.activation(PgT, ps[:, 6, 0:T], ACT.Copy).then_inc(ex_act.sem, 1)
            act.wait_ge(ex_pe.sem, ex_pe.at("gather", t))
            gathered_scalar(act)
            for j in range(N_ED):
                if j + ESLOTS < N_ED:
                    down_hi(act, j + ESLOTS, t)
                act.wait_ge(chunk_done, N_EXP * t + (G_EXP + FE + j + 1 + DONE0))
                nc.scalar.activation(ye[:, j * 256:j * 256 + 256], ps[:, 2 + j % 2, 0:256],
                                     ACT.Copy).then_inc(chunk_read, 1)
            act.drain().then_inc(ex_act.sem, 1)
        each_expert(act, body)
        act.drain().then_inc(last_ye, 1)

    def select_vector(dve, e):
        for n in range(3):
            nc.vector.tensor_scalar(Psel[:, n, :], cst["iota"], rank[:, n, ds(e, 1)],
                                    sel[:, n, ds(e, 1)], ALU.is_equal, ALU.mult)
        dve.drain()
        for n in range(3):
            last = nc.vector.tensor_scalar(Pgat[:, n, :], Psel[:, n, :], gate[:, n, ds(e, 1)],
                                           None, ALU.mult)
        last.then_inc(ex_dve.sem, 1)

    def accumulate_vector(hf):
        return nc.vector.tensor_tensor(acc[:, 4 * hf:4 * hf + 4, :], acc[:, 4 * hf:4 * hf + 4, :],
                                       ps[:, 4:8, 0:T], ALU.add)

    def expert_vector(dve):
        nc.vector.memset(ye, 0.0)
        nc.vector.memset(PgT, 0.0)
        dve.drain().then_inc(ye_zero, 1)
        select_vector(dve, 0)
        dve.drain().then_inc(hid_e, 2)

        def body(e, t):
            for j in range(FE):
                dve.wait_ge(silu_e, FE * t + (j + 1))
                h = htE[j % 2][:, 0, :]
                nc.vector.tensor_tensor(h, sgE[j % 2], ps[:, j % 2, CAP:2 * CAP],
                                        ALU.mult).then_inc(chunk_read, 1)
                dve.drain()
                nc.vector.tensor_copy(he_hi[:, j, :], h)
                dve.drain()
                nc.vector.tensor_tensor(he_lo[:, j, :], h, he_hi[:, j, :].bitcast(F32),
                                        ALU.subtract)
                dve.drain().then_inc(hid_e, 1)
                if j >= FE - 2:
                    down_lo(dve, j - (FE - 2), t)
                if j < 2:
                    dve.wait_ge(ex_pe.sem, ex_pe.at("scatterA" if j == 0 else "scatterB", t))
                    accumulate_vector(j).then_inc(ex_dve.sem, 1)
                if j == 3:
                    dve.wait_ge(ex_pe.sem, ex_pe.at("turned", t))
                    select_vector(dve, e + 1)
            for j in range(2, N_ED):
                down_lo(dve, j, t)

        def after_round():
            dve.drain()
            nc.vector.tensor_scalar(rank[:, :, :], rank[:, :, :], -float(CAP), None, ALU.add)
            dve.drain()
        each_expert(dve, body, after_round)
        dve.wait_ge(last_pe, 1)
        accumulate_vector(0).then_inc(last_acc, 1)
        dve.wait_ge(last_pe, 2)
        accumulate_vector(1)
        dve.drain()
        accs = acc[:, :, TP:T].rearrange("p k (b s) -> p k b s", s=DS)
        nc.vector.tensor_tensor(
            accs, accs,
            modT[:, 1, G2:G2 + KT, 1:NC_].unsqueeze(3).to_broadcast([P, KT, NB, DS]), ALU.mult)
        for m in range(KT):
            nc.vector.scalar_tensor_tensor(xT[:, m, 0:TP], acc[:, m, 0:TP],
                                           modT[:, 1, G2 + m, 0:1], xT[:, m, 0:TP], ALU.mult,
                                           ALU.add)
        dve.drain()
        nc.vector.tensor_tensor(xT[:, :, TP:T], xT[:, :, TP:T], acc[:, :, TP:T], ALU.add)
        dve.drain().then_inc(x_ready, 1)

    EARLY = 3

    def load_weights(sp):
        def phase(g0, n, w, c0=0):
            size = w.shape[2]

            def body(c, k, i):
                sp.wait_ge(chunk_done, c + (g0 + 1))
                sp.dma_start(ring[:, slot(g0, k), 0:size],
                             w[ds(c + c0, 1)].rearrange("o p n -> p (o n)")
                             ).then_inc(landed[slot(g0, k)], 16)
            by_four(sp, n, body)
        phase(G_MOD0, N_MOD_A, a["w_mod"])
        phase(G_IN_E, N_IN_E, a["w_in_e"])
        phase(G_MOD1, N_MOD_ATTN - 4, a["w_mod"], N_MOD_A)
        first_keys(sp)
        phase(G_MOD1 + N_MOD_ATTN - 4, 4, a["w_mod"], N_MOD_A + N_MOD_ATTN - 4)
        other_keys(sp)
        phase(G_MOD1 + N_MOD_ATTN, N_MOD_B - N_MOD_ATTN, a["w_mod"], N_MOD_A + N_MOD_ATTN)
        phase(G_OUT_E, N_OUT_E, a["w_out_e"])
        phase(G_GU, N_GU, a["ffn_gu"])
        phase(G_DN, N_DN, a["ffn_down"])
        phase(G_IN_O, N_IN_O, a["w_in_o"])
        phase(G_OUT_O, N_OUT_O, a["w_out_o"])

        def load(j, e, t):
            s = expert_slot(j)
            back = [q for q in range(j) if expert_slot(q) == s]
            if back:
                need = back[-1] + 1
            else:
                need = max([q for q in range(N_EXP) if expert_slot(q) == s][-1] + 1 - N_EXP,
                           j - RING + 1)
            sp.wait_ge(chunk_done, N_EXP * t + (G_EXP + DONE0 + need))
            if j < FE:
                src, size = a["exp_gu"][ds(e * FE + j, 1)], 2 * KT * P
            else:
                src, size = a["exp_down"][ds(e * 4 + (j - FE), 1)], FE * 256
            sp.dma_start(ring[:, s, 0:size], src.rearrange("o p n -> p (o n)")
                         ).then_inc(landed[s], 16)

        def body(e, t):
            for j in range(EARLY, N_EXP):
                load(j, e, t)
            for j in range(EARLY):
                load(j, e + 1, t + 1)
        for j in range(EARLY):
            load(j, 0, 0)
        each_expert(sp, body)
        n = sp.value_load(rounds_i[0:1, 0:1], min_val=1, max_val=3)
        for j in range(EARLY):
            sp.wait_ge(landed[expert_slot(j)], 16 * expert_use(j, n * NE))

    CONST_LOADS = [
        (gains[:, :, :], a["gains"]), (bmod[:, :, :], a["b_mod"]), (colsE[:, :], a["colsE"]),
        (lamw[:, :, :].rearrange("p a k -> p (a k)"), a["lamv"].partition_broadcast(P)),
        (ptab[:, :], a["page_table"])]
    N_CONST_LOADS = len(CONST_LOADS) + 1

    block = ctx.enter_context(nc.Block())

    @block.sync
    def _(sp):
        sp.dma_start(xT[:, :, :], a["x_t"]).then_inc(inputs_in, 16)
        sp.dma_start(cT[:, :, :], a["c_t"]).then_inc(inputs_in, 16)
        sp.dma_start(consts[:, :], a["consts"]).then_inc(inputs_in, 16)
        load_weights(sp)
        sp.wait_ge(h_ready, 5)
        sp.dma_start(o["y"], hT[:, :, :]).then_inc(stores, 16)
        sp.wait_ge(stores, 16)

    @block.gpsimd
    def _(pool):
        for dst, src in CONST_LOADS:
            pool.dma_start(dst, src).then_inc(consts_in, 16)
        pool.dma_start(shift_in[:, :, :], a["shift"]).then_inc(consts_in, 16)
        split_lo_all(pool, G_IN_E, S_IN_E, 2, KT, 2 * P)
        pool.dma_start(attc, a["attc"]).then_inc(attn_consts_in, 16)
        pool.wait_ge(proj_ready, 1)
        pool.dma_start(o["k"], projT[:, 4:8, :]).then_inc(kv_stored, 16)
        pool.dma_start(o["v"], projT[:, 8:12, :]).then_inc(kv_stored, 16)
        shift_pool(pool)
        values_load(pool)
        pool.wait_ge(shift_saved, 1)
        pool.dma_start(o["shift"], shift_out[:, :, :]).then_inc(shift_stored, 16)
        rwkv_loads(pool)
        pool.wait_ge(rw_over, 1)
        pool.dma_start(o["wkv"], S9[:, :, :]).then_inc(kv_stored, 16)
        pool.wait_ge(kv_stored, 16 * 3)
        pool.wait_ge(mix_ready, 1)
        split_lo_all(pool, G_GU, S_GU, N_GU, 2 * KT, P)
        split_lo_all(pool, G_DN, S_DN, N_DN, FT, P)
        odd_loads(pool)
        v_norm_sample(pool)
        pool.wait_ge(v_ready_sample, 2)
        pool.dma_start(o["cv"], vtk[0:TS, 2, :]).then_inc(kv_stored, 16)
        split_lo_all(pool, G_OUT_O, S_OUT_O, 2, *out_o_kn)
        mixed_lo(pool, range(LO_POOL), gated_lo)
        split_lo_all(pool, G_OUT_O + 2, S_OUT_O + 2, N_OUT_O - 2, *out_o_kn)
        pool.wait_ge(kv_stored, 16 * 4)
        pool.wait_ge(shift_stored, 16)
        router_loads(pool)

    @block.scalar
    def _(act):
        act.wait_ge(inputs_in, 48)
        nc.scalar.activation(cT[:, :, :], cT[:, :, :], ACT.Silu).then_inc(silu_ready, 1)
        norm_scalar(act, 0)
        with act.Fori(0, 2) as u:
            mod_scalar(act, G_MOD0, u, u)
        split_hi_all(act, G_IN_E, S_IN_E, 2, KT, 2 * P)
        norm_split(act, 0)
        in_e_scalar(act)
        lambda_scalar(act)
        vtok_scalar(act)
        for par in range(2):
            act.drain().then_inc(sa_act[par].sem, 4)
        act.drain().then_inc(pa_act.sem, 4)
        pattn_exp(act, 0)
        mod_scalar(act, G_MOD1, 0, 2)
        with act.Fori(0, 3) as j:
            pattn_scalar(act, j, True)
            mod_scalar(act, G_MOD1, j + 1, j + 3)
        pattn_scalar(act, 3, False)
        mod_scalar(act, G_MOD1, 4, 6)
        sattn_newvalues(act, 0, 0)
        sattn_exp(act, 0, 0)
        sattn_scalar(act, 0, True, True)
        with act.Fori(1, NB // 2 - 1) as i:
            sattn_scalar(act, i, False, True)
        rwkv_gates_scalar(act)
        sattn_scalar(act, NB // 2 - 1, False, False)
        sattn_mix(act, 1, NB // 2 - 1)
        rwkv_scalar(act)
        gu_split_first(act)
        norm_scalar(act, 1)
        norm_split(act, 1)
        gu_scalar(act)
        split_hi_all(act, G_DN, S_DN, N_DN, FT, P)
        norm_scalar(act, 2)
        split_hi_all(act, G_IN_O, S_IN_O, 2, *odd_kn)
        norm_split(act, 2)
        in_o_scalar(act)
        split_hi_all(act, G_OUT_O, S_OUT_O, 2, *out_o_kn)
        mixed_scalar(act)
        split_hi_all(act, G_OUT_O + 2, S_OUT_O + 2, N_OUT_O - 2, *out_o_kn)
        norm_scalar(act, 3)
        router_scalar(act)
        expert_scalar(act)
        norm_scalar(act, 4)

    @block.vector
    def _(dve):
        nc.vector.memset(ones[:, :], 1.0).then_inc(ones_ready, 1)
        dve.drain().then_inc(mod_ready, 1)
        dve.drain().then_inc(chunk_read, READ0)
        dve.wait_ge(inputs_in, 48)
        dve.drain().then_inc(x_ready, 1)
        norm_scale(dve, 0)
        dve.wait_ge(consts_in, 16 * N_CONST_LOADS)
        with dve.Fori(0, 2) as u:
            mod_vector(dve, u)
        norm_gain(dve, 0, 0, SC1, 2)
        dve.drain()
        norm_shift(dve, 0, 0, SH1)
        dve.wait_ge(lo_ready, S_IN_E + 2)
        split_both(dve, G_IN_E + 2, S_IN_E + 2, N_IN_E - 2, KT, 2 * P)
        lambda_vector(dve)
        dve.wait_ge(proj_ready, 1)
        pattn_queries(dve, 0)
        dve.wait_ge(attn_consts_in, 16)
        dve.wait_ge(vtok_act, 1)
        pattn_max(dve, 0)
        shift_vector(dve)
        mod_vector(dve, 2)
        with dve.Fori(0, 3) as j:
            pattn_vector(dve, j, True)
            mod_vector(dve, j + 3)
        pattn_vector(dve, 3, False)
        for par in range(2):
            sattn_queries(dve, par, 0)
        mod_vector(dve, 6)
        sattn_max(dve, 0, 0)
        sattn_weights(dve, 0, 0)
        with dve.Fori(0, NB // 2 - 1) as i:
            sattn_vector(dve, i, True)
        sattn_vector(dve, NB // 2 - 1, False)
        rwkv_vector(dve)
        residual_vector(dve, G_OUT_E, N_OUT_E, 2, 0, G1)
        norm_vector(dve, 1, 0, SC2, SH2, 12)
        gu_vector(dve)
        residual_vector(dve, G_DN, N_DN, 1, 0, G2)
        norm_vector(dve, 2, 1, SC1, SH1, 12)
        v_norm_vector(dve)
        mixed_vector(dve)
        residual_vector(dve, G_OUT_O, N_OUT_O, 1, 1, G1)
        norm_vector(dve, 3, 1, SC2, SH2, 12)
        router_vector(dve)
        expert_vector(dve)
        norm_vector(dve, 4, None, 0, 0, 12)

    @block.tensor
    def _(pe):
        pe.drain().then_inc(chunk_done, DONE0)
        pe.drain().then_inc(pa_pe.sem, 4)
        for par in range(2):
            pe.drain().then_inc(sa_pe[par].sem, 4)
        pe.wait_ge(ones_ready, 1)
        pe.wait_ge(inputs_in, 48)
        norm_tensor(pe, 0)
        with pe.Fori(0, 2) as u:
            mod_tensor(pe, G_MOD0, u, u)
        columns_split(pe, G_IN_E, S_IN_E, N_IN_E, KT, 2, (hx_hi, hx_lo),
                      lambda e: e.wait_ge(h_ready, 1))
        vtok_tensor(pe)
        pe.wait_ge(vtok_act, 1)
        pattn_scores(pe, 0)
        mod_tensor(pe, G_MOD1, 0, 2)
        with pe.Fori(0, 3) as j:
            pattn_tensor(pe, j, True)
            mod_tensor(pe, G_MOD1, j + 1, j + 3)
        pattn_tensor(pe, 3, False)
        mod_tensor(pe, G_MOD1, 4, 6)
        sattn_scores(pe, 0, 0)
        pe.wait_ge(mod_ready, 7 + 1)
        sattn_tensor(pe, 0, True, True)
        with pe.Fori(1, NB // 2 - 1) as i:
            sattn_tensor(pe, i, False, True)
        sattn_tensor(pe, NB // 2 - 1, False, False)
        sattn_outputs(pe, 1, NB // 2 - 1)
        rwkv_tensor(pe)
        columns_tensor(pe, G_OUT_E, N_OUT_E, KT, 2, mixT, lambda e: (e.wait_ge(mix_ready, 1)))
        norm_tensor(pe, 1)
        gu_tensor(pe)
        columns_split(pe, G_DN, S_DN, N_DN, FT, 1, (hid_hi, hid_lo),
                      lambda e: e.wait_ge(hid_ready, N_GU + 2))
        norm_tensor(pe, 2)
        in_o_tensor(pe)
        mixed_tensor(pe)
        columns_split(pe, G_OUT_O, S_OUT_O, N_OUT_O, EC // P, 1, (um_hi, um_lo),
                      lambda e: (e.wait_ge(gated_lo, LO_POOL),
                                 e.wait_ge(gated_lo_v, EC // P - LO_POOL)), KT * 256)
        norm_tensor(pe, 3)
        router_tensor(pe)
        expert_tensor(pe)
        norm_tensor(pe, 4)


def kernel(**inputs):
    import concourse.bacc as _bacc
    from concourse.bass_utils import run_bass_kernel_spmd as _run

    n = {k: np.asarray(v) for k, v in inputs.items()}

    def tiles(w, cols):
        k, m = w.shape
        return w.reshape(k // P, P, m // cols, cols).transpose(2, 1, 0, 3).reshape(m // cols, P, -1)

    def columns(v):
        return v.reshape(-1, P).T

    x = np.concatenate([n["x_prompt"].reshape(TP, D), n["x_sample"].reshape(TS, D)])
    c = np.concatenate([n["c_prompt"], n["c_sample"], np.zeros((32 - NC_, D), np.float32)])
    k, v = n["cache_k"][0], n["cache_v"][0]
    wo = n["w_in_o"][0]
    ws = n["w_s"][0].transpose(2, 0, 1)
    gu = np.stack([tiles(n["ffn_gate"][0], P), tiles(n["ffn_up"][0], P)], 2)
    eg = np.stack([np.stack([tiles(n[w][0][e], P) for e in range(NE)]) for w in ("exp_gate", "exp_up")], 3)
    given = {
        "x_t": x.reshape(T, KT, P).transpose(2, 1, 0),
        "c_t": c.reshape(32, KT, P).transpose(2, 1, 0),
        "consts": np.concatenate(list(const_columns().values()), 1),
        "attc": attention_constants(),
        "scan_keep": scan_mask(),
        "gains": np.stack([columns(g) for g in (n["norm1_g"][0], n["norm2_g"][0], n["norm1_g"][1],
                                                n["norm2_g"][1], n["final_g"])], 1),
        "b_mod": n["b_mod"].reshape(2, 48, P).transpose(2, 0, 1),
        "colsE": np.concatenate(
            [columns(n["mu_b"][0])] + [columns(n[q].reshape(-1)) for q in
             ("w0", "a0", "k_k", "k_a", "r_k", "lnx_g", "lnx_b")]
            + [np.tile(n["subln_g"][0], 2)[:, None]] + [np.zeros((P, 31), np.float32)], 1),
        "lamv": np.stack([n[q][0] for q in ("lam_q1", "lam_k1", "lam_q2", "lam_k2")]).reshape(-1),
        "page_table": n["page_table"].reshape(1, -1),
        "shift": n["state_shift"][0].reshape(NB, 14, P).transpose(2, 1, 0),
        "s_init": n["state_wkv"][0].reshape(NB, 4, 2, 64, 64).transpose(2, 4, 0, 1, 3).reshape(P, NB, 256),
        "cache_k": k.reshape(N_POOL, PAGE, 4, P).transpose(0, 3, 2, 1).reshape(N_POOL, P, -1),
        "cache_v": v.reshape(N_POOL, PAGE, 512),
        "wa_up": np.concatenate([n["w_up"][0], n["a_up"][0]]),
        "g_up": n["g_up"][0],
        "w_mod": n["w_mod"].reshape(2, 4, 2, P, 6, D).transpose(0, 4, 1, 3, 2, 5).reshape(48, P, -1),
        "w_in_e": tiles(n["w_in_e"][0], 256),
        "w_out_e": tiles(n["w_out_e"][0], 256),
        "ffn_gu": gu.reshape(FT, P, -1),
        "ffn_down": tiles(n["ffn_down"][0], P),
        "w_in_o": tiles(wo, 256),
        "lnv_g": n["lnv_g"][0], "lnv_b": n["lnv_b"][0],
        "b_s": np.concatenate([n["b_s"][0], n["b_s"][0], np.tile(n["b_s"][0][:, :DS], (1, NB))], 1).reshape(-1),
        "w_s": ws,
        "w_s8": np.tile(ws[:DS, :, :DS], (NB, 1, NB)),
        "w_out_o": tiles(n["w_out_o"][0], P),
        "router_w": n["router_w"][0].reshape(KT, P, NE).transpose(1, 0, 2),
        "router_b": n["router_b"][0],
        "exp_gu": np.concatenate([eg.reshape(NE * FE, P, -1), eg[0, 0:3].reshape(3, P, -1)]),
        "exp_down": np.concatenate([tiles(n["exp_down"][0][e], 256) for e in range(NE)]),
    }
    returned = {"y": [P, KT, T], "k": [P, 4, T], "v": [P, 4, T], "shift": [P, 14, NC_],
                "wkv": [P, NC_, 256], "cv": [TS, EC]}
    nc = _bacc.Bacc("TRN2", target_bir_lowering=False, num_devices=1)
    arrays, a, o = {}, {}, {}
    for name, array in given.items():
        array = np.ascontiguousarray(array)
        arrays["in_" + name] = array
        a[name] = nc.dram_tensor("in_" + name, array.shape, mybir.dt.from_np(array.dtype),
                                 kind="ExternalInput").ap()
    for name, shape in returned.items():
        o[name] = nc.dram_tensor("out_" + name, shape, F32, kind="ExternalOutput").ap()
    build(nc, a, o)
    r = _run(nc, [arrays], core_ids=[0]).results[0]
    r = {name: np.asarray(r["out_" + name]) for name in returned}

    def rows(v):
        return v.transpose(2, 1, 0).reshape(v.shape[2], -1)
    y, kn, vn, sh = rows(r["y"]), rows(r["k"]), rows(r["v"]), rows(r["shift"])
    s = r["wkv"].reshape(2, 64, NC_, 4, 64).transpose(2, 3, 0, 4, 1).reshape(NC_, H, 64, 64)
    return (y[:TP].reshape(1, TP, D), y[TP:].reshape(NB, DS, D),
            kn[:TP].reshape(1, 1, TP, H, 2 * DK), vn[:TP].reshape(1, 1, TP, H, DV),
            s[:1][None], sh[:1][None],
            kn[TP:].reshape(1, NB, DS, H, 2 * DK), vn[TP:].reshape(1, NB, DS, H, DV),
            s[1:][None], sh[1:][None], r["cv"].reshape(1, NB, DS, EC))
```
